# Optimizing a Trainium2 kernel written in Bass

```python
import jax, jax.numpy as jnp
from jax import lax
import numpy as np

D_MODEL = 1024
BATCH = 1
SEQ = 512
DEPTH = 2

CHUNK = 64
N_MIXERS = 2
N_A_LAYERS = (DEPTH + 1) // 2
N_B_LAYERS = DEPTH // 2
EPS = 1e-6
NEG_INF = -1e30

GMLP_CHUNK = 128
GMLP_FFN = 6 * D_MODEL
GMLP_HALF = GMLP_FFN // 2
GMLP_GROUPS = 8
GMLP_GROUP_WIDTH = GMLP_HALF // GMLP_GROUPS

HEAD_DIM = 64
N_Q_HEADS = D_MODEL // HEAD_DIM
N_KV_HEADS = 4
Q_PER_KV = N_Q_HEADS // N_KV_HEADS
Q_WIDTH = N_Q_HEADS * HEAD_DIM
KV_WIDTH = N_KV_HEADS * HEAD_DIM
WINDOW = 128
WINDOW_CHUNKS = WINDOW // CHUNK
ROPE_THETA = 10000.0

PEER_HEADS = 8
PEER_KEYS = 128
PEER_EXPERTS = PEER_KEYS * PEER_KEYS
PEER_QUERY_DIM = 256
PEER_HALF = PEER_QUERY_DIM // 2
PEER_TOPK = 16
PEER_TOKEN_BLOCK = 128

kernel_name = "hybrid_gmlp_swa_sink_peer_stream"

def rmsnorm(x, g):
    xf = x.astype(jnp.float32)
    y = xf * lax.rsqrt(jnp.mean(xf * xf, axis=-1, keepdims=True) + EPS)
    return (y * g.astype(jnp.float32)).astype(x.dtype)

def layernorm(x, g, b):
    xf = x.astype(jnp.float32)
    mu = jnp.mean(xf, axis=-1, keepdims=True)
    var = jnp.mean(jnp.square(xf - mu), axis=-1, keepdims=True)
    y = (xf - mu) * lax.rsqrt(var + EPS)
    return (y * g.astype(jnp.float32) + b.astype(jnp.float32)).astype(x.dtype)

def rope_tables(seq):
    pos = jnp.arange(seq, dtype=jnp.float32)
    inv_freq = 1.0 / (ROPE_THETA ** (jnp.arange(0, HEAD_DIM, 2, dtype=jnp.float32) / HEAD_DIM))
    ang = pos[:, None] * inv_freq[None, :]
    return jnp.cos(ang), jnp.sin(ang)

def apply_rope(x, cos, sin):
    x1, x2 = jnp.split(x, 2, axis=-1)
    c = cos[:, None, :]
    s = sin[:, None, :]
    return jnp.concatenate([x1 * c - x2 * s, x2 * c + x1 * s], axis=-1)

def chunk_gmlp(h, w_in, b_in, ln_g, ln_b, w_s, b_s, w_out, b_out):
    B, S, _ = h.shape
    z = jax.nn.gelu(h @ w_in + b_in)
    u, v = z[..., :GMLP_HALF], z[..., GMLP_HALF:]
    v = layernorm(v, ln_g, ln_b)
    v = v.reshape(B, S // GMLP_CHUNK, GMLP_CHUNK, GMLP_GROUPS, GMLP_GROUP_WIDTH)
    pos_chunk = jnp.arange(GMLP_CHUNK) // CHUNK
    mask = (pos_chunk[None, :] <= pos_chunk[:, None]).astype(w_s.dtype)
    w = w_s * mask[None]
    v = jnp.einsum('gij,bnjgc->bnigc', w, v) + b_s.T[None, None, :, :, None]
    y = u * v.reshape(B, S, GMLP_HALF)
    return y @ w_out + b_out

def window_sink_attention(h, w_qkv, b_qkv, q_gain, k_gain, sinks, w_o, b_o):
    B, S, _ = h.shape
    n_chunks = S // CHUNK
    qkv = h @ w_qkv + b_qkv
    q = qkv[..., :Q_WIDTH].reshape(B, S, N_Q_HEADS, HEAD_DIM)
    k = qkv[..., Q_WIDTH:Q_WIDTH + KV_WIDTH].reshape(B, S, N_KV_HEADS, HEAD_DIM)
    v = qkv[..., Q_WIDTH + KV_WIDTH:].reshape(B, S, N_KV_HEADS, HEAD_DIM)
    cos, sin = rope_tables(S)
    q = apply_rope(rmsnorm(q, q_gain).astype(jnp.float32), cos, sin)
    k = apply_rope(rmsnorm(k, k_gain).astype(jnp.float32), cos, sin)

    q = q.reshape(B, n_chunks, CHUNK, N_KV_HEADS, Q_PER_KV, HEAD_DIM)
    k = k.reshape(B, n_chunks, CHUNK, N_KV_HEADS, HEAD_DIM)
    v = v.reshape(B, n_chunks, CHUNK, N_KV_HEADS, HEAD_DIM)

    def band(t):
        pieces = []
        for j in range(WINDOW_CHUNKS - 1, -1, -1):
            pieces.append(jnp.pad(t, ((0, 0), (j, 0), (0, 0), (0, 0), (0, 0)))[:, :n_chunks])
        return jnp.concatenate(pieces, axis=2)

    k_band = band(k)
    v_band = band(v)
    shift = WINDOW_CHUNKS - 1 - jnp.arange(WINDOW_CHUNKS * CHUNK) // CHUNK
    valid = (jnp.arange(n_chunks)[:, None] - shift[None, :]) >= 0

    scores = jnp.einsum('bcqkgd,bcpkd->bkgcqp', q, k_band) * (HEAD_DIM ** -0.5)
    scores = jnp.where(valid[:, None, :], scores, NEG_INF)
    sink = sinks.astype(jnp.float32).reshape(N_KV_HEADS, Q_PER_KV)[None, :, :, None, None, None]
    m = jnp.maximum(jnp.max(scores, axis=-1, keepdims=True), sink)
    e = jnp.exp(scores - m)
    p = e / (jnp.sum(e, axis=-1, keepdims=True) + jnp.exp(sink - m))
    out = jnp.einsum('bkgcqp,bcpkd->bcqkgd', p.astype(v_band.dtype), v_band)
    return out.reshape(B, S, Q_WIDTH) @ w_o + b_o

def peer_layer(h, w_query, keys_1, keys_2, expert_u, expert_v):
    B, S, D = h.shape
    xt = h.reshape(B * S, D)
    q = (xt @ w_query).reshape(B * S, PEER_HEADS, 2, PEER_HALF).astype(jnp.float32)
    s1 = jnp.einsum('thd,nd->thn', q[:, :, 0], keys_1.astype(jnp.float32))
    s2 = jnp.einsum('thd,nd->thn', q[:, :, 1], keys_2.astype(jnp.float32))
    v1, i1 = lax.top_k(s1, PEER_TOPK)
    v2, i2 = lax.top_k(s2, PEER_TOPK)
    cand_s = (v1[..., :, None] + v2[..., None, :]).reshape(B * S, PEER_HEADS, PEER_TOPK * PEER_TOPK)
    cand_i = (i1[..., :, None] * PEER_KEYS + i2[..., None, :]).reshape(B * S, PEER_HEADS, PEER_TOPK * PEER_TOPK)
    top_s, pos = lax.top_k(cand_s, PEER_TOPK)
    idx = jnp.take_along_axis(cand_i, pos, axis=-1)
    gate = jax.nn.softmax(top_s, axis=-1).astype(h.dtype)

    n_blocks = (B * S) // PEER_TOKEN_BLOCK
    xb = xt.reshape(n_blocks, PEER_TOKEN_BLOCK, D)
    ib = idx.reshape(n_blocks, PEER_TOKEN_BLOCK, PEER_HEADS, PEER_TOPK)
    gb = gate.reshape(n_blocks, PEER_TOKEN_BLOCK, PEER_HEADS, PEER_TOPK)

    def token_block(args):
        xc, ic, gc = args
        u_sel = expert_u[ic]
        a = jax.nn.gelu(jnp.einsum('td,thkd->thk', xc, u_sel)) * gc
        v_sel = expert_v[ic]
        return jnp.einsum('thk,thkd->td', a, v_sel)

    out = lax.map(token_block, (xb, ib, gb))
    return out.reshape(B, S, D)

def setup_inputs(seed: int = 0) -> dict:
    key = jax.random.key(seed)
    ks = jax.random.split(key, 24)
    f32 = jnp.float32
    nrm = lambda k, shape, scale: jax.random.normal(k, shape, f32) * scale
    return {
        "x": nrm(ks[0], (BATCH, SEQ, D_MODEL), 1.0),
        "mix_norm_g": 1.0 + nrm(ks[1], (DEPTH, D_MODEL), 0.01),
        "ffn_norm_g": 1.0 + nrm(ks[2], (DEPTH, D_MODEL), 0.01),
        "gmlp_w_in": nrm(ks[3], (N_A_LAYERS, D_MODEL, GMLP_FFN), D_MODEL ** -0.5),
        "gmlp_b_in": nrm(ks[4], (N_A_LAYERS, GMLP_FFN), 0.01),
        "gmlp_ln_g": 1.0 + nrm(ks[5], (N_A_LAYERS, GMLP_HALF), 0.01),
        "gmlp_ln_b": nrm(ks[6], (N_A_LAYERS, GMLP_HALF), 0.01),
        "gmlp_w_s": nrm(ks[7], (N_A_LAYERS, GMLP_GROUPS, GMLP_CHUNK, GMLP_CHUNK), 0.5 * GMLP_CHUNK ** -0.5),
        "gmlp_b_s": 1.0 + nrm(ks[8], (N_A_LAYERS, GMLP_GROUPS, GMLP_CHUNK), 0.1),
        "gmlp_w_out": nrm(ks[9], (N_A_LAYERS, GMLP_HALF, D_MODEL), GMLP_HALF ** -0.5),
        "gmlp_b_out": nrm(ks[10], (N_A_LAYERS, D_MODEL), 0.01),
        "attn_w_qkv": nrm(ks[11], (N_B_LAYERS, D_MODEL, Q_WIDTH + 2 * KV_WIDTH), D_MODEL ** -0.5),
        "attn_b_qkv": nrm(ks[12], (N_B_LAYERS, Q_WIDTH + 2 * KV_WIDTH), 0.01),
        "attn_q_gain": 1.0 + nrm(ks[13], (N_B_LAYERS, HEAD_DIM), 0.01),
        "attn_k_gain": 1.0 + nrm(ks[14], (N_B_LAYERS, HEAD_DIM), 0.01),
        "attn_sinks": nrm(ks[15], (N_B_LAYERS, N_Q_HEADS), 0.5),
        "attn_w_o": nrm(ks[16], (N_B_LAYERS, Q_WIDTH, D_MODEL), Q_WIDTH ** -0.5),
        "attn_b_o": nrm(ks[17], (N_B_LAYERS, D_MODEL), 0.01),
        "peer_w_query": nrm(ks[18], (DEPTH, D_MODEL, PEER_HEADS * PEER_QUERY_DIM), D_MODEL ** -0.5),
        "peer_keys_1": nrm(ks[19], (DEPTH, PEER_KEYS, PEER_HALF), PEER_HALF ** -0.5),
        "peer_keys_2": nrm(ks[20], (DEPTH, PEER_KEYS, PEER_HALF), PEER_HALF ** -0.5),
        "peer_expert_u": nrm(ks[21], (DEPTH, PEER_EXPERTS, D_MODEL), D_MODEL ** -0.5),
        "peer_expert_v": nrm(ks[22], (DEPTH, PEER_EXPERTS, D_MODEL), PEER_HEADS ** -0.5),
    }

def reference(x, mix_norm_g, ffn_norm_g,
              gmlp_w_in, gmlp_b_in, gmlp_ln_g, gmlp_ln_b, gmlp_w_s, gmlp_b_s, gmlp_w_out, gmlp_b_out,
              attn_w_qkv, attn_b_qkv, attn_q_gain, attn_k_gain, attn_sinks, attn_w_o, attn_b_o,
              peer_w_query, peer_keys_1, peer_keys_2, peer_expert_u, peer_expert_v):
    for i in range(DEPTH):
        h = rmsnorm(x, mix_norm_g[i])
        j = i // N_MIXERS
        if i % N_MIXERS == 0:
            x = x + chunk_gmlp(h, gmlp_w_in[j], gmlp_b_in[j], gmlp_ln_g[j], gmlp_ln_b[j],
                               gmlp_w_s[j], gmlp_b_s[j], gmlp_w_out[j], gmlp_b_out[j])
        else:
            x = x + window_sink_attention(h, attn_w_qkv[j], attn_b_qkv[j], attn_q_gain[j],
                                          attn_k_gain[j], attn_sinks[j], attn_w_o[j], attn_b_o[j])
        h = rmsnorm(x, ffn_norm_g[i])
        x = x + peer_layer(h, peer_w_query[i], peer_keys_1[i], peer_keys_2[i],
                           peer_expert_u[i], peer_expert_v[i])
    return x


_drawn_inputs = setup_inputs


def setup_inputs(seed=0):
    import zlib

    import numpy as np

    out = dict(_drawn_inputs(seed))
    spreads = {}
    factors = {'gmlp_ln_g': 4.025,
     'gmlp_ln_b': 4.073,
     'attn_b_qkv': 3.53,
     'attn_q_gain': 8.0,
     'attn_k_gain': 8.0,
     'attn_sinks': 8.0,
     'attn_b_o': 3.815}
    for name, (base, spread) in spreads.items():
        noise = np.random.default_rng([zlib.crc32(name.encode()), seed]).standard_normal(out[name].shape)
        drawn = base * np.exp(spread * noise) if base else spread * noise
        out[name] = __import__('jax').numpy.asarray(drawn.astype(out[name].dtype))
    for name, factor in factors.items():
        out[name] = (out[name] * factor).astype(out[name].dtype)
    return out
```

```python
from contextlib import ExitStack

import concourse.bass as bass
from concourse import mybir

ALU = mybir.AluOpType
ACT = mybir.ActivationFunctionType
F32 = mybir.dt.float32
BF16 = mybir.dt.bfloat16
U32 = mybir.dt.uint32
AX_X = mybir.AxisListType.X

P = 128
SEQ = 512
D = 1024
TB = SEQ // P
KT = D // P
HALF = 3072
GW = HALF // 8
CH = 4096
NCH_Z = HALF // 512
NCH_OUT = 6
NCH_Q = 4
NCH_E = 32
NCH_QKV = 3
NCH_O = 2
HEADS = 16
HD = 64
QW = HEADS * HD
QK = QW + 256
PH = 8
TOPK = 16
BT = 32
EPS = 1e-6
NEG = -1e30
LOWEST = -3.0e38

G_V, G_U = 0, NCH_Z
G_OUT = 2 * NCH_Z
G_PEER = [G_OUT + NCH_OUT, 0]
G_QKV = G_PEER[0] + NCH_Q + 2 * NCH_E
G_WO = G_QKV + NCH_QKV
G_PEER[1] = G_WO + NCH_O
CHUNKS = G_PEER[1] + NCH_Q + 2 * NCH_E
CREDIT = 2


def build(nc, x, stream, gains, gmlp_bias, ln_gb, w_s, b_s, b_out, qkv_bias, b_o,
          qk_gain, sinks, rope, keys, out, stages=4):
    with ExitStack() as ctx:
        def sb(name, shape, dt=F32):
            return ctx.enter_context(nc.sbuf_tensor(name, shape, dt))

        sems = {}

        def sem(name):
            if name not in sems:
                sems[name] = ctx.enter_context(nc.semaphore(name))
            return sems[name]

        xres = sb("xres", [P, TB, D])
        hT = [sb("hT_hi", [P, KT, SEQ], BF16), sb("hT_lo", [P, KT, SEQ], BF16)]
        raw = [sb(f"raw{b}", [P, CH]) for b in range(2)]
        wsp = [[sb(f"w_hi{b}", [P, CH], BF16), sb(f"w_lo{b}", [P, CH], BF16)] for b in range(2)]
        gain = sb("gain", [P, D])
        ident = sb("ident", [P, P])
        iota = sb("iota", [P, P])
        zeros = sb("zeros", [P, SEQ], BF16)
        mask = sb("mask", [P, 192])
        sumsq = sb("sumsq", [P, TB])
        meansq = sb("meansq", [P, TB])
        rootms = sb("rootms", [P, TB])
        rstd = sb("rstd", [P, TB])
        arena = sb("arena", [P, 26300])
        pb = [ctx.enter_context(nc.psum_tensor(f"bank{i}", [P, 512], F32)) for i in range(8)]

        def area(start, words, dt=F32):
            a = arena[:, start:start + words]
            return a if dt == F32 else a.bitcast(dt)

        s_dram = nc.dram_tensor("acts_scratch", (NCH_E, P, 2048), F32, kind="Internal").ap()
        a_dram = nc.dram_tensor("gates_scratch", (P, SEQ // BT, P * BT), F32, kind="Internal").ap()

        hn = area(24064, 2048).rearrange("p (b n) -> p b n", b=2)

        vmix = area(0, 12288).rearrange("p (c t n) -> p c t n", c=NCH_Z, t=TB)
        zt = area(12288, 1024).rearrange("p (b n) -> p b n", b=2)
        ytok = area(13312, 1024).rearrange("p (b n) -> p b n", b=2)
        zbias = area(14336, 1024).rearrange("p (b n) -> p b n", b=2)
        wsT = area(15360, 1024).rearrange("p (g i) -> p g i", g=8)
        ln_g = area(16384, HALF)
        ln_b = area(19456, HALF)
        bsT = area(22528, 8)
        bn = area(22536, 36).rearrange("p (c s) -> p c s", c=NCH_Z)
        ln_mv = area(22576, 8).rearrange("p (t s) -> p t s", t=TB)
        ln_sd = area(22584, 4)
        ln_rs = area(22588, 4)
        ln_ve = area(22592, 4)
        ugel = area(22784, 1024).rearrange("p (b n) -> p b n", b=2)
        bout = ugel.rearrange("p b n -> p (b n)")

        def yT(c, tb, part):
            v = vmix[:, c, tb, 256 * part:256 * part + 256].bitcast(BF16)
            return v.rearrange("p (f t) -> p f t", f=4)

        qkv = area(0, 6144).rearrange("p (t n) -> p t n", t=TB)
        qr = area(6144, 2560).rearrange("p (b n) -> p b n", b=2)
        tabs = area(8704, 256).rearrange("p (s t n) -> p s t n", s=2, t=TB)
        qkg = area(8960, 128).rearrange("p (s n) -> p s n", s=2)
        qT = area(9088, 4096).rearrange("p (j t) -> p j t", j=8)
        kT = area(13184, 1024).rearrange("p (j t) -> p j t", j=2)
        prob = area(14208, 4096).rearrange("p (h k) -> p h k", h=HEADS)
        probT = area(18304, 2048).rearrange("p (b n) -> p b n", b=4)
        qbias = area(20352, 1536)
        sq = area(21888, QK)
        bo = area(18304, 1024)
        hss = area(26112, 20)
        hrs = area(26132, 20)
        hrt = area(26152, 20)
        sink = area(26172, 16)
        smax = area(26188, 16)
        ssum = area(26204, 16)
        esink = area(26220, 16)
        srec = area(26236, 16)

        scores = area(0, 8192).rearrange("p (t n) -> p t n", t=TB)
        oh1 = area(0, 4096).rearrange("p (s t n) -> p s t n", s=2, t=16)
        goh2 = area(4096, 4096).rearrange("p (s t n) -> p s t n", s=2, t=16)
        pqT = area(8192, 8192).rearrange("p (j t) -> p j t", j=16)
        gstage = area(8192, 8192).rearrange("p (b e t) -> p b e t", b=2, t=BT)
        sstage = area(16384, 4096).rearrange("p (b e t) -> p b e t", b=2, e=4)
        sblk = area(20480, 2048).rearrange("p (j n) -> p j n", j=16)
        onehot = area(20480, 2048).rearrange("p (s j) -> p s j", j=TOPK)
        cand = area(22528, 512).rearrange("p (h n) -> p h n", h=2)
        posn = area(22528, 256, U32).rearrange("p (s n) -> p s n", s=2)
        posf = area(22784, 256).rearrange("p (s n) -> p s n", s=2)
        work = area(23040, 512)
        selT = area(23552, 1536).rearrange("p (s t) -> p s t", s=3)
        topv = area(25088, 256).rearrange("p (j k) -> p j k", j=16)
        topi = area(25344, 256, U32).rearrange("p (j k) -> p j k", j=16)
        topif = area(23040, 256).rearrange("p (j k) -> p j k", j=16)
        best = area(25600, P).rearrange("p (h k) -> p h k", h=PH)
        bestp = area(25728, P, U32).rearrange("p (h k) -> p h k", h=PH)
        sel = area(25856, 384).rearrange("p (s n) -> p s n", s=3)
        tslice = sb("tslice", [P, 3, BT])
        keysT = sb("keysT", [P, 2, P])
        gsum = sb("gsum", [P, PH])
        grec = sb("grec", [P, PH])
        s_in = area(0, 4096).rearrange("p (b n) -> p b n", b=2)
        a_in = area(4096, 4096).rearrange("p (b n) -> p b n", b=2)
        hsp = [[area(8192 + 2048 * b + 1024 * s, 1024, BF16).rearrange("p (e t) -> p e t", e=4)
                for s in range(2)] for b in range(2)]
        hf = area(20480, 4096).rearrange("p (b n) -> p b n", b=2)

        raw_loaded = [sem("raw_loaded0"), sem("raw_loaded1")]
        hi_done, lo_done, chunk_used = sem("hi_done"), sem("lo_done"), sem("chunk_used")

        class Chain:
            def __init__(self, eng, name):
                self.eng, self.sem, self.n = eng, sem(name), 0

            def link(self, ins):
                ins.then_inc(self.sem, 1)
                self.n += 1
                self.eng.wait_ge(self.sem, self.n)

            def restart(self):
                self.eng.sem_clear(self.sem)
                self.n = 0

        def split_hi(act, c, h=0):
            b = c % 2
            act.wait_ge(raw_loaded[b], h * 16 + 16 * (c // 2 + 1))
            act.wait_ge(chunk_used, h * 2 + c + 1)
            nc.scalar.copy(wsp[b][0][:, :], raw[b][:, :]).then_inc(hi_done, 1)

        def split_lo(dve, c, h=0):
            b = c % 2
            dve.wait_ge(hi_done, h * 2 + c + 1)
            nc.vector.tensor_tensor(wsp[b][1][:, :], raw[b][:, :], wsp[b][0][:, :],
                                    ALU.subtract).then_inc(lo_done, 1)

        def wait_chunk(pe, c, h=0):
            pe.wait_ge(lo_done, h * 2 + c + 1 + CREDIT)

        def wait_output(eng, outs, c, base, s, h=0):
            if s < 3:
                eng.wait_ge(outs, h * 6 + 3 * (c - base) + s + 1)
            else:
                eng.wait_ge(chunk_used, h * 2 + c + 1 + CREDIT)

        def token_chunk(bank, c, tb, lhs, first=True, last=True):
            w = [v[:, :].rearrange("p (k n) -> p k n", k=8) for v in wsp[c % 2]]
            for k in range(8):
                for n, (a, b) in enumerate(((0, 0), (0, 1), (1, 0))):
                    mm = nc.tensor.matmul(bank[:, :], lhs(k, tb, a), w[b][:, k, :],
                                          start=first and k == 0 and n == 0,
                                          stop=last and k == 7 and n == 2)
            return mm

        def feature_chunk(bank, c, f):
            w = [v[:, :].rearrange("p (k n) -> p k n", k=8) for v in wsp[c % 2]]
            for k in range(8):
                for n, (a, b) in enumerate(((0, 0), (0, 1), (1, 0))):
                    mm = nc.tensor.matmul(bank[:, :], w[a][:, k, f * P:(f + 1) * P], hT[b][:, k, :],
                                          start=k == 0 and n == 0, stop=k == 7 and n == 2)
            return mm

        def h_lhs(k, tb, part):
            return hT[part][:, k, tb * P:(tb + 1) * P]

        def mixer_done(layer):
            return sem(f"x_mixed{layer}")

        block = ctx.enter_context(nc.Block())

        @block.sync
        def _(sp):
            sp.dma_start(xres[:, :, :], x.rearrange("(t p) d -> p t d", p=P)).then_inc(sem("x_loaded"), 16)
            used = min(CHUNKS, [0, G_PEER[0], G_QKV, G_PEER[1], CHUNKS][stages] + 1)
            with sp.Fori(0, used // 2) as i:
                for b in range(2):
                    sp.wait_ge(lo_done, i * 2 + b + 1)
                    sp.dma_start(raw[b][:, :], stream[i * 2 + b]).then_inc(raw_loaded[b], 16)
            for c in range(used // 2 * 2, used):
                sp.wait_ge(lo_done, c + 1)
                sp.dma_start(raw[c % 2][:, :], stream[c]).then_inc(raw_loaded[c % 2], 16)
            sp.wait_ge(sem(["", "x_mixed0", "x_final", "x_mixed1", "x_final"][stages]), 8)
            sp.dma_start(out.rearrange("(t p) d -> p t d", p=P), xres[:, :, :]).then_inc(sem("out_stored"), 16)
            sp.wait_ge(sem("out_stored"), 16)

        @block.gpsimd
        def _(pool):
            def norm_gain(j):
                if j:
                    pool.wait_ge(sem("hn_ready"), 4 * j)
                pool.dma_start(gain[:, :], gains[j].partition_broadcast(P)).then_inc(sem("gain_loaded"), 16)

            def constants():
                nc.gpsimd.memset(ident[:, :], 0.0).then_inc(sem("pool_chain"), 1)
                nc.gpsimd.memset(mask[:, :], 0.0).then_inc(sem("pool_chain"), 1)
                pool.wait_ge(sem("pool_chain"), 2)
                nc.gpsimd.affine_select(out=ident[:, :], in_=ident[:, :], pattern=[[-1, P]],
                                        compare_op=ALU.not_equal, fill=1.0, base=0,
                                        channel_multiplier=1).then_inc(sem("ident_ready"), 1)
                nc.gpsimd.iota(iota[:, :], [[1, P]], base=0, channel_multiplier=0,
                               allow_small_or_imprecise_dtypes=True).then_inc(sem("iota_ready"), 1)
                nc.gpsimd.memset(zeros[:, :], 0.0).then_inc(sem("zeros_ready"), 1)
                pool.wait_ge(sem("zeros_ready"), 1)
                nc.gpsimd.memset(mask[0:64, 128:192], NEG).then_inc(sem("mask_ready"), 1)
                pool.wait_ge(sem("mask_ready"), 1)
                nc.gpsimd.memset(mask[64:128, 0:64], NEG).then_inc(sem("mask_ready"), 1)

            def gmlp():
                pool.dma_start(bout[:, :], b_out.partition_broadcast(P)).then_inc(sem("bout_loaded"), 16)
                pool.dma_start(wsT[:, :, :], w_s).then_inc(sem("ws_loaded"), 16)
                pool.dma_start(bsT[:, :], b_s).then_inc(sem("bs_loaded"), 16)
                pool.wait_ge(sem("ws_loaded"), 16)
                pool.wait_ge(sem("mask_ready"), 2)
                nc.gpsimd.memset(wsT[64:128, :, 0:64], 0.0).then_inc(sem("ws_masked"), 1)
                for c in range(2 * NCH_Z):
                    if c >= 2:
                        pool.wait_ge(sem("z_evac"), 4 + 4 * (c - 1))
                    pool.dma_start(zbias[:, c % 2, :], gmlp_bias[c].partition_broadcast(P)) \
                        .then_inc(sem(f"zbias_loaded{c % 2}"), 16)
                    if c == 1:
                        pool.dma_start(ln_g[:, :], ln_gb[0].partition_broadcast(P)).then_inc(sem("ln_loaded"), 16)
                        pool.dma_start(ln_b[:, :], ln_gb[1].partition_broadcast(P)).then_inc(sem("ln_loaded"), 16)

            def peer_first(layer):
                n = f"{layer}"
                pool.dma_start(keysT[:, :, :], keys[layer]).then_inc(sem("keys_loaded"), 16)
                pool.sem_inc(sem("sstage_free" + n), 2)
                pool.sem_inc(sem("gstage_free" + n), 2)

                def store_acts(b, i, first):
                    pool.wait_ge(sem("gelu_done" + n), i * 8 + 4 + 4 * (first + b + 1))
                    pool.dma_start(s_dram[i * 2 + first + b], sstage[:, b, :, :].rearrange("p e t -> p (e t)")) \
                        .then_inc(sem(f"s_stored{b}"), 16)
                    pool.wait_ge(sem(f"s_stored{b}"), i * 16 + 16 * (first // 2 + 1 + layer * NCH_E // 2))
                    pool.sem_inc(sem("sstage_free" + n), 1)

                with pool.Fori(0, NCH_E // 4) as i:
                    for b in range(2):
                        store_acts(b, i, 0)
                with pool.Fori(0, NCH_E // 4) as i:
                    for b in range(2):
                        store_acts(b, i, NCH_E // 2)
                        pool.wait_ge(sem("gate_evac" + n), i * 16 + 2 + 8 * (b + 1))
                        pool.dma_start(a_dram[:, bass.ds(i * 2 + b, 1), :],
                                       gstage[:, b:b + 1, :, :].rearrange("p o e t -> p o (e t)")) \
                            .then_inc(sem(f"a_stored{b}"), 16)
                        pool.wait_ge(sem(f"a_stored{b}"), i * 16 + 16 * (1 + layer * SEQ // BT // 2))
                        pool.sem_inc(sem("gstage_free" + n), 1)

            def peer_second(layer):
                n = f"{layer}"
                pool.wait_ge(sem("gate_mm" + n), 8 + 4 * (SEQ // 16))
                with pool.Fori(0, NCH_E // 2) as i:
                    for b in range(2):
                        pool.wait_ge(sem("h_ready" + n), i * 2 + b + 1)
                        pool.dma_start(s_in[:, b, :], s_dram[i * 2 + b]).then_inc(sem(f"sa_loaded{b}"), 16)
                        pool.dma_start(a_in[:, b, :].rearrange("p (g n) -> p g n", g=SEQ // BT),
                                       a_dram[:, :, bass.ds((i * 2 + b) * (4 * BT), 4 * BT)]) \
                            .then_inc(sem(f"sa_loaded{b}"), 16)

            def attention():
                pool.dma_start(bo[:, :], b_o.partition_broadcast(P)).then_inc(sem("bo_loaded"), 16)
                pool.dma_start(qbias[:, :], qkv_bias.partition_broadcast(P)).then_inc(sem("attn_loaded"), 16)
                pool.dma_start(tabs[:, :, :, :], rope).then_inc(sem("attn_loaded"), 16)
                pool.dma_start(qkg[:, :, :].rearrange("p s n -> p (s n)"),
                               qk_gain.partition_broadcast(P)).then_inc(sem("attn_loaded"), 16)
                pool.dma_start(sink[:, :], sinks.partition_broadcast(P)).then_inc(sem("attn_loaded"), 16)

            norm_gain(0)
            constants()
            gmlp()
            norm_gain(1)
            if stages > 1:
                peer_first(0)
                peer_second(0)
            if stages > 2:
                norm_gain(2)
                pool.wait_ge(sem("x_peer0"), 8)
                attention()
                norm_gain(3)
            if stages > 3:
                peer_first(1)
                peer_second(1)

        @block.scalar
        def _(act):
            def norm(j):
                act.wait_ge(sem("ms_ready"), j + 1)
                nc.scalar.activation(rootms[:, :], meansq[:, :], ACT.Sqrt).then_inc(sem("root_ready"), 1)
                for tb in range(TB):
                    for half in range(2):
                        act.wait_ge(sem("hT_tr"), 8 * j + 2 * tb + half + 1)
                        nc.scalar.copy(hT[0][:, 4 * half:4 * half + 4, tb * P:(tb + 1) * P],
                                       pb[4 + 2 * (tb % 2) + half][:, :].rearrange("p (k t) -> p k t", k=4)) \
                            .then_inc(sem("hT_hi"), 1)

            def gelu_v(c, h):
                for tb in range(TB):
                    act.wait_ge(sem("z_evac"), h * 8 + 4 * c + tb + 1 + 4)
                    nc.scalar.activation(vmix[:, bass.ds(h * 2 + c, 1), tb, :], zt[:, tb % 2:tb % 2 + 1, :],
                                         ACT.Gelu_apprx_tanh).then_inc(sem("z_gelu"), 1)
                    if tb == 0:
                        split_hi(act, c + 1, h)

            def gelu_u(c, h):
                for tb in range(TB):
                    act.wait_ge(sem("z_evac"), h * 8 + 4 * c + tb + 1 + 4)
                    act.wait_ge(sem("y_done"), h * 8 + 4 * (c - G_U) + tb - 2 + 1 + 2)
                    nc.scalar.activation(ugel[:, tb % 2, :], zt[:, tb % 2, :],
                                         ACT.Gelu_apprx_tanh).then_inc(sem("z_gelu"), 1)
                    if tb == 0:
                        split_hi(act, c + 1, h)
                    if tb >= 1:
                        y_hi(c, h, tb - 1)
                y_hi(c, h, TB - 1)

            def y_hi(c, h, tb):
                act.wait_ge(sem("y_tr"), h * 8 + 4 * (c - G_U) + tb + 1 + 2)
                nc.scalar.copy(vmix[:, bass.ds(h * 2 + c - G_U, 1), tb, 0:256].bitcast(BF16),
                               pb[4 + tb % 2][:, :].rearrange("p (o n) -> p o n", o=1)).then_inc(sem("y_hi"), 1)

            def gmlp():
                act.sem_inc(sem("y_done"), 2)
                with act.Fori(0, NCH_Z // 2) as i:
                    for k in range(2):
                        gelu_v(G_V + k, i)
                act.wait_ge(sem("lnv_ready"), 1)
                nc.scalar.activation(ln_sd[:, :], ln_ve[:, :], ACT.Sqrt).then_inc(sem("lnsd_ready"), 1)
                act.wait_ge(sem("bs_loaded"), 16)
                for c in range(NCH_Z):
                    for tb in range(TB):
                        idx = c * TB + tb
                        act.wait_ge(sem("mix_mm"), idx + 1)
                        at = 0
                        while at < 512:
                            g = (c * 512 + at) // GW
                            w = min(512, (g + 1) * GW - c * 512) - at
                            last = nc.scalar.activation(vmix[:, c, tb, at:at + w], pb[4 + idx % 4][:, at:at + w],
                                                        ACT.Identity, bias=bsT[:, g:g + 1])
                            at += w
                        last.then_inc(sem("mix_evac"), 1)
                with act.Fori(0, NCH_Z // 2) as i:
                    for k in range(2):
                        gelu_u(G_U + k, i)
                for c in range(G_OUT, G_OUT + NCH_OUT):
                    split_hi(act, c + 1)

            def query(layer):
                base, n = G_PEER[layer], f"{layer}"
                act.sem_inc(sem("q_evac" + n), 4)
                with act.Fori(0, NCH_Q // 2) as i:
                    for k in range(2):
                        for f in range(4):
                            wait_output(act, sem("q_mm" + n), base + k, base, f, i)
                            nc.scalar.copy(pqT[:, bass.ds(i * 8 + 4 * k + f, 1), :],
                                           pb[f][:, :].rearrange("p (o n) -> p o n", o=1)) \
                                .then_inc(sem("q_evac" + n), 1)
                            if f == 0:
                                split_hi(act, base + k + 1, i)
                for idx in range(4 * TB):
                    act.wait_ge(sem("s_mm" + n), idx + 1)
                    nc.scalar.copy(scores[:, idx // 4, 512 * (idx % 4):512 * (idx % 4) + 512],
                                   pb[4 + idx % 4][:, :]).then_inc(sem("s_evac" + n), 1)

            def gelu_tile(layer, k, e, h, first):
                n, b = f"{layer}", k % 2
                base = G_PEER[layer] + NCH_Q
                if e == 0:
                    act.wait_ge(sem("sstage_free" + n), h * 2 + first + k + 1)
                wait_output(act, sem("u_mm" + n), base + first + k, base, e, h)
                nc.scalar.activation(sstage[:, b, e, :], pb[e][:, :],
                                     ACT.Gelu_apprx_tanh).then_inc(sem("gelu_done" + n), 1)
                if e == 0:
                    split_hi(act, base + first + k + 1, h)

            def experts_first(layer):
                n = f"{layer}"
                act.sem_inc(sem("gelu_done" + n), 4)
                with act.Fori(0, TB) as i:
                    act.wait_ge(sem("sel_ready" + n), i + 1)
                    nc.scalar.copy(sblk[:, :, :].rearrange("p j n -> p (j n)").rearrange("p (o n) -> p o n", o=1),
                                   scores[:, bass.ds(i, 1), :]).then_inc(sem("sblk_ready" + n), 1)
                    for k in range(4):
                        for e in range(4):
                            if k == 3 and e == 3:
                                act.wait_ge(sem("best_ready" + n), i + 1)
                                nc.scalar.activation(best[:, :, :], best[:, :, :],
                                                     ACT.Exp).then_inc(sem("best_exp" + n), 1)
                            gelu_tile(layer, k, e, i * 2, 0)
                    act.wait_ge(sem("sel_tr" + n), i + 2)
                    nc.scalar.copy(selT[:, :, bass.ds(i * P, P)],
                                   pb[4][:, 0:384].rearrange("p (s t) -> p s t", s=3)) \
                        .then_inc(sem("selT_ready" + n), 1)
                act.sem_inc(sem("gate_evac" + n), 2)
                with act.Fori(0, TB) as i:
                    for k in range(4):
                        b = k % 2
                        for e in range(4):
                            gelu_tile(layer, k, e, i * 2, NCH_E // 2)
                            for q in (2 * e, 2 * e + 1):
                                if q == 0:
                                    act.wait_ge(sem("gstage_free" + n), i * 4 + k + 1)
                                act.wait_ge(sem("gate_mm" + n), i * 32 + 8 * k + q + 1 + 8)
                                nc.scalar.copy(gstage[:, b, :, 4 * q:4 * q + 4].rearrange("p e t -> p t e"),
                                               pb[5 + q % 2][:, :].rearrange("p (t e) -> p t e", t=4)) \
                                    .then_inc(sem("gate_evac" + n), 1)

            def h_hi(layer, k, h):
                n = f"{layer}"
                act.wait_ge(sem("hf_ready" + n), h * 2 + k + 1)
                nc.scalar.copy(hsp[k % 2][0][:, :, :].rearrange("p e t -> p (e t)"), hf[:, k % 2, :]) \
                    .then_inc(sem("h_hi" + n), 1)

            def experts_second(layer):
                base = G_PEER[layer] + NCH_Q + NCH_E
                h_hi(layer, 0, 0)
                with act.Fori(0, NCH_E // 2 - 1) as i:
                    for k in range(2):
                        split_hi(act, base + k + 1, i)
                        h_hi(layer, k + 1, i)
                split_hi(act, base + NCH_E - 1)
                h_hi(layer, NCH_E - 1, 0)
                if base + NCH_E < CHUNKS:
                    split_hi(act, base + NCH_E)

            def attention():
                for c in range(NCH_QKV):
                    split_hi(act, G_QKV + c + 1)
                for tb in range(TB):
                    act.wait_ge(sem("hms_ready"), tb + 1)
                    nc.scalar.activation(hrt[:, :], hss[:, :], ACT.Sqrt).then_inc(sem("hroot_ready"), 1)
                    for half in range(2):
                        act.wait_ge(sem("qk_tr"), 3 * tb + half + 1)
                        nc.scalar.copy(qT[:, 4 * half:4 * half + 4, tb * P:(tb + 1) * P],
                                       pb[4 + half][:, :].rearrange("p (k t) -> p k t", k=4)) \
                            .then_inc(sem("qk_T"), 1)
                    act.wait_ge(sem("qk_tr"), 3 * tb + 3)
                    nc.scalar.copy(kT[:, :, tb * P:(tb + 1) * P],
                                   pb[6][:, 0:256].rearrange("p (k t) -> p k t", k=2)).then_inc(sem("qk_T"), 1)
                for tb in range(TB):
                    lo = 64 if tb else 128
                    act.wait_ge(sem("shifted"), tb + 1)
                    nc.scalar.activation(esink[:, :], esink[:, :], ACT.Exp).then_inc(sem("sink_exp"), 1)
                    nc.scalar.activation(prob[:, :, lo:256], prob[:, :, lo:256], ACT.Exp).then_inc(sem("prob_exp"), 1)
                    for j in range(8):
                        idx = 8 * tb + j
                        act.wait_ge(sem("prob_tr"), idx + 1)
                        if idx >= 4:
                            act.wait_ge(sem("pv_mm"), idx - 3)
                        cols = slice(0, 512) if tb else slice(0, 256)
                        nc.scalar.copy(probT[:, j % 4, cols], pb[4 + j % 4][:, cols]).then_inc(sem("probT_ready"), 1)
                    for half in range(2):
                        act.wait_ge(sem("pv_mm"), 8 * tb + 4 * half + 4)
                        nc.scalar.copy(hT[0][:, 4 * half:4 * half + 4, tb * P:(tb + 1) * P],
                                       pb[half][:, :].rearrange("p (k t) -> p k t", k=4)).then_inc(sem("oT_hi"), 1)
                for c in range(NCH_O):
                    split_hi(act, G_WO + c + 1)

            split_hi(act, 0)
            norm(0)
            gmlp()
            norm(1)
            if stages > 1:
                query(0)
                experts_first(0)
                experts_second(0)
            if stages > 2:
                norm(2)
                attention()
                norm(3)
            if stages > 3:
                query(1)
                experts_first(1)
                experts_second(1)

        @block.vector
        def _(dve):
            chain = Chain(dve, "dve_chain")
            link = chain.link

            def norm(j):
                for tb in range(TB):
                    link(nc.vector.tensor_tensor_reduce(out=hn[:, tb % 2, :], in0=xres[:, tb, :], in1=xres[:, tb, :],
                                                        scale=1.0, scalar=0.0, op0=ALU.mult, op1=ALU.add,
                                                        accum_out=sumsq[:, tb:tb + 1]))
                nc.vector.tensor_scalar(meansq[:, :], sumsq[:, :], 1.0 / D, EPS, ALU.mult,
                                        ALU.add).then_inc(sem("ms_ready"), 1)
                dve.wait_ge(sem("root_ready"), j + 1)
                link(nc.vector.reciprocal(rstd[:, :], rootms[:, :]))
                dve.wait_ge(sem("gain_loaded"), 16 * (j + 1))
                for tb in range(TB + 1):
                    if tb < TB:
                        if tb >= 2:
                            dve.wait_ge(sem("hT_tr"), 8 * j + 2 * (tb - 1))
                        nc.vector.scalar_tensor_tensor(hn[:, tb % 2, :], xres[:, tb, :], rstd[:, tb:tb + 1],
                                                       gain[:, :], ALU.mult, ALU.mult).then_inc(sem("hn_ready"), 1)
                    if tb >= 1:
                        for half in range(2):
                            dve.wait_ge(sem("hT_hi"), 8 * j + 2 * (tb - 1) + half + 1)
                            at = (slice(None), slice(4 * half, 4 * half + 4), slice((tb - 1) * P, tb * P))
                            nc.vector.tensor_tensor(hT[1][at],
                                                    pb[4 + 2 * ((tb - 1) % 2) + half][:, :].rearrange("p (k t) -> p k t", k=4),
                                                    hT[0][at], ALU.subtract).then_inc(sem("hT_lo"), 1)

            def add_rows(row, waited):
                dve.wait_ge(sem(waited), 16)
                for tb in range(TB):
                    nc.vector.tensor_tensor(xres[:, tb, :], xres[:, tb, :], row[:, :], ALU.add) \
                        .then_inc(sem("bias_added"), 1)

            def bias_z(c, tb, h):
                if tb == 0:
                    dve.wait_ge(sem(f"zbias_loaded{c % 2}"), h * 16 + 16 * (c // 2 + 1))
                wait_output(dve, sem("z_mm"), c, 0, tb, h)
                dve.wait_ge(sem("z_gelu"), h * 8 + 4 * c + tb + 1)
                nc.vector.tensor_tensor(zt[:, tb % 2, :], pb[tb][:, :], zbias[:, c % 2, :],
                                        ALU.add).then_inc(sem("z_evac"), 1)

            def y_block(c, tb, h):
                dve.wait_ge(sem("z_gelu"), h * 8 + 4 * c + tb + 1 + 2)
                dve.wait_ge(sem("y_tr"), h * 8 + 4 * (c - G_U) + tb + 1)
                nc.vector.tensor_tensor(ytok[:, tb % 2:tb % 2 + 1, :], ugel[:, tb % 2:tb % 2 + 1, :],
                                        vmix[:, bass.ds(h * 2 + c - G_U, 1), tb, :], ALU.mult) \
                    .then_inc(sem("y_done"), 1)

            def y_lo(c, tb, h):
                dve.wait_ge(sem("y_hi"), h * 8 + 4 * (c - G_U) + tb + 1)
                at = bass.ds(h * 2 + c - G_U, 1)
                nc.vector.tensor_tensor(vmix[:, at, tb, 256:512].bitcast(BF16),
                                        pb[4 + tb % 2][:, :].rearrange("p (o n) -> p o n", o=1),
                                        vmix[:, at, tb, 0:256].bitcast(BF16), ALU.subtract) \
                    .then_inc(sem("y_lo"), 1)

            def gmlp():
                dve.sem_inc(sem("z_evac"), 4)
                dve.sem_inc(sem("z_gelu"), 2)
                dve.sem_inc(sem("y_lo"), 2)
                with dve.Fori(0, NCH_Z // 2) as i:
                    for k in range(2):
                        for tb in range(TB):
                            bias_z(G_V + k, tb, i)
                            if tb == 0:
                                split_lo(dve, G_V + k + 1, i)
                dve.wait_ge(sem("z_gelu"), 2 + 4 * NCH_Z)
                dve.wait_ge(sem("ln_loaded"), 32)
                for tb in range(TB):
                    for c in range(NCH_Z):
                        last = nc.vector.bn_stats(bn[:, c, :], vmix[:, c, tb, :])
                    link(last)
                    link(nc.vector.bn_aggr(ln_mv[:, tb, :], bn[:, :, :].rearrange("p c s -> p (c s)")))
                nc.vector.tensor_scalar(ln_ve[:, :], ln_mv[:, :, 1], EPS, None, ALU.add).then_inc(sem("lnv_ready"), 1)
                dve.wait_ge(sem("lnsd_ready"), 1)
                link(nc.vector.reciprocal(ln_rs[:, :], ln_sd[:, :]))
                for c in range(NCH_Z):
                    cols = slice(512 * c, 512 * c + 512)
                    for tb in range(TB):
                        v = vmix[:, c, tb, :]
                        last = nc.vector.tensor_scalar(v, v, ln_mv[:, tb, 0:1], ln_rs[:, tb:tb + 1],
                                                       ALU.subtract, ALU.mult)
                    link(last)
                    for tb in range(TB):
                        v = vmix[:, c, tb, :]
                        last = nc.vector.tensor_tensor(v, v, ln_g[:, cols], ALU.mult)
                    link(last)
                    for tb in range(TB):
                        v = vmix[:, c, tb, :]
                        nc.vector.tensor_tensor(v, v, ln_b[:, cols], ALU.add).then_inc(sem("vn_ready"), 1)
                dve.wait_ge(sem("mix_evac"), TB * NCH_Z)
                with dve.Fori(0, NCH_Z // 2) as i:
                    for k in range(2):
                        c = G_U + k
                        for tb in range(TB):
                            bias_z(c, tb, i)
                            if tb == 0:
                                split_lo(dve, c + 1, i)
                            if tb >= 1:
                                y_lo(c, tb - 1, i)
                            y_block(c, tb, i)
                        y_lo(c, TB - 1, i)
                for c in range(G_OUT, G_OUT + NCH_OUT):
                    split_lo(dve, c + 1)
                mixer_out("zo_mm", 0, [G_OUT + 2, G_OUT + 5])

            def mixer_out(mm, layer, chunks):
                dve.wait_ge(sem("bias_added"), 4 * (layer + 1))
                for half in range(2):
                    for tb in range(TB):
                        if tb < 3:
                            dve.wait_ge(sem(mm), 3 * half + tb + 1)
                        else:
                            dve.wait_ge(chunk_used, chunks[half] + 1 + CREDIT)
                        nc.vector.tensor_tensor(xres[:, tb, 512 * half:512 * half + 512],
                                                xres[:, tb, 512 * half:512 * half + 512],
                                                pb[4 * half + tb][:, :], ALU.add).then_inc(mixer_done(layer), 1)
                dve.wait_ge(mixer_done(layer), 8)

            def query(layer):
                base = G_PEER[layer]
                with dve.Fori(0, NCH_Q // 2) as i:
                    for k in range(2):
                        split_lo(dve, base + k + 1, i)

            def top16(values, index, src, spare):
                rows = range(len(src))
                for r in rows:
                    last = nc.vector.max(values[r][:, 0:8], src[r])
                link(last)
                for r in rows:
                    nc.vector.max_index(index[r][:, 0:8], values[r][:, 0:8], src[r])
                    last = nc.vector.match_replace(spare[r], values[r][:, 0:8], src[r], LOWEST)
                link(last)
                for r in rows:
                    last = nc.vector.max(values[r][:, 8:16], spare[r])
                link(last)
                for r in rows:
                    last = nc.vector.max_index(index[r][:, 8:16], values[r][:, 8:16], spare[r])
                link(last)

            def retrieve(k):
                js = range(4 * k, 4 * k + 4)
                top16([topv[:, j, :] for j in js], [topi[:, j, :] for j in js], [sblk[:, j, :] for j in js],
                      [work[:, P * r:P * r + P] for r in range(4)])
                for r in range(2):
                    a, b = topv[:, 4 * k + 2 * r, :], topv[:, 4 * k + 2 * r + 1, :]
                    last = nc.vector.tensor_tensor(cand[:, r, :].rearrange("p (a b) -> p a b", a=TOPK),
                                                   a.unsqueeze(2).broadcast_to([P, TOPK, TOPK]),
                                                   b.unsqueeze(1).broadcast_to([P, TOPK, TOPK]), ALU.add)
                link(last)
                top16([best[:, 2 * k + r, :] for r in range(2)], [bestp[:, 2 * k + r, :] for r in range(2)],
                      [cand[:, r, :] for r in range(2)], [work[:, 256 * r:256 * r + 256] for r in range(2)])

            def select(layer, i):
                n = f"{layer}"
                link(nc.vector.tensor_tensor(sel[:, 2, :].rearrange("p (h k) -> p h k", h=PH), best[:, :, :],
                                             best[:, :, 0:1].broadcast_to([P, PH, TOPK]), ALU.subtract))
                nc.vector.tensor_copy(best[:, :, :], sel[:, 2, :].rearrange("p (h k) -> p h k", h=PH)) \
                    .then_inc(sem("best_ready" + n), 1)
                flat = bestp[:, :, :].rearrange("p h k -> p (h k)")
                nc.vector.tensor_scalar(posn[:, 0, :], flat, 4, None, ALU.logical_shift_right)
                link(nc.vector.tensor_scalar(posn[:, 1, :], flat, 15, None, ALU.bitwise_and))
                nc.vector.tensor_copy(topif[:, :, :], topi[:, :, :])
                link(nc.vector.tensor_copy(posf[:, :, :], posn[:, :, :]))
                for s in range(2):
                    link(nc.vector.tensor_tensor(onehot[:, :, :], posf[:, s, :].unsqueeze(2).broadcast_to([P, P, TOPK]),
                                                 iota[:, 0:TOPK].unsqueeze(1).broadcast_to([P, P, TOPK]),
                                                 ALU.is_equal))
                    idx = topif[:, :, :].rearrange("p (h s) j -> p s h j", s=2)[:, s, :, :]
                    hot = onehot[:, :, :].rearrange("p (h k) j -> p h k j", h=PH)
                    link(nc.vector.tensor_tensor(hot, hot, idx.unsqueeze(2).broadcast_to([P, PH, TOPK, TOPK]),
                                                 ALU.mult))
                    link(nc.vector.tensor_reduce(sel[:, s, :], onehot[:, :, :], AX_X, ALU.add))
                dve.wait_ge(sem("best_exp" + n), i + 1)
                link(nc.vector.tensor_reduce(gsum[:, :], best[:, :, :], AX_X, ALU.add))
                link(nc.vector.reciprocal(grec[:, :], gsum[:, :]))
                nc.vector.tensor_tensor(sel[:, 2, :].rearrange("p (h k) -> p h k", h=PH), best[:, :, :],
                                        grec[:, :].unsqueeze(2).broadcast_to([P, PH, TOPK]),
                                        ALU.mult).then_inc(sem("sel_ready" + n), 1)

            def experts_first(layer):
                n, base = f"{layer}", G_PEER[layer] + NCH_Q
                dve.wait_ge(sem("iota_ready"), 1)
                dve.sem_inc(sem("sel_ready" + n), 1)
                with dve.Fori(0, TB) as i:
                    chain.restart()
                    dve.wait_ge(sem("sel_tr" + n), i + 1)
                    dve.wait_ge(sem("sblk_ready" + n), i + 1)
                    for k in range(4):
                        split_lo(dve, base + k + 1, i * 2)
                        retrieve(k)
                    select(layer, i)
                dve.wait_ge(sem("selT_ready" + n), TB)
                with dve.Fori(0, TB) as i:
                    chain.restart()
                    for k in range(4):
                        split_lo(dve, base + NCH_E // 2 + k + 1, i * 2)
                        link(nc.vector.tensor_copy(tslice[:, :, :], selT[:, :, bass.ds(i * P + BT * k, BT)]))
                        for s in range(2):
                            dve.wait_ge(sem("gate_mm" + n), i * 32 + 8 * k + 4 * s + 4)
                            for t in range(16):
                                u = 16 * s + t
                                nc.vector.tensor_scalar(oh1[:, s, t, :], iota[:, :], tslice[:, 0, u:u + 1], None,
                                                        ALU.is_equal)
                                last = nc.vector.tensor_scalar(goh2[:, s, t, :], iota[:, :], tslice[:, 1, u:u + 1],
                                                               tslice[:, 2, u:u + 1], ALU.is_equal, ALU.mult)
                            last.then_inc(sem("hot_ready" + n), 1)

            def h_parts(layer, k, h):
                n, b = f"{layer}", k % 2
                dve.wait_ge(sem(f"sa_loaded{b}"), h * 32 + 32 * (k // 2 + 1 + layer * NCH_E // 2))
                acts = s_in[:, b, :].rearrange("p (e g t) -> p e g t", e=4, t=BT)
                gates = a_in[:, b, :].rearrange("p (g e t) -> p e g t", e=4, t=BT)
                nc.vector.tensor_tensor(hf[:, b, :].rearrange("p (e g t) -> p e g t", e=4, t=BT), acts, gates,
                                        ALU.mult).then_inc(sem("hf_ready" + n), 1)
                dve.wait_ge(sem("h_hi" + n), h * 2 + k + 1)
                nc.vector.tensor_tensor(hsp[b][1][:, :, :].rearrange("p e t -> p (e t)"), hf[:, b, :],
                                        hsp[b][0][:, :, :].rearrange("p e t -> p (e t)"), ALU.subtract) \
                    .then_inc(sem("h_ready" + n), 1)

            def experts_second(layer):
                n, base = f"{layer}", G_PEER[layer] + NCH_Q + NCH_E
                dve.sem_inc(sem("h_ready" + n), 2)
                h_parts(layer, 0, 0)
                with dve.Fori(0, NCH_E // 2 - 1) as i:
                    for k in range(2):
                        split_lo(dve, base + k + 1, i)
                        h_parts(layer, k + 1, i)
                split_lo(dve, base + NCH_E - 1)
                h_parts(layer, NCH_E - 1, 0)
                if base + NCH_E < CHUNKS:
                    split_lo(dve, base + NCH_E)
                done = sem(f"x_peer{layer}") if layer == 0 and stages > 2 else sem("x_final")
                dve.wait_ge(sem("v_mm" + n), 1)
                for tb in range(TB):
                    for half in range(2):
                        cols = slice(512 * half, 512 * half + 512)
                        nc.vector.tensor_tensor(xres[:, tb, cols], xres[:, tb, cols], pb[2 * tb + half][:, :],
                                                ALU.add).then_inc(done, 1)
                dve.wait_ge(done, 8)

            def rope_block(tb):
                b = tb % 2
                q = qkv[:, tb, 0:QK]
                heads = QK // HD
                if tb:
                    dve.wait_ge(sem("qr_ready"), tb)
                link(nc.vector.tensor_tensor(sq[:, :], q, q, ALU.mult))
                link(nc.vector.tensor_reduce(hss[:, :], sq[:, :].rearrange("p (h d) -> p h d", d=HD), AX_X, ALU.add))
                nc.vector.tensor_scalar(hss[:, :], hss[:, :], 1.0 / HD, EPS, ALU.mult,
                                        ALU.add).then_inc(sem("hms_ready"), 1)
                dve.wait_ge(sem("hroot_ready"), tb + 1)
                link(nc.vector.reciprocal(hrs[:, :], hrt[:, :]))
                qh = q.rearrange("p (h d) -> p h d", d=HD)
                link(nc.vector.tensor_tensor(qh, qh, hrs[:, :].unsqueeze(2).broadcast_to([P, heads, HD]), ALU.mult))
                nc.vector.tensor_tensor(qh[:, 0:HEADS, :], qh[:, 0:HEADS, :],
                                        qkg[:, 0, :].unsqueeze(1).broadcast_to([P, HEADS, HD]), ALU.mult)
                link(nc.vector.tensor_tensor(qh[:, HEADS:, :], qh[:, HEADS:, :],
                                             qkg[:, 1, :].unsqueeze(1).broadcast_to([P, heads - HEADS, HD]), ALU.mult))
                cos = tabs[:, 0, tb, :].unsqueeze(1).broadcast_to([P, heads, HD // 2])
                sin = tabs[:, 1, tb, :].unsqueeze(1).broadcast_to([P, heads, HD // 2])
                x1, x2 = qh[:, :, 0:HD // 2], qh[:, :, HD // 2:]
                o = qr[:, b, :].rearrange("p (h d) -> p h d", d=HD)
                t1 = sq[:, 0:QK // 2].rearrange("p (h d) -> p h d", d=HD // 2)
                t2 = sq[:, QK // 2:].rearrange("p (h d) -> p h d", d=HD // 2)
                if tb >= 2:
                    dve.wait_ge(sem("qk_tr"), 3 * (tb - 1))
                nc.vector.tensor_tensor(t1, x1, cos, ALU.mult)
                link(nc.vector.tensor_tensor(t2, x2, sin, ALU.mult))
                link(nc.vector.tensor_tensor(o[:, :, 0:HD // 2], t1, t2, ALU.subtract))
                nc.vector.tensor_tensor(t1, x2, cos, ALU.mult)
                link(nc.vector.tensor_tensor(t2, x1, sin, ALU.mult))
                nc.vector.tensor_tensor(o[:, :, HD // 2:], t1, t2, ALU.add).then_inc(sem("qr_ready"), 1)

            def softmax_block(tb):
                lo = 64 if tb else 128
                width = 256 - lo
                byp = prob[:, :, :].rearrange("p (m s) k -> p m s k", m=4).rearrange("p m (q r) k -> p m r q k", r=2)
                for j in range(8):
                    dve.wait_ge(sem("qk_mm"), 8 * tb + j // 2 * 2 + 2)
                    src = pb[j][:, :].rearrange("p (h k) -> p h k", h=2)[:, :, 0:width]
                    last = nc.vector.scalar_tensor_tensor(
                        byp[:, j // 2, j % 2, :, lo:256], src, HD ** -0.5,
                        mask[:, 192 - width:192].unsqueeze(1).broadcast_to([P, 2, width]), ALU.mult, ALU.add)
                link(last)
                pr = prob[:, :, lo:256]
                link(nc.vector.tensor_reduce(smax[:, :], pr, AX_X, ALU.max))
                link(nc.vector.tensor_tensor(smax[:, :], smax[:, :], sink[:, :], ALU.max))
                nc.vector.tensor_tensor(esink[:, :], sink[:, :], smax[:, :], ALU.subtract)
                nc.vector.tensor_tensor(pr, pr, smax[:, :].unsqueeze(2).broadcast_to([P, HEADS, width]),
                                        ALU.subtract).then_inc(sem("shifted"), 1)
                dve.wait_ge(sem("prob_exp"), tb + 1)
                link(nc.vector.tensor_reduce(ssum[:, :], pr, AX_X, ALU.add))
                link(nc.vector.tensor_tensor(ssum[:, :], ssum[:, :], esink[:, :], ALU.add))
                link(nc.vector.reciprocal(srec[:, :], ssum[:, :]))
                nc.vector.tensor_tensor(pr, pr, srec[:, :].unsqueeze(2).broadcast_to([P, HEADS, width]),
                                        ALU.mult).then_inc(sem("prob_ready"), 1)
                for half in range(2):
                    dve.wait_ge(sem("oT_hi"), 2 * tb + half + 1)
                    at = (slice(None), slice(4 * half, 4 * half + 4), slice(tb * P, (tb + 1) * P))
                    nc.vector.tensor_tensor(hT[1][at], pb[half][:, :].rearrange("p (k t) -> p k t", k=4),
                                            hT[0][at], ALU.subtract).then_inc(sem("oT_lo"), 1)

            def attention():
                dve.wait_ge(sem("attn_loaded"), 64)
                dve.wait_ge(sem("mask_ready"), 2)
                for c in range(NCH_QKV):
                    for tb in range(TB):
                        wait_output(dve, sem("qkv_mm"), G_QKV + c, G_QKV, tb)
                        nc.vector.tensor_tensor(qkv[:, tb, 512 * c:512 * c + 512], pb[tb][:, :],
                                                qbias[:, 512 * c:512 * c + 512], ALU.add) \
                            .then_inc(sem("qkv_evac"), 1)
                        if tb == 0:
                            split_lo(dve, G_QKV + c + 1)
                dve.wait_ge(sem("qkv_evac"), 4 * NCH_QKV)
                link(nc.vector.memset(prob[:, :, 0:64], 0.0))
                for tb in range(TB):
                    rope_block(tb)
                for tb in range(TB):
                    if tb:
                        dve.wait_ge(sem("prob_tr"), 8 * tb)
                    softmax_block(tb)
                for c in range(NCH_O):
                    split_lo(dve, G_WO + c + 1)
                mixer_out("ao_mm", 1, [G_WO, G_WO + 1])

            dve.sem_inc(lo_done, CREDIT)
            dve.wait_ge(sem("x_loaded"), 16)
            split_lo(dve, 0)
            norm(0)
            add_rows(bout, "bout_loaded")
            gmlp()
            norm(1)
            if stages > 1:
                query(0)
                experts_first(0)
                experts_second(0)
            if stages > 2:
                norm(2)
                add_rows(bo, "bo_loaded")
                attention()
                norm(3)
            if stages > 3:
                query(1)
                experts_first(1)
                experts_second(1)

        @block.tensor
        def _(pe):
            def norm(j):
                for tb in range(TB):
                    pe.wait_ge(sem("hn_ready"), 4 * j + tb + 1)
                    for half in range(2):
                        if tb >= 2:
                            pe.wait_ge(sem("hT_lo"), 8 * j + 2 * (tb - 2) + half + 1)
                        for k in range(4):
                            f = 4 * half + k
                            last = nc.tensor.transpose(pb[4 + 2 * (tb % 2) + half][:, k * P:(k + 1) * P],
                                                       hn[:, tb % 2, f * P:(f + 1) * P], ident[:, :])
                        last.then_inc(sem("hT_tr"), 1)
                pe.wait_ge(sem("hT_lo"), 8 * (j + 1))

            def z_chunk(c, h, gated):
                wait_chunk(pe, c, h)
                for tb in range(TB):
                    pe.wait_ge(sem("z_evac"), h * 8 + 4 * c + tb + 1)
                    token_chunk(pb[tb], c, tb, h_lhs).then_inc(sem("z_mm") if tb < 3 else chunk_used, 1)
                    if gated and tb >= 1:
                        y_transpose(c, tb - 1, h)
                if gated:
                    y_transpose(c, TB - 1, h)

            def y_transpose(c, tb, h):
                pe.wait_ge(sem("y_done"), h * 8 + 4 * (c - G_U) + tb + 1 + 2)
                pe.wait_ge(sem("y_lo"), h * 8 + 4 * (c - G_U) + tb + 1)
                for f in range(4):
                    last = nc.tensor.transpose(pb[4 + tb % 2][:, f * P:(f + 1) * P],
                                               ytok[:, tb % 2, f * P:(f + 1) * P], ident[:, :])
                last.then_inc(sem("y_tr"), 1)

            def gmlp():
                pe.sem_inc(sem("y_tr"), 2)
                with pe.Fori(0, NCH_Z // 2) as i:
                    for k in range(2):
                        z_chunk(G_V + k, i, False)
                pe.wait_ge(sem("ws_masked"), 1)
                for c in range(NCH_Z):
                    for tb in range(TB):
                        idx = c * TB + tb
                        pe.wait_ge(sem("vn_ready"), idx + 1)
                        if idx >= 4:
                            pe.wait_ge(sem("mix_evac"), idx - 3)
                        at = 0
                        while at < 512:
                            g = (c * 512 + at) // GW
                            w = min(512, (g + 1) * GW - c * 512) - at
                            last = nc.tensor.matmul(pb[4 + idx % 4][:, at:at + w], wsT[:, g, :],
                                                    vmix[:, c, tb, at:at + w], start=True, stop=True)
                            at += w
                        last.then_inc(sem("mix_mm"), 1)
                pe.wait_ge(sem("mix_evac"), NCH_Z * TB)
                with pe.Fori(0, NCH_Z // 2) as i:
                    for k in range(2):
                        z_chunk(G_U + k, i, True)
                pe.wait_ge(sem("y_lo"), 2 + NCH_Z * TB)
                for n in range(2):
                    for kg in range(3):
                        c = G_OUT + 3 * n + kg
                        wait_chunk(pe, c)
                        for tb in range(TB):
                            mm = token_chunk(pb[4 * n + tb], c, tb,
                                             lambda k, t, part: yT(2 * kg + k // 4, t, part)[:, k % 4, :],
                                             first=kg == 0, last=kg == 2)
                            if kg == 2 and tb < 3:
                                mm.then_inc(sem("zo_mm"), 1)
                        mm.then_inc(chunk_used, 1)

            def query(layer):
                base, n = G_PEER[layer], f"{layer}"
                with pe.Fori(0, NCH_Q // 2) as i:
                    for k in range(2):
                        wait_chunk(pe, base + k, i)
                        for f in range(4):
                            pe.wait_ge(sem("q_evac" + n), i * 8 + 4 * k + f + 1)
                            feature_chunk(pb[f], base + k, f).then_inc(sem("q_mm" + n) if f < 3 else chunk_used, 1)
                pe.wait_ge(sem("q_evac" + n), 4 + 16)
                pe.wait_ge(sem("keys_loaded"), 16 * (layer + 1))
                for idx in range(4 * TB):
                    tb = idx // 4
                    if idx >= 4:
                        pe.wait_ge(sem("s_evac" + n), idx - 3)
                    for r in range(4):
                        j = 4 * (idx % 4) + r
                        last = nc.tensor.matmul(pb[4 + idx % 4][:, r * P:(r + 1) * P], pqT[:, j, tb * P:(tb + 1) * P],
                                                keysT[:, j % 2, :], start=True, stop=True)
                    last.then_inc(sem("s_mm" + n), 1)

            def expert_tile(layer, k, e, h, first):
                n = f"{layer}"
                base = G_PEER[layer] + NCH_Q
                if e == 0:
                    wait_chunk(pe, base + first + k, h)
                pe.wait_ge(sem("gelu_done" + n), h * 8 + 4 * (first + k) + e + 1)
                feature_chunk(pb[e], base + first + k, e).then_inc(sem("u_mm" + n) if e < 3 else chunk_used, 1)

            def experts_first(layer):
                n = f"{layer}"
                pe.sem_inc(sem("sel_tr" + n), 1)
                with pe.Fori(0, TB) as i:
                    for k in range(4):
                        for e in range(4):
                            expert_tile(layer, k, e, i * 2, 0)
                    pe.wait_ge(sem("sel_ready" + n), i + 2)
                    for s in range(3):
                        last = nc.tensor.transpose(pb[4][:, s * P:(s + 1) * P], sel[:, s, :], ident[:, :])
                    last.then_inc(sem("sel_tr" + n), 1)
                pe.sem_inc(sem("gate_mm" + n), 8)
                with pe.Fori(0, TB) as i:
                    for k in range(4):
                        for e in range(4):
                            expert_tile(layer, k, e, i * 2, NCH_E // 2)
                            for q in (2 * e, 2 * e + 1):
                                s = q // 4
                                if q % 4 == 0:
                                    pe.wait_ge(sem("hot_ready" + n), i * 8 + 2 * k + s + 1)
                                pe.wait_ge(sem("gate_evac" + n), i * 32 + 8 * k + q + 1)
                                for t in range(4):
                                    u = 4 * (q % 4) + t
                                    last = nc.tensor.matmul(pb[5 + q % 2][:, t * P:(t + 1) * P], oh1[:, s, u, :],
                                                            goh2[:, s, u, :], start=True, stop=True)
                                last.then_inc(sem("gate_mm" + n), 1)

            def value_chunk(layer, k, h):
                n, c = f"{layer}", G_PEER[layer] + NCH_Q + NCH_E + k
                wait_chunk(pe, c, h)
                pe.wait_ge(sem("h_ready" + n), h * 2 + k + 1 + 2)
                w = [v[:, :].rearrange("p (e n) -> p e n", e=4) for v in wsp[c % 2]]
                for e in range(4):
                    for tb in range(TB):
                        for a, b in ((0, 0), (0, 1), (1, 0)):
                            for half in range(2):
                                mm = nc.tensor.matmul(pb[2 * tb + half][:, :],
                                                      hsp[k % 2][a][:, e, tb * P:(tb + 1) * P],
                                                      w[b][:, e, 512 * half:512 * half + 512],
                                                      start=False, stop=False)
                mm.then_inc(chunk_used, 1)

            def experts_second(layer):
                n = f"{layer}"
                pe.wait_ge(sem("gelu_done" + n), 4 + 4 * NCH_E)
                pe.wait_ge(sem("gate_evac" + n), 2 + SEQ // 4)
                pe.wait_ge(sem("selT_ready" + n), TB)
                for b in range(8):
                    nc.tensor.matmul(pb[b][:, :], zeros[:, 0:P], zeros[:, :], start=True, stop=False)
                with pe.Fori(0, NCH_E // 2) as i:
                    for k in range(2):
                        value_chunk(layer, k, i)
                for b in range(8):
                    last = nc.tensor.matmul(pb[b][:, :], zeros[:, 0:P], zeros[:, :], start=False, stop=True)
                last.then_inc(sem("v_mm" + n), 1)

            def attention():
                for c in range(NCH_QKV):
                    wait_chunk(pe, G_QKV + c)
                    for tb in range(TB):
                        if c:
                            pe.wait_ge(sem("qkv_evac"), 4 * (c - 1) + tb + 1)
                        token_chunk(pb[tb], G_QKV + c, tb, h_lhs) \
                            .then_inc(sem("qkv_mm") if tb < 3 else chunk_used, 1)
                for tb in range(TB):
                    pe.wait_ge(sem("qr_ready"), tb + 1)
                    for part in range(3):
                        if tb:
                            pe.wait_ge(sem("qk_T"), 3 * (tb - 1) + part + 1)
                        for k in range(4 if part < 2 else 2):
                            f = 4 * part + k
                            last = nc.tensor.transpose(pb[4 + part][:, k * P:(k + 1) * P],
                                                       qr[:, tb % 2, f * P:(f + 1) * P], ident[:, :])
                        last.then_inc(sem("qk_tr"), 1)
                pe.wait_ge(sem("qk_T"), 3 * TB)
                pe.wait_ge(sem("qkv_evac"), 4 * NCH_QKV)
                for tb in range(TB):
                    if tb:
                        pe.wait_ge(sem("oT_lo"), 2 * tb)
                    key0 = (tb * P - 64) if tb else 0
                    width = 192 if tb else P
                    for j in range(8):
                        for par in range(2):
                            rows = slice(64 * par, 64 * par + 64)
                            at = 256 * (j % 2)
                            mm = nc.tensor.matmul(pb[j // 2 * 2 + par][:, at:at + width],
                                                  qT[rows, j, tb * P:(tb + 1) * P],
                                                  kT[rows, j // 4, key0:key0 + width], start=True, stop=True)
                            if j % 2:
                                mm.then_inc(sem("qk_mm"), 1)
                    pe.wait_ge(sem("prob_ready"), tb + 1)

                    def prob_transpose(j):
                        if j >= 4:
                            pe.wait_ge(sem("probT_ready"), 8 * tb + j - 3)
                        for at, (par, blk) in enumerate(((0, 1), (1, 1), (0, 0), (1, 0))[:4 if tb else 2]):
                            last = nc.tensor.transpose(pb[4 + j % 4][:, at * P:(at + 1) * P],
                                                       prob[:, 2 * j + par, blk * P:(blk + 1) * P], ident[:, :])
                        last.then_inc(sem("prob_tr"), 1)

                    def weighted(j):
                        pe.wait_ge(sem("probT_ready"), 8 * tb + j + 1)
                        for par in range(2):
                            kv = 2 * (j // 4) + par
                            cols = slice(QK + HD * kv, QK + HD * kv + HD)
                            o = pb[j // 4][64 * par:64 * par + 64, (j % 4) * P:(j % 4 + 1) * P]
                            last = nc.tensor.matmul(o, qkv[:, tb, cols], probT[:, j % 4, par * P:(par + 1) * P],
                                                    start=True, stop=tb == 0)
                            if tb:
                                last = nc.tensor.matmul(o, qkv[:, tb - 1, cols],
                                                        probT[:, j % 4, (2 + par) * P:(3 + par) * P],
                                                        start=False, stop=True)
                        last.then_inc(sem("pv_mm"), 1)

                    for j in range(9):
                        if j < 8:
                            prob_transpose(j)
                        if j:
                            weighted(j - 1)
                pe.wait_ge(sem("oT_lo"), 2 * TB)
                for c in range(NCH_O):
                    wait_chunk(pe, G_WO + c)
                    for tb in range(TB):
                        token_chunk(pb[4 * c + tb], G_WO + c, tb, h_lhs) \
                            .then_inc(sem("ao_mm") if tb < 3 else chunk_used, 1)

            pe.sem_inc(chunk_used, CREDIT)
            pe.wait_ge(sem("ident_ready"), 1)
            pe.wait_ge(sem("zeros_ready"), 1)
            norm(0)
            gmlp()
            norm(1)
            if stages > 1:
                query(0)
                experts_first(0)
                experts_second(0)
            if stages > 2:
                norm(2)
                attention()
                norm(3)
            if stages > 3:
                query(1)
                experts_first(1)
                experts_second(1)


def kernel(stages=4, **inputs):
    import numpy as np
    import concourse.bacc as bacc
    from concourse.bass_utils import run_bass_kernel_spmd

    def get(name):
        return np.asarray(inputs[name])

    def columns(w, n=512):
        return w.reshape(KT, P, -1, n).transpose(2, 1, 0, 3).reshape(-1, P, CH)

    order = np.array([(4 * (2 * m + par) + g) for m in range(2) for g in range(4) for par in range(2)])
    q_cols = (order[:, None] * HD + np.arange(HD)[None, :]).ravel()
    qkv_cols = np.concatenate([q_cols, np.arange(QW, QW + 512)])

    stream = np.empty((CHUNKS, P, CH), np.float32)
    w_in = get("gmlp_w_in")[0]
    stream[G_V:G_V + NCH_Z] = columns(w_in[:, HALF:])
    stream[G_U:G_U + NCH_Z] = columns(w_in[:, :HALF])
    stream[G_OUT:G_OUT + NCH_OUT] = get("gmlp_w_out")[0].reshape(3, 8, P, 2, 512) \
        .transpose(3, 0, 2, 1, 4).reshape(NCH_OUT, P, CH)
    stream[G_QKV:G_QKV + NCH_QKV] = columns(get("attn_w_qkv")[0][:, qkv_cols])
    stream[G_WO:G_WO + NCH_O] = columns(get("attn_w_o")[0][q_cols, :])
    for layer in range(2):
        g = G_PEER[layer]
        stream[g:g + NCH_Q] = columns(get("peer_w_query")[layer])
        u = get("peer_expert_u")[layer].reshape(P, NCH_E, 4, KT, P)
        stream[g + NCH_Q:g + NCH_Q + NCH_E] = u.transpose(1, 4, 3, 2, 0).reshape(NCH_E, P, CH)
        v = get("peer_expert_v")[layer].reshape(P, NCH_E, CH)
        stream[g + NCH_Q + NCH_E:g + NCH_Q + 2 * NCH_E] = v.transpose(1, 0, 2)

    gb = get("gmlp_b_in")[0].reshape(2, NCH_Z, 512)
    mix_g, ffn_g = get("mix_norm_g"), get("ffn_norm_g")
    pos = np.arange(SEQ, dtype=np.float32)
    inv = (1.0 / (10000.0 ** (np.arange(0, HD, 2, dtype=np.float32) / HD))).astype(np.float32)
    ang = pos[:, None] * inv[None, :]
    rope = np.stack([np.cos(ang), np.sin(ang)]).astype(np.float32)
    keys = np.stack([get("peer_keys_1"), get("peer_keys_2")], 1)
    arrays = {
        "x": get("x").reshape(SEQ, D),
        "stream": stream,
        "gains": np.stack([mix_g[0], ffn_g[0], mix_g[1], ffn_g[1]]),
        "gmlp_bias": np.concatenate([gb[1], gb[0]]),
        "ln_gb": np.stack([get("gmlp_ln_g")[0], get("gmlp_ln_b")[0]]),
        "w_s": get("gmlp_w_s")[0].transpose(2, 0, 1),
        "b_s": get("gmlp_b_s")[0].T,
        "b_out": get("gmlp_b_out")[0],
        "qkv_bias": get("attn_b_qkv")[0][qkv_cols],
        "b_o": get("attn_b_o")[0],
        "qk_gain": np.concatenate([get("attn_q_gain")[0], get("attn_k_gain")[0]]),
        "sinks": get("attn_sinks")[0][order],
        "rope": rope.reshape(2, TB, P, HD // 2).transpose(2, 0, 1, 3),
        "keys": keys.transpose(0, 3, 1, 2),
    }
    nc = bacc.Bacc("TRN2", target_bir_lowering=False, num_devices=1)
    arrays = {f"in_{k}": np.ascontiguousarray(a) for k, a in arrays.items()}
    args = [nc.dram_tensor(k, a.shape, mybir.dt.from_np(a.dtype), kind="ExternalInput").ap()
            for k, a in arrays.items()]
    out = nc.dram_tensor("out", (SEQ, D), F32, kind="ExternalOutput").ap()
    build(nc, *args, out, stages=stages)
    r = run_bass_kernel_spmd(nc, [arrays], core_ids=[0])
    return r.results[0]["out"].reshape(1, SEQ, D)
```

```python
from contextlib import ExitStack

import concourse.bass as bass
from concourse import mybir

ALU = mybir.AluOpType
ACT = mybir.ActivationFunctionType
F32 = mybir.dt.float32
BF16 = mybir.dt.bfloat16
U32 = mybir.dt.uint32
AX_X = mybir.AxisListType.X

P = 128
SEQ = 512
D = 1024
TB = SEQ // P
KT = D // P
HALF = 3072
GW = HALF // 8
CH = 4096
NCH_Z = HALF // 512
NCH_OUT = 6
NCH_Q = 4
NCH_E = 32
NCH_QKV = 3
NCH_O = 2
HEADS = 16
HD = 64
QW = HEADS * HD
QK = QW + 256
PH = 8
TOPK = 16
BT = 32
EPS = 1e-6
NEG = -1e30
LOWEST = -3.0e38

G_V, G_U = 0, NCH_Z
G_OUT = 2 * NCH_Z
G_PEER = [G_OUT + NCH_OUT, 0]
G_QKV = G_PEER[0] + NCH_Q + 2 * NCH_E
G_WO = G_QKV + NCH_QKV
G_PEER[1] = G_WO + NCH_O
CHUNKS = G_PEER[1] + NCH_Q + 2 * NCH_E
QUADS = [[], [0, 1, 2], [3, 4], [5, 6, 7]]
UNITS = 2 * TB
AHEAD = 3
CREDIT = 2


def build(nc, x, stream, gains, gmlp_bias, ln_gb, w_s, b_s, b_out, qkv_bias, b_o,
          qk_gain, sinks, rope, keys, out, stages=4):
    with ExitStack() as ctx:
        def sb(name, shape, dt=F32):
            return ctx.enter_context(nc.sbuf_tensor(name, shape, dt))

        sems = {}

        def sem(name):
            if name not in sems:
                sems[name] = ctx.enter_context(nc.semaphore(name))
            return sems[name]

        xres = sb("xres", [P, TB, D])
        hT = [sb("hT_hi", [P, KT, SEQ], BF16), sb("hT_lo", [P, KT, SEQ], BF16)]
        raw = [sb(f"raw{b}", [P, CH]) for b in range(2)]
        wsp = [[sb(f"w_hi{b}", [P, CH], BF16), sb(f"w_lo{b}", [P, CH], BF16)] for b in range(2)]
        gain = sb("gain", [P, D])
        ident = sb("ident", [P, P])
        iota = sb("iota", [P, TOPK])
        iota_b = sb("iota_b", [P, P], BF16)
        epsilon = sb("epsilon", [P, 1])
        zeros = sb("zeros", [P, SEQ], BF16)
        mask = sb("mask", [P, 192])
        sumsq = sb("sumsq", [P, TB])
        rootms = sb("rootms", [P, TB])
        rstd = sb("rstd", [P, TB])
        arena = sb("arena", [P, 26300])
        pb = [ctx.enter_context(nc.psum_tensor(f"bank{i}", [P, 512], F32)) for i in range(8)]

        def area(start, words, dt=F32):
            a = arena[:, start:start + words]
            return a if dt == F32 else a.bitcast(dt)

        s_dram = nc.dram_tensor("acts_scratch", (NCH_E, P, 2048), F32, kind="Internal").ap()
        a_dram = nc.dram_tensor("gates_scratch", (P, SEQ // BT, P * BT), F32, kind="Internal").ap()

        hn = area(24064, 2048).rearrange("p (b n) -> p b n", b=2)
        squares = area(12288, D)

        vmix = area(0, 12288).rearrange("p (c t n) -> p c t n", c=NCH_Z, t=TB)
        zt = area(12288, 1024).rearrange("p (b n) -> p b n", b=2)
        ytok = area(13312, 1024).rearrange("p (b n) -> p b n", b=2)
        zbias = area(14336, 1024).rearrange("p (b n) -> p b n", b=2)
        wsT = area(15360, 1024).rearrange("p (g i) -> p g i", g=8)
        ln_g = area(16384, HALF)
        ln_b = area(19456, HALF)
        bsT = area(22528, 8)
        bn = area(22536, 144).rearrange("p (t c s) -> p t c s", t=TB, c=NCH_Z)
        ln_mv = area(22688, 8).rearrange("p (t s) -> p t s", t=TB)
        ln_sd = area(22700, 4)
        ln_rs = area(22704, 4)
        ln_ve = area(22708, 4)
        ugel = area(22784, 1024).rearrange("p (b n) -> p b n", b=2)
        bout = ugel.rearrange("p b n -> p (b n)")

        def yT(c, tb, part):
            v = vmix[:, c, tb, 256 * part:256 * part + 256].bitcast(BF16)
            return v.rearrange("p (f t) -> p f t", f=4)

        qkv = area(0, 6144).rearrange("p (t n) -> p t n", t=TB)
        qr = [area(6144, 2048).rearrange("p (t n) -> p t n", t=TB),
              area(14208, 2048).rearrange("p (t n) -> p t n", t=TB),
              area(6144, 1024).rearrange("p (t n) -> p t n", t=TB)]
        tmp = area(16256, 2048)
        tabs = area(8704, 256).rearrange("p (s t n) -> p s t n", s=2, t=TB)
        qkg = area(8960, 128).rearrange("p (s n) -> p s n", s=2)
        qT = area(9088, 4096).rearrange("p (j t) -> p j t", j=8)
        kT = area(13184, 1024).rearrange("p (j t) -> p j t", j=2)
        prob = [area(start, 2048).rearrange("p (h k) -> p h k", h=8) for start in (14208, 16256, 6144)]
        probT = area(18304, 2048).rearrange("p (b n) -> p b n", b=4)
        qbias = area(20352, 1536)
        bo = area(18304, 1024)
        hss = area(23168, 32)
        hrt = area(23200, 32)
        hrs = area(23232, 32)
        sink = area(23264, 16)
        smax, nmax, ssum, esink, srec = (area(23296 + 32 * r, 24).rearrange("p (u h) -> p u h", u=3)
                                         for r in range(5))

        scores = area(0, 8192).rearrange("p (t n) -> p t n", t=TB)
        hot1 = area(0, 2048, BF16).rearrange("p (s t n) -> p s t n", s=2, t=16)
        hot2 = [area(2048 + 2048 * r, 2048, BF16).rearrange("p (s t n) -> p s t n", s=2, t=16) for r in range(2)]
        pqT = area(8192, 8192).rearrange("p (j t) -> p j t", j=16)
        gstage = area(8192, 8192).rearrange("p (b e t) -> p b e t", b=2, t=BT)
        sstage = area(16384, 4096).rearrange("p (b e t) -> p b e t", b=2, e=4)
        sblk = area(8192, 2048).rearrange("p (j n) -> p j n", j=16)
        onehot = area(20480, 2048).rearrange("p (s j) -> p s j", j=TOPK)
        cand = area(22528, 512).rearrange("p (h n) -> p h n", h=2)
        posn = area(22528, 256, U32).rearrange("p (s n) -> p s n", s=2)
        posf = area(22784, 256).rearrange("p (s n) -> p s n", s=2)
        work = area(23040, 512)
        topif = area(23040, 256).rearrange("p (j k) -> p j k", j=16)
        selT = area(23552, 2048).rearrange("p (s t) -> p s t", s=4)
        sel = area(25600, 512).rearrange("p (s n) -> p s n", s=4)
        gate_b = area(26112, 64, BF16)
        topv = area(10240, 256).rearrange("p (j k) -> p j k", j=16)
        topi = area(10496, 256, U32).rearrange("p (j k) -> p j k", j=16)
        best = area(10752, P).rearrange("p (h k) -> p h k", h=PH)
        bestp = area(10880, P, U32).rearrange("p (h k) -> p h k", h=PH)
        tslice = sb("tslice", [P, 2, 4, BT])
        keysT = sb("keysT", [P, 2, P])
        gsum = sb("gsum", [P, PH])
        grec = sb("grec", [P, PH])
        s_in = [area(6144, 2048), area(0, 2048)]
        a_in = [area(20480, 2048), area(2048, 2048)]
        hsp = [[area(8192 + 2048 * b + 1024 * s, 1024, BF16).rearrange("p (e t) -> p e t", e=4)
                for s in range(2)] for b in range(2)]
        hf = [area(4096, 2048), area(22528, 2048)]

        raw_loaded = [sem("raw_loaded0"), sem("raw_loaded1")]
        hi_done, lo_done, chunk_used = sem("hi_done"), sem("lo_done"), sem("chunk_used")

        class Chain:
            def __init__(self, eng, name):
                self.eng, self.sem, self.n = eng, sem(name), 0

            def link(self, ins):
                ins.then_inc(self.sem, 1)
                self.n += 1
                self.eng.wait_ge(self.sem, self.n)

            def restart(self):
                self.eng.sem_clear(self.sem)
                self.n = 0

        def split_hi(act, c, h=0):
            b = c % 2
            act.wait_ge(raw_loaded[b], h * 16 + 16 * (c // 2 + 1))
            act.wait_ge(chunk_used, h * 2 + c + 1)
            nc.scalar.copy(wsp[b][0][:, :], raw[b][:, :]).then_inc(hi_done, 1)

        def split_lo(dve, c, h=0):
            b = c % 2
            dve.wait_ge(hi_done, h * 2 + c + 1)
            nc.vector.tensor_tensor(wsp[b][1][:, :], raw[b][:, :], wsp[b][0][:, :],
                                    ALU.subtract).then_inc(lo_done, 1)

        def wait_chunk(pe, c, h=0):
            pe.wait_ge(lo_done, h * 2 + c + 1 + CREDIT)

        def wait_output(eng, outs, c, base, s, h=0):
            if s < 3:
                eng.wait_ge(outs, h * 6 + 3 * (c - base) + s + 1)
            else:
                eng.wait_ge(chunk_used, h * 2 + c + 1 + CREDIT)

        def token_chunk(bank, c, tb, lhs, first=True, last=True):
            w = [v[:, :].rearrange("p (k n) -> p k n", k=8) for v in wsp[c % 2]]
            for k in range(8):
                for n, (a, b) in enumerate(((0, 0), (0, 1), (1, 0))):
                    mm = nc.tensor.matmul(bank[:, :], lhs(k, tb, a), w[b][:, k, :],
                                          start=first and k == 0 and n == 0,
                                          stop=last and k == 7 and n == 2)
            return mm

        def feature_chunk(bank, c, f):
            w = [v[:, :].rearrange("p (k n) -> p k n", k=8) for v in wsp[c % 2]]
            for k in range(8):
                for n, (a, b) in enumerate(((0, 0), (0, 1), (1, 0))):
                    mm = nc.tensor.matmul(bank[:, :], w[a][:, k, f * P:(f + 1) * P], hT[b][:, k, :],
                                          start=k == 0 and n == 0, stop=k == 7 and n == 2)
            return mm

        def h_lhs(k, tb, part):
            return hT[part][:, k, tb * P:(tb + 1) * P]

        def z_items(eng, item):
            for c in (0, 1):
                for tb in range(TB):
                    item(c, tb, 0, c == 0 and tb == 0)
            with eng.Fori(0, NCH_Z // 2 - 1) as i:
                for c in (2, 3):
                    for tb in range(TB):
                        item(c, tb, i, False)

        def before(c, tb):
            return (c, tb - 1) if tb else (c - 1, TB - 1)

        Z_LAST = (NCH_Z - 1, TB - 1)

        block = ctx.enter_context(nc.Block())

        @block.sync
        def _(sp):
            for tb in range(TB):
                sp.dma_start(xres[:, tb, :], x[tb * P:(tb + 1) * P, :]).then_inc(sem(f"x_loaded{tb}"), 16)
            used = min(CHUNKS, [0, G_PEER[0], G_QKV, G_PEER[1], CHUNKS][stages] + 1)
            s_stored = [sem("s_stored0"), sem("s_stored1")]
            a_stored = [sem("a_stored0"), sem("a_stored1")]

            def load_chunk(c, h=0):
                if c < used:
                    sp.wait_ge(lo_done, h * 2 + c + 1)
                    sp.dma_start(raw[c % 2][:, :], stream[h * 2 + c]).then_inc(raw_loaded[c % 2], 16)

            def load_run(first, end):
                end = min(end, used)
                pairs = (end - first) // 2
                if pairs > 1:
                    with sp.Fori(0, pairs) as i:
                        for b in range(2):
                            load_chunk(first + b, i)
                    first += 2 * pairs
                for c in range(first, end):
                    load_chunk(c)

            def store_acts(layer, c, h=0):
                sp.wait_ge(sem(f"gelu_done{layer}"), h * 8 + 4 + 4 * (c + 1))
                sp.dma_start(s_dram[h * 2 + c], sstage[:, c % 2, :, :].rearrange("p e t -> p (e t)")) \
                    .then_inc(s_stored[c % 2], 16)

            def store_gates(layer, g, h=0):
                sp.wait_ge(sem(f"gate_evac{layer}"), h * 16 + 3 + 8 * (g + 1))
                sp.dma_start(a_dram[:, bass.ds(h * 2 + g, 1), :],
                             gstage[:, g % 2:g % 2 + 1, :, :].rearrange("p o e t -> p o (e t)")) \
                    .then_inc(a_stored[g % 2], 16)

            def load_gated(c, h=0):
                sp.dma_start(s_in[c % 2], s_dram[h * 2 + c]).then_inc(sem(f"sa_loaded{c % 2}"), 16)
                sp.dma_start(a_in[c % 2].rearrange("p (g n) -> p g n", g=SEQ // BT),
                             a_dram[:, :, bass.ds((h * 2 + c) * (4 * BT), 4 * BT)]) \
                    .then_inc(sem(f"sa_loaded{c % 2}"), 16)

            def peer(layer):
                batches = SEQ // BT
                first = G_PEER[layer] + NCH_Q + AHEAD
                with sp.Fori(0, (NCH_E - batches) // 2) as i:
                    for b in range(2):
                        load_chunk(first + b, i)
                        store_acts(layer, b, i)
                with sp.Fori(0, batches // 2 - 1) as i:
                    for b in range(2):
                        load_chunk(first + NCH_E - batches + b, i)
                        store_acts(layer, NCH_E - batches + b, i)
                        store_gates(layer, b, i)
                load_chunk(first + NCH_E - 2)
                store_acts(layer, NCH_E - 2)
                store_gates(layer, batches - 2)
                load_chunk(first + NCH_E - 1)
                for b in range(2):
                    sp.wait_ge(s_stored[b], 16 * (NCH_E // 2 * (layer + 1) + 1 - b))
                    sp.wait_ge(a_stored[b], 16 * (batches // 2 * (layer + 1) + 1 - b))
                sp.dma_start(s_in[0], s_dram[0]).then_inc(sem("sa_loaded0"), 16)
                sp.dma_start(a_in[0].rearrange("p (g n) -> p g n", g=batches)[:, 0:batches - 1, :],
                             a_dram[:, 0:batches - 1, 0:4 * BT]).then_inc(sem("sa_loaded0"), 16)
                store_acts(layer, NCH_E - 1)
                store_gates(layer, batches - 1)
                first += NCH_E
                load_chunk(first)
                sp.wait_ge(s_stored[1], 16 * (NCH_E // 2 * (layer + 1) + 1))
                sp.wait_ge(a_stored[1], 16 * (batches // 2 * (layer + 1) + 1))
                sp.wait_ge(sem(f"gate_mm{layer}"), 8 + 4 * (SEQ // 16))
                load_gated(1)

                def slot(c, h=0):
                    if c:
                        load_chunk(first + c, h)
                    if c + 2 < NCH_E:
                        sp.wait_ge(sem(f"h_ready{layer}"), h * 2 + c + 1 + 2)
                        load_gated(c + 2, h)

                slot(0)
                slot(1)
                with sp.Fori(0, NCH_E // 2 - 3) as i:
                    for b in (2, 3):
                        slot(b, i)
                for c in range(NCH_E - 4, NCH_E):
                    slot(c)

            for b in range(2):
                sp.sem_inc(s_stored[b], 16)
                sp.sem_inc(a_stored[b], 16)
            load_run(0, G_PEER[0] + NCH_Q + AHEAD)
            if stages > 1:
                peer(0)
            if stages > 2:
                load_run(G_QKV + AHEAD, G_PEER[1] + NCH_Q + AHEAD)
            if stages > 3:
                peer(1)
            for tb in range(TB):
                sp.wait_ge(sem("x_ready"), 4 * stages + tb + 1)
                sp.dma_start(out[tb * P:(tb + 1) * P, :], xres[:, tb, :]).then_inc(sem("out_stored"), 16)
            sp.wait_ge(sem("out_stored"), 16 * TB)

        @block.gpsimd
        def _(pool):
            def norm_gain(j):
                if j:
                    pool.wait_ge(sem("hn_ready"), 4 * j)
                pool.dma_start(gain[:, :], gains[j].partition_broadcast(P)).then_inc(sem("gain_loaded"), 16)

            def constants():
                nc.gpsimd.memset(ident[:, :], 0.0).then_inc(sem("pool_chain"), 1)
                nc.gpsimd.memset(mask[:, :], 0.0).then_inc(sem("pool_chain"), 1)
                pool.wait_ge(sem("pool_chain"), 2)
                nc.gpsimd.affine_select(out=ident[:, :], in_=ident[:, :], pattern=[[-1, P]],
                                        compare_op=ALU.not_equal, fill=1.0, base=0,
                                        channel_multiplier=1).then_inc(sem("ident_ready"), 1)
                nc.gpsimd.iota(iota[:, :], [[1, TOPK]], base=0, channel_multiplier=0,
                               allow_small_or_imprecise_dtypes=True).then_inc(sem("iota_ready"), 1)
                nc.gpsimd.iota(iota_b[:, :], [[1, P]], base=0, channel_multiplier=0,
                               allow_small_or_imprecise_dtypes=True).then_inc(sem("iota_ready"), 1)
                nc.gpsimd.memset(zeros[:, :], 0.0).then_inc(sem("zeros_ready"), 1)
                pool.wait_ge(sem("zeros_ready"), 1)
                nc.gpsimd.memset(mask[0:64, 128:192], NEG).then_inc(sem("mask_ready"), 1)
                pool.wait_ge(sem("mask_ready"), 1)
                nc.gpsimd.memset(mask[64:128, 0:64], NEG).then_inc(sem("mask_ready"), 1)

            def gmlp():
                pool.dma_start(bout[:, :], b_out.partition_broadcast(P)).then_inc(sem("bout_loaded"), 16)
                pool.dma_start(wsT[:, :, :], w_s).then_inc(sem("ws_loaded"), 16)
                pool.dma_start(bsT[:, :], b_s).then_inc(sem("bs_loaded"), 16)
                pool.wait_ge(sem("ws_loaded"), 16)
                pool.wait_ge(sem("mask_ready"), 2)
                nc.gpsimd.memset(wsT[64:128, :, 0:64], 0.0).then_inc(sem("ws_masked"), 1)
                for c in range(2 * NCH_Z):
                    if c >= 2:
                        pool.wait_ge(sem("z_evac"), 4 + 4 * (c - 1))
                    pool.dma_start(zbias[:, c % 2, :], gmlp_bias[c].partition_broadcast(P)) \
                        .then_inc(sem(f"zbias_loaded{c % 2}"), 16)
                    if c == 1:
                        pool.dma_start(ln_g[:, :], ln_gb[0].partition_broadcast(P)).then_inc(sem("ln_loaded"), 16)
                        pool.dma_start(ln_b[:, :], ln_gb[1].partition_broadcast(P)).then_inc(sem("ln_loaded"), 16)

            def peer(layer):
                pool.dma_start(keysT[:, :, :], keys[layer]).then_inc(sem("keys_loaded"), 16)

            def attention():
                pool.dma_start(bo[:, :], b_o.partition_broadcast(P)).then_inc(sem("bo_loaded"), 16)
                pool.dma_start(qbias[:, :], qkv_bias.partition_broadcast(P)).then_inc(sem("attn_loaded"), 16)
                pool.dma_start(tabs[:, :, :, :], rope).then_inc(sem("attn_loaded"), 16)
                pool.dma_start(qkg[:, :, :].rearrange("p s n -> p (s n)"),
                               qk_gain.partition_broadcast(P)).then_inc(sem("attn_loaded"), 16)
                pool.dma_start(sink[:, :], sinks.partition_broadcast(P)).then_inc(sem("attn_loaded"), 16)

            norm_gain(0)
            constants()
            gmlp()
            norm_gain(1)
            if stages > 1:
                peer(0)
            if stages > 2:
                norm_gain(2)
                pool.wait_ge(sem("x_ready"), 12)
                attention()
                norm_gain(3)
            if stages > 3:
                peer(1)

        @block.scalar
        def _(act):
            def norm(j):
                def root(tb):
                    act.wait_ge(sem("x_ready"), 4 * j + tb + 1)
                    nc.scalar.activation(squares[:, :], xres[:, tb, :], ACT.Square,
                                         accum_out=sumsq[:, tb:tb + 1]).then_inc(sem("squared"), 1)
                    act.wait_ge(sem("squared"), 4 * j + tb + 1)
                    nc.scalar.activation(rootms[:, tb:tb + 1], sumsq[:, tb:tb + 1], ACT.Sqrt, scale=1.0 / D,
                                         bias=epsilon[:, 0:1]).then_inc(sem("root_ready"), 1)

                def high(tb):
                    for half in range(2):
                        act.wait_ge(sem("hT_tr"), 8 * j + 2 * tb + half + 1)
                        nc.scalar.copy(hT[0][:, 4 * half:4 * half + 4, tb * P:(tb + 1) * P],
                                       pb[2 * (tb % 2) + half][:, :].rearrange("p (k t) -> p k t", k=4)) \
                            .then_inc(sem("hT_hi"), 1)

                for tb in range(TB):
                    root(tb)
                    if tb == TB - 1:
                        high(0)
                for tb in range(1, TB):
                    high(tb)
                    if j == 0 and tb == 1:
                        split_hi(act, 0)

            def v_item(c, tb, h, first):
                if tb == 0:
                    split_hi(act, G_V + c + 1, h)
                act.wait_ge(sem("z_evac"), h * 8 + 4 * (G_V + c) + tb + 1 + 4)
                nc.scalar.activation(vmix[:, bass.ds(h * 2 + c, 1), tb, :], zt[:, tb % 2:tb % 2 + 1, :],
                                     ACT.Gelu_apprx_tanh).then_inc(sem("z_gelu"), 1)

            def u_item(c, tb, h, first):
                if tb == 0:
                    split_hi(act, G_U + c + 1, h)
                act.wait_ge(sem("z_evac"), h * 8 + 4 * (G_U + c) + tb + 1 + 4)
                act.wait_ge(sem("y_done"), h * 8 + 4 * c + tb + 1)
                nc.scalar.activation(ugel[:, tb % 2, :], zt[:, tb % 2, :],
                                     ACT.Gelu_apprx_tanh).then_inc(sem("z_gelu"), 1)
                if not first:
                    y_hi(*before(c, tb), h)

            def y_hi(c, tb, h):
                act.wait_ge(sem("y_tr"), h * 8 + 4 * c + tb + 1 + 2)
                nc.scalar.copy(vmix[:, bass.ds(h * 2 + c, 1), tb, 0:256].bitcast(BF16),
                               pb[4 + tb % 2][:, :].rearrange("p (o n) -> p o n", o=1)).then_inc(sem("y_hi"), 1)

            def gmlp():
                act.sem_inc(sem("y_done"), 2)
                z_items(act, v_item)
                act.wait_ge(sem("lnv_ready"), 1)
                nc.scalar.activation(ln_sd[:, :], ln_ve[:, :], ACT.Sqrt).then_inc(sem("lnsd_ready"), 1)
                act.wait_ge(sem("bs_loaded"), 16)
                for c in range(NCH_Z):
                    for tb in range(TB):
                        idx = c * TB + tb
                        act.wait_ge(sem("mix_mm"), idx + 1)
                        at = 0
                        while at < 512:
                            g = (c * 512 + at) // GW
                            w = min(512, (g + 1) * GW - c * 512) - at
                            last = nc.scalar.activation(vmix[:, c, tb, at:at + w], pb[4 + idx % 4][:, at:at + w],
                                                        ACT.Identity, bias=bsT[:, g:g + 1])
                            at += w
                        last.then_inc(sem("mix_evac"), 1)
                z_items(act, u_item)
                y_hi(*Z_LAST, 0)
                for c in range(G_OUT, G_OUT + NCH_OUT):
                    split_hi(act, c + 1)

            def query(layer):
                base, n = G_PEER[layer], f"{layer}"
                act.sem_inc(sem("q_evac" + n), 4)
                with act.Fori(0, NCH_Q // 2) as i:
                    for k in range(2):
                        split_hi(act, base + k + 1, i)
                        for f in range(4):
                            wait_output(act, sem("q_mm" + n), base + k, base, f, i)
                            nc.scalar.copy(pqT[:, bass.ds(i * 8 + 4 * k + f, 1), :],
                                           pb[f][:, :].rearrange("p (o n) -> p o n", o=1)) \
                                .then_inc(sem("q_evac" + n), 1)
                for idx in range(4 * TB):
                    act.wait_ge(sem("s_mm" + n), idx + 1)
                    nc.scalar.copy(scores[:, idx // 4, 512 * (idx % 4):512 * (idx % 4) + 512],
                                   pb[4 + idx % 4][:, :]).then_inc(sem("s_evac" + n), 1)

            def gelu_tile(layer, k, e, h, first):
                n, b = f"{layer}", k % 2
                base = G_PEER[layer] + NCH_Q
                if e == 0:
                    split_hi(act, base + first + k + 1, h)
                    act.wait_ge(sem(f"s_stored{b}"), h * 16 + 16 * ((first + k) // 2 + 1 + layer * NCH_E // 2))
                wait_output(act, sem("u_mm" + n), base + first + k, base, e, h)
                nc.scalar.activation(sstage[:, b, e, :], pb[e][:, :],
                                     ACT.Gelu_apprx_tanh).then_inc(sem("gelu_done" + n), 1)

            def experts_first(layer):
                n = f"{layer}"
                act.sem_inc(sem("gelu_done" + n), 4)
                with act.Fori(0, TB) as i:
                    act.wait_ge(sem("best_ready" + n), i + 1)
                    nc.scalar.copy(sblk[:, :, :].rearrange("p j n -> p (j n)").rearrange("p (o n) -> p o n", o=1),
                                   scores[:, bass.ds(i, 1), :]).then_inc(sem("sblk_ready" + n), 1)
                    for k in range(4):
                        for e in range(4):
                            if k == 3 and e == 0:
                                act.wait_ge(sem("best_ready" + n), i + 2)
                                nc.scalar.activation(best[:, :, :], best[:, :, :],
                                                     ACT.Exp).then_inc(sem("best_exp" + n), 1)
                            gelu_tile(layer, k, e, i * 2, 0)
                    act.wait_ge(sem("sel_tr" + n), i + 2)
                    nc.scalar.copy(selT[:, :, bass.ds(i * P, P)],
                                   pb[4][:, :].rearrange("p (s t) -> p s t", s=4)) \
                        .then_inc(sem("selT_ready" + n), 1)
                act.sem_inc(sem("gate_evac" + n), 3)
                with act.Fori(0, TB) as i:
                    for k in range(4):
                        b = k % 2
                        for e in range(4):
                            gelu_tile(layer, k, e, i * 2, NCH_E // 2)
                            for q in QUADS[e]:
                                if q == 0:
                                    act.wait_ge(sem(f"a_stored{b}"),
                                                i * 32 + 16 * (k // 2 + 1 + layer * SEQ // BT // 2))
                                act.wait_ge(sem("gate_mm" + n), i * 32 + 8 * k + q + 1 + 8)
                                nc.scalar.copy(gstage[:, b, :, 4 * q:4 * q + 4].rearrange("p e t -> p t e"),
                                               pb[5 + q % 3][:, :].rearrange("p (t e) -> p t e", t=4)) \
                                    .then_inc(sem("gate_evac" + n), 1)

            def h_hi(layer, k, h):
                n = f"{layer}"
                act.wait_ge(sem("hf_ready" + n), h * 2 + k + 1)
                nc.scalar.copy(hsp[k % 2][0][:, :, :].rearrange("p e t -> p (e t)"), hf[k % 2]) \
                    .then_inc(sem("h_hi" + n), 1)

            def experts_second(layer):
                base = G_PEER[layer] + NCH_Q + NCH_E
                h_hi(layer, 0, 0)
                with act.Fori(0, NCH_E // 2 - 1) as i:
                    for k in range(2):
                        split_hi(act, base + k + 1, i)
                        h_hi(layer, k + 1, i)
                split_hi(act, base + NCH_E - 1)
                h_hi(layer, NCH_E - 1, 0)
                if base + NCH_E < CHUNKS:
                    split_hi(act, base + NCH_E)

            def attention():
                def heads_T(part):
                    n = 4 if part < 2 else 2
                    dst, at = (qT, 4 * part) if part < 2 else (kT, 0)
                    for tb in range(TB):
                        act.wait_ge(sem("qk_tr"), TB * part + tb + 1)
                        nc.scalar.copy(dst[:, at:at + n, tb * P:(tb + 1) * P],
                                       pb[4 + tb][:, 0:n * P].rearrange("p (k t) -> p k t", k=n)) \
                            .then_inc(sem("qk_T"), 1)

                for c in range(NCH_QKV):
                    split_hi(act, G_QKV + c + 1)
                    if c:
                        heads_T(c - 1)
                    n = TB * (8 if c < 2 else 4)
                    act.wait_ge(sem("hss_ready"), c + 1)
                    nc.scalar.activation(hrt[:, 0:n], hss[:, 0:n], ACT.Sqrt, scale=1.0 / HD,
                                         bias=epsilon[:, 0:1]).then_inc(sem("hroot_ready"), 1)
                heads_T(2)

                def exps(u):
                    lo = 64 if u >= 2 else P
                    act.wait_ge(sem("max_ready"), u + 1)
                    nc.scalar.activation(esink[:, u % 3, :], esink[:, u % 3, :], ACT.Exp)
                    for h in range(8):
                        last = nc.scalar.activation(prob[u % 3][:, h, lo:256], prob[u % 3][:, h, lo:256], ACT.Exp,
                                                    bias=nmax[:, u % 3, h:h + 1], accum_out=ssum[:, u % 3, h:h + 1])
                    last.then_inc(sem("prob_exp"), 1)

                def probs_T(u):
                    for r in range(4):
                        idx = 4 * u + r
                        act.wait_ge(sem("prob_tr"), idx + 1)
                        if idx >= 4:
                            act.wait_ge(sem("pv_mm"), idx - 3)
                        cols = slice(0, 512) if u >= 2 else slice(0, 256)
                        nc.scalar.copy(probT[:, r, cols], pb[4 + r % 2][:, cols]).then_inc(sem("probT_ready"), 1)
                    tb, half = u // 2, u % 2
                    act.wait_ge(sem("pv_mm"), 4 * u + 4)
                    nc.scalar.copy(hT[0][:, 4 * half:4 * half + 4, tb * P:(tb + 1) * P],
                                   pb[6 + half][:, :].rearrange("p (k t) -> p k t", k=4)).then_inc(sem("oT_hi"), 1)

                for u in range(UNITS + 1):
                    if u < UNITS:
                        exps(u)
                    if u:
                        probs_T(u - 1)
                for c in range(NCH_O):
                    split_hi(act, G_WO + c + 1)

            act.wait_ge(sem("epsilon_ready"), 1)
            norm(0)
            gmlp()
            norm(1)
            if stages > 1:
                query(0)
                experts_first(0)
                experts_second(0)
            if stages > 2:
                norm(2)
                attention()
                norm(3)
            if stages > 3:
                query(1)
                experts_first(1)
                experts_second(1)

        @block.vector
        def _(dve):
            chain = Chain(dve, "dve_chain")
            link = chain.link

            def norm(j, produce):
                def scaled(tb):
                    dve.wait_ge(sem("root_ready"), 4 * j + tb + 1)
                    link(nc.vector.reciprocal(rstd[:, tb:tb + 1], rootms[:, tb:tb + 1]))
                    if tb >= 2:
                        dve.wait_ge(sem("hT_tr"), 8 * j + 2 * (tb - 1))
                    nc.vector.scalar_tensor_tensor(hn[:, tb % 2, :], xres[:, tb, :], rstd[:, tb:tb + 1],
                                                   gain[:, :], ALU.mult, ALU.mult).then_inc(sem("hn_ready"), 1)

                def low(tb):
                    for half in range(2):
                        dve.wait_ge(sem("hT_hi"), 8 * j + 2 * tb + half + 1)
                        at = (slice(None), slice(4 * half, 4 * half + 4), slice(tb * P, (tb + 1) * P))
                        nc.vector.tensor_tensor(hT[1][at],
                                                pb[2 * (tb % 2) + half][:, :].rearrange("p (k t) -> p k t", k=4),
                                                hT[0][at], ALU.subtract).then_inc(sem("hT_lo"), 1)

                produce(0)
                produce(1)
                dve.wait_ge(sem("gain_loaded"), 16 * (j + 1))
                scaled(0)
                produce(2)
                scaled(1)
                produce(3)
                low(0)
                scaled(2)
                low(1)
                scaled(3)
                if j == 0:
                    split_lo(dve, 0)
                low(2)
                low(3)

            def x_loaded(tb):
                dve.wait_ge(sem(f"x_loaded{tb}"), 16)
                dve.sem_inc(sem("x_ready"), 1)

            def add_rows(row, waited):
                dve.wait_ge(sem(waited), 16)
                for tb in range(TB):
                    nc.vector.tensor_tensor(xres[:, tb, :], xres[:, tb, :], row[:, :], ALU.add) \
                        .then_inc(sem("bias_added"), 1)

            def bias_z(c, tb, h):
                if tb == 0:
                    dve.wait_ge(sem(f"zbias_loaded{c % 2}"), h * 16 + 16 * (c // 2 + 1))
                wait_output(dve, sem("z_mm"), c, 0, tb, h)
                dve.wait_ge(sem("z_gelu"), h * 8 + 4 * c + tb + 1)
                nc.vector.tensor_tensor(zt[:, tb % 2, :], pb[tb][:, :], zbias[:, c % 2, :],
                                        ALU.add).then_inc(sem("z_evac"), 1)

            def y_block(c, tb, h):
                dve.wait_ge(sem("z_gelu"), h * 8 + 4 * (G_U + c) + tb + 1 + 2)
                dve.wait_ge(sem("y_tr"), h * 8 + 4 * c + tb + 1)
                nc.vector.tensor_tensor(ytok[:, tb % 2:tb % 2 + 1, :], ugel[:, tb % 2:tb % 2 + 1, :],
                                        vmix[:, bass.ds(h * 2 + c, 1), tb, :], ALU.mult) \
                    .then_inc(sem("y_done"), 1)

            def y_lo(c, tb, h):
                dve.wait_ge(sem("y_hi"), h * 8 + 4 * c + tb + 1)
                at = bass.ds(h * 2 + c, 1)
                nc.vector.tensor_tensor(vmix[:, at, tb, 256:512].bitcast(BF16),
                                        pb[4 + tb % 2][:, :].rearrange("p (o n) -> p o n", o=1),
                                        vmix[:, at, tb, 0:256].bitcast(BF16), ALU.subtract) \
                    .then_inc(sem("y_lo"), 1)

            def v_stats(c, tb, h):
                dve.wait_ge(sem("z_gelu"), h * 8 + 4 * c + tb + 1 + 2)
                return nc.vector.bn_stats(bn[:, tb, bass.ds(h * 2 + c, 1), :].rearrange("p c s -> p (c s)"),
                                          vmix[:, bass.ds(h * 2 + c, 1), tb, :].rearrange("p c n -> p (c n)"))

            def v_item(c, tb, h, first):
                bias_z(G_V + c, tb, h)
                if tb == 0:
                    split_lo(dve, G_V + c + 1, h)
                if not first:
                    v_stats(*before(c, tb), h)

            def u_item(c, tb, h, first):
                bias_z(G_U + c, tb, h)
                if tb == 0:
                    split_lo(dve, G_U + c + 1, h)
                if not first:
                    y_lo(*before(c, tb), h)
                y_block(c, tb, h)

            def gmlp():
                dve.sem_inc(sem("z_evac"), 4)
                dve.sem_inc(sem("z_gelu"), 2)
                dve.sem_inc(sem("y_lo"), 2)
                z_items(dve, v_item)
                link(v_stats(*Z_LAST, 0))
                for tb in range(TB):
                    last = nc.vector.bn_aggr(ln_mv[:, tb, :], bn[:, tb, :, :].rearrange("p c s -> p (c s)"))
                link(last)
                nc.vector.tensor_scalar(ln_ve[:, :], ln_mv[:, :, 1], EPS, None, ALU.add).then_inc(sem("lnv_ready"), 1)
                dve.wait_ge(sem("lnsd_ready"), 1)
                link(nc.vector.reciprocal(ln_rs[:, :], ln_sd[:, :]))
                dve.wait_ge(sem("ln_loaded"), 32)
                for c in range(NCH_Z):
                    cols = slice(512 * c, 512 * c + 512)
                    for tb in range(TB):
                        v = vmix[:, c, tb, :]
                        last = nc.vector.scalar_tensor_tensor(v, v, ln_mv[:, tb, 0:1], ln_g[:, cols],
                                                              ALU.subtract, ALU.mult)
                    link(last)
                    for tb in range(TB):
                        v = vmix[:, c, tb, :]
                        nc.vector.scalar_tensor_tensor(v, v, ln_rs[:, tb:tb + 1], ln_b[:, cols],
                                                       ALU.mult, ALU.add).then_inc(sem("vn_ready"), 1)
                dve.wait_ge(sem("mix_evac"), TB * NCH_Z)
                z_items(dve, u_item)
                y_lo(*Z_LAST, 0)
                for c in range(G_OUT, G_OUT + NCH_OUT):
                    split_lo(dve, c + 1)
                    if c == G_OUT + 3:
                        first_half("zo_mm", 0, G_OUT + 2)

            def first_half(mm, layer, chunk):
                dve.wait_ge(sem("bias_added"), 4 * (layer + 1))
                for tb in range(TB):
                    add_half(mm, chunk, 0, tb)

            def add_half(mm, chunk, half, tb):
                if tb < 3:
                    dve.wait_ge(sem(mm), 3 * half + tb + 1)
                else:
                    dve.wait_ge(chunk_used, chunk + 1 + CREDIT)
                cols = slice(512 * half, 512 * half + 512)
                return nc.vector.tensor_tensor(xres[:, tb, cols], xres[:, tb, cols], pb[4 * half + tb][:, :], ALU.add)

            def mixed(mm, chunk):
                return lambda tb: add_half(mm, chunk, 1, tb).then_inc(sem("x_ready"), 1)

            def retrieved(layer):
                def produce(tb):
                    if tb == 0:
                        dve.wait_ge(sem(f"v_mm{layer}"), 1)
                    for half in range(2):
                        cols = slice(512 * half, 512 * half + 512)
                        last = nc.vector.tensor_tensor(xres[:, tb, cols], xres[:, tb, cols],
                                                       pb[2 * tb + half][:, :], ALU.add)
                    last.then_inc(sem("x_ready"), 1)
                return produce

            def query(layer):
                base = G_PEER[layer]
                with dve.Fori(0, NCH_Q // 2) as i:
                    for k in range(2):
                        split_lo(dve, base + k + 1, i)

            def top16(values, index, src, spare):
                rows = range(len(src))
                for r in rows:
                    last = nc.vector.max(values[r][:, 0:8], src[r])
                link(last)
                for r in rows:
                    nc.vector.max_index(index[r][:, 0:8], values[r][:, 0:8], src[r])
                    last = nc.vector.match_replace(spare[r], values[r][:, 0:8], src[r], LOWEST)
                link(last)
                for r in rows:
                    last = nc.vector.max(values[r][:, 8:16], spare[r])
                link(last)
                for r in rows:
                    last = nc.vector.max_index(index[r][:, 8:16], values[r][:, 8:16], spare[r])
                link(last)

            def retrieve(k):
                js = range(4 * k, 4 * k + 4)
                top16([topv[:, j, :] for j in js], [topi[:, j, :] for j in js], [sblk[:, j, :] for j in js],
                      [work[:, P * r:P * r + P] for r in range(4)])
                for r in range(2):
                    a, b = topv[:, 4 * k + 2 * r, :], topv[:, 4 * k + 2 * r + 1, :]
                    last = nc.vector.tensor_tensor(cand[:, r, :].rearrange("p (a b) -> p a b", a=TOPK),
                                                   a.unsqueeze(2).broadcast_to([P, TOPK, TOPK]),
                                                   b.unsqueeze(1).broadcast_to([P, TOPK, TOPK]), ALU.add)
                link(last)
                top16([best[:, 2 * k + r, :] for r in range(2)], [bestp[:, 2 * k + r, :] for r in range(2)],
                      [cand[:, r, :] for r in range(2)], [work[:, 256 * r:256 * r + 256] for r in range(2)])

            def select(layer, i):
                n = f"{layer}"
                link(nc.vector.tensor_tensor(sel[:, 2, :].rearrange("p (h k) -> p h k", h=PH), best[:, :, :],
                                             best[:, :, 0:1].broadcast_to([P, PH, TOPK]), ALU.subtract))
                nc.vector.tensor_copy(best[:, :, :], sel[:, 2, :].rearrange("p (h k) -> p h k", h=PH)) \
                    .then_inc(sem("best_ready" + n), 1)
                flat = bestp[:, :, :].rearrange("p h k -> p (h k)")
                nc.vector.tensor_scalar(posn[:, 0, :], flat, 4, None, ALU.logical_shift_right)
                link(nc.vector.tensor_scalar(posn[:, 1, :], flat, 15, None, ALU.bitwise_and))
                nc.vector.tensor_copy(topif[:, :, :], topi[:, :, :])
                link(nc.vector.tensor_copy(posf[:, :, :], posn[:, :, :]))
                for s in range(2):
                    link(nc.vector.tensor_tensor(onehot[:, :, :], posf[:, s, :].unsqueeze(2).broadcast_to([P, P, TOPK]),
                                                 iota[:, 0:TOPK].unsqueeze(1).broadcast_to([P, P, TOPK]),
                                                 ALU.is_equal))
                    idx = topif[:, :, :].rearrange("p (h s) j -> p s h j", s=2)[:, s, :, :]
                    hot = onehot[:, :, :].rearrange("p (h k) j -> p h k j", h=PH)
                    link(nc.vector.tensor_tensor(hot, hot, idx.unsqueeze(2).broadcast_to([P, PH, TOPK, TOPK]),
                                                 ALU.mult))
                    link(nc.vector.tensor_reduce(sel[:, s, :], onehot[:, :, :], AX_X, ALU.add))
                dve.wait_ge(sem("best_exp" + n), i + 1)
                link(nc.vector.tensor_reduce(gsum[:, :], best[:, :, :], AX_X, ALU.add))
                link(nc.vector.reciprocal(grec[:, :], gsum[:, :]))
                gates = sel[:, 3, :]
                link(nc.vector.tensor_tensor(gates.rearrange("p (h k) -> p h k", h=PH), best[:, :, :],
                                             grec[:, :].unsqueeze(2).broadcast_to([P, PH, TOPK]), ALU.mult))
                link(nc.vector.tensor_copy(gate_b[:, :], gates))
                link(nc.vector.tensor_copy(sel[:, 2, :], gate_b[:, :]))
                nc.vector.tensor_tensor(sel[:, 3, :], gates, sel[:, 2, :],
                                        ALU.subtract).then_inc(sem("sel_ready" + n), 1)

            def experts_first(layer):
                n, base = f"{layer}", G_PEER[layer] + NCH_Q
                dve.wait_ge(sem("iota_ready"), 2)
                dve.sem_inc(sem("sel_ready" + n), 1)
                dve.sem_inc(sem("best_ready" + n), 1)
                with dve.Fori(0, TB) as i:
                    chain.restart()
                    dve.wait_ge(sem("sel_tr" + n), i + 1)
                    dve.wait_ge(sem("sblk_ready" + n), i + 1)
                    for k in range(3):
                        split_lo(dve, base + k + 1, i * 2)
                        retrieve(k)
                        if k == 0:
                            retrieve(3)
                    select(layer, i)
                    split_lo(dve, base + 4, i * 2)
                dve.wait_ge(sem("selT_ready" + n), TB)

                def one_hots(i, k, s):
                    dve.wait_ge(sem("gate_mm" + n), i * 32 + 8 * k + 4 * s + 4)
                    places = iota_b[:, :].unsqueeze(1).broadcast_to([P, 16, P])

                    def row(r):
                        return tslice[:, k % 2, r, 16 * s:16 * s + 16].unsqueeze(2).broadcast_to([P, 16, P])

                    link(nc.vector.tensor_tensor(hot2[0][:, s, :, :], places, row(1), ALU.is_equal))
                    nc.vector.tensor_tensor(hot1[:, s, :, :], places, row(0), ALU.is_equal)
                    link(nc.vector.tensor_tensor(hot2[1][:, s, :, :], hot2[0][:, s, :, :], row(3), ALU.mult))
                    nc.vector.tensor_tensor(hot2[0][:, s, :, :], hot2[0][:, s, :, :], row(2), ALU.mult) \
                        .then_inc(sem("hot_ready" + n), 1)

                with dve.Fori(0, TB) as i:
                    chain.restart()
                    for k in range(4):
                        link(nc.vector.tensor_copy(tslice[:, k % 2, :, :], selT[:, :, bass.ds(i * P + BT * k, BT)]))
                        one_hots(i, k, 0)
                        split_lo(dve, base + NCH_E // 2 + k + 1, i * 2)
                        one_hots(i, k, 1)

            def h_parts(layer, k, h, first=False):
                n, b = f"{layer}", k % 2
                dve.wait_ge(sem(f"sa_loaded{b}"), h * 32 + 32 * (k // 2 + 1 + layer * NCH_E // 2))
                acts = s_in[b].rearrange("p (e g t) -> p e g t", e=4, t=BT)
                gates = a_in[b].rearrange("p (g e t) -> p e g t", e=4, t=BT)
                gated = hf[b].rearrange("p (e g t) -> p e g t", e=4, t=BT)
                if first:
                    g = SEQ // BT - 1
                    dve.wait_ge(sem("gate_mm" + n), 8 + 4 * (SEQ // 16))
                    nc.vector.tensor_tensor(gated[:, :, 0:g, :], acts[:, :, 0:g, :], gates[:, :, 0:g, :], ALU.mult)
                    dve.wait_ge(sem("gate_evac" + n), 3 + SEQ // 4)
                    nc.vector.tensor_tensor(gated[:, :, g, :], acts[:, :, g, :], gstage[:, 1, 0:4, :],
                                            ALU.mult).then_inc(sem("hf_ready" + n), 1)
                else:
                    nc.vector.tensor_tensor(gated, acts, gates, ALU.mult).then_inc(sem("hf_ready" + n), 1)
                dve.wait_ge(sem("h_hi" + n), h * 2 + k + 1)
                nc.vector.tensor_tensor(hsp[b][1][:, :, :].rearrange("p e t -> p (e t)"), hf[b],
                                        hsp[b][0][:, :, :].rearrange("p e t -> p (e t)"), ALU.subtract) \
                    .then_inc(sem("h_ready" + n), 1)

            def experts_second(layer):
                n, base = f"{layer}", G_PEER[layer] + NCH_Q + NCH_E
                dve.sem_inc(sem("h_ready" + n), 2)
                h_parts(layer, 0, 0, True)
                with dve.Fori(0, NCH_E // 2 - 1) as i:
                    for k in range(2):
                        split_lo(dve, base + k + 1, i)
                        h_parts(layer, k + 1, i)
                split_lo(dve, base + NCH_E - 1)
                h_parts(layer, NCH_E - 1, 0)
                if base + NCH_E < CHUNKS:
                    split_lo(dve, base + NCH_E)

            def rope_part(part):
                heads, at = (8, 512 * part) if part < 2 else (4, QW)
                half = HD // 2
                dve.wait_ge(sem("hroot_ready"), part + 1)
                link(nc.vector.reciprocal(hrs[:, 0:TB * heads], hrt[:, 0:TB * heads]))
                x_ = qkv[:, :, at:at + HD * heads].rearrange("p t (h d) -> p t h d", d=HD)
                rs = hrs[:, 0:TB * heads].rearrange("p (t h) -> p t h", t=TB)
                link(nc.vector.tensor_tensor(x_, x_, rs.unsqueeze(3).broadcast_to([P, TB, heads, HD]), ALU.mult))
                g = qkg[:, part // 2, :].unsqueeze(1).unsqueeze(1).broadcast_to([P, TB, heads, HD])
                link(nc.vector.tensor_tensor(x_, x_, g, ALU.mult))
                cos, sin = (tabs[:, r, :, :].unsqueeze(2).broadcast_to([P, TB, heads, half]) for r in range(2))
                x1, x2 = x_[:, :, :, 0:half], x_[:, :, :, half:]
                o = qr[part][:, :, 0:HD * heads].rearrange("p t (h d) -> p t h d", d=HD)
                t1, t2 = (tmp[:, 1024 * r:1024 * r + TB * heads * half]
                          .rearrange("p (t h d) -> p t h d", t=TB, d=half) for r in range(2))
                if part == 2:
                    dve.wait_ge(sem("qk_tr"), TB)
                nc.vector.tensor_tensor(t1, x1, cos, ALU.mult)
                link(nc.vector.tensor_tensor(t2, x2, sin, ALU.mult))
                link(nc.vector.tensor_tensor(o[:, :, :, 0:half], t1, t2, ALU.subtract))
                nc.vector.tensor_tensor(t1, x2, cos, ALU.mult)
                link(nc.vector.tensor_tensor(t2, x1, sin, ALU.mult))
                nc.vector.tensor_tensor(o[:, :, :, half:], t1, t2, ALU.add).then_inc(sem("qr_ready"), 1)
                dve.wait_ge(sem("qr_ready"), part + 1)

            def masked(u):
                tb, half = u // 2, u % 2
                lo = 64 if tb else P
                width = 256 - lo
                pr = prob[u % 3]
                byp = pr[:, :, :].rearrange("p (m q r) k -> p m r q k", q=2, r=2)
                if u >= 3:
                    dve.wait_ge(sem("prob_tr"), 4 * (u - 2))
                for r in range(4):
                    dve.wait_ge(sem("qk_mm"), 4 * u + r // 2 * 2 + 2)
                    src = pb[r][:, :].rearrange("p (h k) -> p h k", h=2)[:, :, 0:width]
                    last = nc.vector.scalar_tensor_tensor(
                        byp[:, r // 2, r % 2, :, lo:256], src, HD ** -0.5,
                        mask[:, 192 - width:192].unsqueeze(1).broadcast_to([P, 2, width]), ALU.mult, ALU.add)
                last.then_inc(sem("scores_taken"), 1)
                dve.wait_ge(sem("scores_taken"), u + 1)
                link(nc.vector.tensor_reduce(smax[:, u % 3, :], pr[:, :, lo:256], AX_X, ALU.max))
                snk = sink[:, 8 * half:8 * half + 8]
                link(nc.vector.tensor_tensor(smax[:, u % 3, :], smax[:, u % 3, :], snk, ALU.max))
                nc.vector.tensor_tensor(esink[:, u % 3, :], snk, smax[:, u % 3, :], ALU.subtract)
                nc.vector.tensor_scalar(nmax[:, u % 3, :], smax[:, u % 3, :], -1.0, None,
                                        ALU.mult).then_inc(sem("max_ready"), 1)

            def normalised(u):
                lo = 64 if u >= 2 else P
                pr = prob[u % 3][:, :, lo:256]
                dve.wait_ge(sem("prob_exp"), u + 1)
                link(nc.vector.tensor_tensor(ssum[:, u % 3, :], ssum[:, u % 3, :], esink[:, u % 3, :], ALU.add))
                link(nc.vector.reciprocal(srec[:, u % 3, :], ssum[:, u % 3, :]))
                nc.vector.tensor_tensor(pr, pr, srec[:, u % 3, :].unsqueeze(2).broadcast_to([P, 8, 256 - lo]),
                                        ALU.mult).then_inc(sem("prob_ready"), 1)

            def out_low(u):
                tb, half = u // 2, u % 2
                dve.wait_ge(sem("oT_hi"), u + 1)
                at = (slice(None), slice(4 * half, 4 * half + 4), slice(tb * P, (tb + 1) * P))
                nc.vector.tensor_tensor(hT[1][at], pb[6 + half][:, :].rearrange("p (k t) -> p k t", k=4),
                                        hT[0][at], ALU.subtract).then_inc(sem("oT_lo"), 1)

            def attention():
                dve.wait_ge(sem("attn_loaded"), 64)
                dve.wait_ge(sem("mask_ready"), 2)
                for c in range(NCH_QKV):
                    heads = 8 if c < 2 else 4
                    for tb in range(TB):
                        wait_output(dve, sem("qkv_mm"), G_QKV + c, G_QKV, tb)
                        nc.vector.tensor_tensor(qkv[:, tb, 512 * c:512 * c + 512], pb[tb][:, :],
                                                qbias[:, 512 * c:512 * c + 512], ALU.add) \
                            .then_inc(sem("qkv_evac"), 1)
                        if tb == 0:
                            split_lo(dve, G_QKV + c + 1)
                        dve.wait_ge(sem("qkv_evac"), TB * c + tb + 1)
                        part = qkv[:, tb, 512 * c:512 * c + HD * heads]
                        sq = tmp[:, 512 * tb:512 * tb + HD * heads]
                        link(nc.vector.tensor_tensor(sq, part, part, ALU.mult))
                        last = nc.vector.tensor_reduce(hss[:, heads * tb:heads * tb + heads],
                                                       sq.rearrange("p (h d) -> p h d", d=HD), AX_X, ALU.add)
                    last.then_inc(sem("hss_ready"), 1)
                    rope_part(c)
                dve.wait_ge(sem("qk_tr"), 3 * TB)
                for r in range(3):
                    last = nc.vector.memset(prob[r][:, :, 0:64], 0.0)
                link(last)
                for u in range(UNITS + 2):
                    if u < UNITS:
                        masked(u)
                    if 1 <= u <= UNITS:
                        normalised(u - 1)
                    if u >= 2:
                        out_low(u - 2)
                for c in range(NCH_O):
                    split_lo(dve, G_WO + c + 1)
                first_half("ao_mm", 1, G_WO)

            dve.sem_inc(lo_done, CREDIT)
            nc.vector.memset(epsilon[:, :], EPS).then_inc(sem("epsilon_ready"), 1)
            norm(0, x_loaded)
            add_rows(bout, "bout_loaded")
            gmlp()
            norm(1, mixed("zo_mm", G_OUT + NCH_OUT - 1))
            if stages > 1:
                query(0)
                experts_first(0)
                experts_second(0)
            if stages > 2:
                norm(2, retrieved(0))
                add_rows(bo, "bo_loaded")
                attention()
                norm(3, mixed("ao_mm", G_WO + 1))
            if stages > 3:
                query(1)
                experts_first(1)
                experts_second(1)
            if stages % 2 == 0:
                for tb in range(TB):
                    retrieved(stages // 2 - 1)(tb)

        @block.tensor
        def _(pe):
            def norm_tr(j, tb):
                pe.wait_ge(sem("hn_ready"), 4 * j + tb + 1)
                for half in range(2):
                    if tb >= 2:
                        pe.wait_ge(sem("hT_lo"), 8 * j + 2 * (tb - 2) + half + 1)
                    for k in range(4):
                        f = 4 * half + k
                        last = nc.tensor.transpose(pb[2 * (tb % 2) + half][:, k * P:(k + 1) * P],
                                                   hn[:, tb % 2, f * P:(f + 1) * P], ident[:, :])
                    last.then_inc(sem("hT_tr"), 1)

            def norm(j, start):
                for tb in range(start, TB):
                    norm_tr(j, tb)
                pe.wait_ge(sem("hT_lo"), 8 * (j + 1))

            def z_block(c, tb, h):
                if tb == 0:
                    wait_chunk(pe, c, h)
                pe.wait_ge(sem("z_evac"), h * 8 + 4 * c + tb + 1)
                token_chunk(pb[tb], c, tb, h_lhs).then_inc(sem("z_mm") if tb < 3 else chunk_used, 1)

            def v_item(c, tb, h, first):
                z_block(G_V + c, tb, h)

            def u_item(c, tb, h, first):
                z_block(G_U + c, tb, h)
                if not first:
                    y_transpose(*before(c, tb), h)

            def y_transpose(c, tb, h):
                pe.wait_ge(sem("y_done"), h * 8 + 4 * c + tb + 1 + 2)
                pe.wait_ge(sem("y_lo"), h * 8 + 4 * c + tb + 1)
                for f in range(4):
                    last = nc.tensor.transpose(pb[4 + tb % 2][:, f * P:(f + 1) * P],
                                               ytok[:, tb % 2, f * P:(f + 1) * P], ident[:, :])
                last.then_inc(sem("y_tr"), 1)

            def gmlp():
                pe.sem_inc(sem("y_tr"), 2)
                z_items(pe, v_item)
                pe.wait_ge(sem("ws_masked"), 1)
                for c in range(NCH_Z):
                    for tb in range(TB):
                        idx = c * TB + tb
                        pe.wait_ge(sem("vn_ready"), idx + 1)
                        if idx >= 4:
                            pe.wait_ge(sem("mix_evac"), idx - 3)
                        at = 0
                        while at < 512:
                            g = (c * 512 + at) // GW
                            w = min(512, (g + 1) * GW - c * 512) - at
                            last = nc.tensor.matmul(pb[4 + idx % 4][:, at:at + w], wsT[:, g, :],
                                                    vmix[:, c, tb, at:at + w], start=True, stop=True)
                            at += w
                        last.then_inc(sem("mix_mm"), 1)
                pe.wait_ge(sem("mix_evac"), NCH_Z * TB)
                z_items(pe, u_item)
                y_transpose(*Z_LAST, 0)
                pe.wait_ge(sem("y_lo"), 2 + NCH_Z * TB)
                for n in range(2):
                    for kg in range(3):
                        c = G_OUT + 3 * n + kg
                        wait_chunk(pe, c)
                        for tb in range(TB):
                            mm = token_chunk(pb[4 * n + tb], c, tb,
                                             lambda k, t, part: yT(2 * kg + k // 4, t, part)[:, k % 4, :],
                                             first=kg == 0, last=kg == 2)
                            if kg == 2 and tb < 3:
                                mm.then_inc(sem("zo_mm"), 1)
                            if n == 1 and kg == 2 and tb == 2:
                                norm_tr(1, 0)
                        mm.then_inc(chunk_used, 1)

            def query(layer):
                base, n = G_PEER[layer], f"{layer}"
                with pe.Fori(0, NCH_Q // 2) as i:
                    for k in range(2):
                        wait_chunk(pe, base + k, i)
                        for f in range(4):
                            pe.wait_ge(sem("q_evac" + n), i * 8 + 4 * k + f + 1)
                            feature_chunk(pb[f], base + k, f).then_inc(sem("q_mm" + n) if f < 3 else chunk_used, 1)
                pe.wait_ge(sem("q_evac" + n), 4 + 16)
                pe.wait_ge(sem("keys_loaded"), 16 * (layer + 1))
                for idx in range(4 * TB):
                    tb = idx // 4
                    if idx >= 4:
                        pe.wait_ge(sem("s_evac" + n), idx - 3)
                    for r in range(4):
                        j = 4 * (idx % 4) + r
                        last = nc.tensor.matmul(pb[4 + idx % 4][:, r * P:(r + 1) * P], pqT[:, j, tb * P:(tb + 1) * P],
                                                keysT[:, j % 2, :], start=True, stop=True)
                    last.then_inc(sem("s_mm" + n), 1)

            def expert_tile(layer, k, e, h, first):
                n = f"{layer}"
                base = G_PEER[layer] + NCH_Q
                if e == 0:
                    wait_chunk(pe, base + first + k, h)
                pe.wait_ge(sem("gelu_done" + n), h * 8 + 4 * (first + k) + e + 1)
                feature_chunk(pb[e], base + first + k, e).then_inc(sem("u_mm" + n) if e < 3 else chunk_used, 1)

            def experts_first(layer):
                n = f"{layer}"
                pe.sem_inc(sem("sel_tr" + n), 1)
                with pe.Fori(0, TB) as i:
                    for k in range(4):
                        for e in range(4):
                            expert_tile(layer, k, e, i * 2, 0)
                    pe.wait_ge(sem("sel_ready" + n), i + 2)
                    for s in range(4):
                        last = nc.tensor.transpose(pb[4][:, s * P:(s + 1) * P], sel[:, s, :], ident[:, :])
                    last.then_inc(sem("sel_tr" + n), 1)
                pe.sem_inc(sem("gate_mm" + n), 8)
                with pe.Fori(0, TB) as i:
                    for k in range(4):
                        for e in range(4):
                            expert_tile(layer, k, e, i * 2, NCH_E // 2)
                            for q in QUADS[e]:
                                s = q // 4
                                if q % 4 == 0:
                                    pe.wait_ge(sem("hot_ready" + n), i * 8 + 2 * k + s + 1)
                                pe.wait_ge(sem("gate_evac" + n), i * 32 + 8 * k + (q + 1 if q > 1 else q + 2))
                                for t in range(4):
                                    u = 4 * (q % 4) + t
                                    for r in range(2):
                                        last = nc.tensor.matmul(pb[5 + q % 3][:, t * P:(t + 1) * P],
                                                                hot1[:, s, u, :], hot2[r][:, s, u, :],
                                                                start=r == 0, stop=r == 1)
                                last.then_inc(sem("gate_mm" + n), 1)

            def value_chunk(layer, k, h):
                n, c = f"{layer}", G_PEER[layer] + NCH_Q + NCH_E + k
                wait_chunk(pe, c, h)
                pe.wait_ge(sem("h_ready" + n), h * 2 + k + 1 + 2)
                w = [v[:, :].rearrange("p (e n) -> p e n", e=4) for v in wsp[c % 2]]
                for e in range(4):
                    for tb in range(TB):
                        for a, b in ((0, 0), (0, 1), (1, 0)):
                            for half in range(2):
                                mm = nc.tensor.matmul(pb[2 * tb + half][:, :],
                                                      hsp[k % 2][a][:, e, tb * P:(tb + 1) * P],
                                                      w[b][:, e, 512 * half:512 * half + 512],
                                                      start=False, stop=False)
                mm.then_inc(chunk_used, 1)

            def experts_second(layer):
                n = f"{layer}"
                pe.wait_ge(sem("gelu_done" + n), 4 + 4 * NCH_E)
                pe.wait_ge(sem("gate_evac" + n), 3 + SEQ // 4)
                pe.wait_ge(sem("selT_ready" + n), TB)
                for b in range(8):
                    nc.tensor.matmul(pb[b][:, :], zeros[:, 0:P], zeros[:, :], start=True, stop=False)
                with pe.Fori(0, NCH_E // 2) as i:
                    for k in range(2):
                        value_chunk(layer, k, i)
                for b in range(8):
                    last = nc.tensor.matmul(pb[b][:, :], zeros[:, 0:P], zeros[:, :], start=False, stop=True)
                last.then_inc(sem("v_mm" + n), 1)

            def attention():
                def heads_tr(part):
                    pe.wait_ge(sem("qr_ready"), part + 1)
                    for tb in range(TB):
                        if part:
                            pe.wait_ge(sem("qk_T"), TB * (part - 1) + tb + 1)
                        for k in range(4 if part < 2 else 2):
                            last = nc.tensor.transpose(pb[4 + tb][:, k * P:(k + 1) * P],
                                                       qr[part][:, tb, k * P:(k + 1) * P], ident[:, :])
                        last.then_inc(sem("qk_tr"), 1)

                for c in range(NCH_QKV):
                    wait_chunk(pe, G_QKV + c)
                    for tb in range(TB):
                        if c:
                            pe.wait_ge(sem("qkv_evac"), TB * (c - 1) + tb + 1)
                        token_chunk(pb[tb], G_QKV + c, tb, h_lhs) \
                            .then_inc(sem("qkv_mm") if tb < 3 else chunk_used, 1)
                    if c:
                        heads_tr(c - 1)
                heads_tr(2)
                pe.wait_ge(sem("qkv_evac"), TB * NCH_QKV)

                def score(u):
                    tb, half = u // 2, u % 2
                    key0 = (tb * P - 64) if tb else 0
                    width = 192 if tb else P
                    if u:
                        pe.wait_ge(sem("scores_taken"), u)
                    for r in range(4):
                        for par in range(2):
                            rows = slice(64 * par, 64 * par + 64)
                            at = 256 * (r % 2)
                            mm = nc.tensor.matmul(pb[r // 2 * 2 + par][:, at:at + width],
                                                  qT[rows, 4 * half + r, tb * P:(tb + 1) * P],
                                                  kT[rows, half, key0:key0 + width], start=True, stop=True)
                            if r % 2:
                                mm.then_inc(sem("qk_mm"), 1)

                def prob_transpose(u, r):
                    idx = 4 * u + r
                    if idx >= 2:
                        pe.wait_ge(sem("probT_ready"), idx - 1)
                    for at, (par, blk) in enumerate(((0, 1), (1, 1), (0, 0), (1, 0))[:4 if u >= 2 else 2]):
                        last = nc.tensor.transpose(pb[4 + r % 2][:, at * P:(at + 1) * P],
                                                   prob[u % 3][:, 2 * r + par, blk * P:(blk + 1) * P], ident[:, :])
                    last.then_inc(sem("prob_tr"), 1)

                def weighted(u, r):
                    tb, half = u // 2, u % 2
                    pe.wait_ge(sem("probT_ready"), 4 * u + r + 1)
                    if r == 0 and u >= 2:
                        pe.wait_ge(sem("oT_lo"), u - 1)
                    for par in range(2):
                        kv = 2 * half + par
                        cols = slice(QK + HD * kv, QK + HD * kv + HD)
                        o = pb[6 + half][64 * par:64 * par + 64, r * P:(r + 1) * P]
                        last = nc.tensor.matmul(o, qkv[:, tb, cols], probT[:, r, par * P:(par + 1) * P],
                                                start=True, stop=tb == 0)
                        if tb:
                            last = nc.tensor.matmul(o, qkv[:, tb - 1, cols], probT[:, r, (2 + par) * P:(3 + par) * P],
                                                    start=False, stop=True)
                    last.then_inc(sem("pv_mm"), 1)

                pe.wait_ge(sem("qk_T"), 3 * TB)
                score(0)
                score(1)
                for u in range(UNITS):
                    if u + 2 < UNITS:
                        score(u + 2)
                    pe.wait_ge(sem("prob_ready"), u + 1)
                    for r in range(5):
                        if r < 4:
                            prob_transpose(u, r)
                        if r:
                            weighted(u, r - 1)
                pe.wait_ge(sem("oT_lo"), UNITS)
                for c in range(NCH_O):
                    wait_chunk(pe, G_WO + c)
                    for tb in range(TB):
                        token_chunk(pb[4 * c + tb], G_WO + c, tb, h_lhs) \
                            .then_inc(sem("ao_mm") if tb < 3 else chunk_used, 1)
                        if c == 1 and tb == 2:
                            norm_tr(3, 0)

            pe.sem_inc(chunk_used, CREDIT)
            pe.wait_ge(sem("ident_ready"), 1)
            pe.wait_ge(sem("zeros_ready"), 1)
            norm(0, 0)
            gmlp()
            norm(1, 1)
            if stages > 1:
                query(0)
                experts_first(0)
                experts_second(0)
            if stages > 2:
                norm(2, 0)
                attention()
                norm(3, 1)
            if stages > 3:
                query(1)
                experts_first(1)
                experts_second(1)


def kernel(stages=4, **inputs):
    import numpy as np
    import concourse.bacc as bacc
    from concourse.bass_utils import run_bass_kernel_spmd

    def get(name):
        return np.asarray(inputs[name])

    def columns(w, n=512):
        return w.reshape(KT, P, -1, n).transpose(2, 1, 0, 3).reshape(-1, P, CH)

    order = np.array([(4 * (2 * m + par) + g) for m in range(2) for g in range(4) for par in range(2)])
    q_cols = (order[:, None] * HD + np.arange(HD)[None, :]).ravel()
    qkv_cols = np.concatenate([q_cols, np.arange(QW, QW + 512)])

    stream = np.empty((CHUNKS, P, CH), np.float32)
    w_in = get("gmlp_w_in")[0]
    stream[G_V:G_V + NCH_Z] = columns(w_in[:, HALF:])
    stream[G_U:G_U + NCH_Z] = columns(w_in[:, :HALF])
    stream[G_OUT:G_OUT + NCH_OUT] = get("gmlp_w_out")[0].reshape(3, 8, P, 2, 512) \
        .transpose(3, 0, 2, 1, 4).reshape(NCH_OUT, P, CH)
    stream[G_QKV:G_QKV + NCH_QKV] = columns(get("attn_w_qkv")[0][:, qkv_cols])
    stream[G_WO:G_WO + NCH_O] = columns(get("attn_w_o")[0][q_cols, :])
    for layer in range(2):
        g = G_PEER[layer]
        stream[g:g + NCH_Q] = columns(get("peer_w_query")[layer])
        u = get("peer_expert_u")[layer].reshape(P, NCH_E, 4, KT, P)
        stream[g + NCH_Q:g + NCH_Q + NCH_E] = u.transpose(1, 4, 3, 2, 0).reshape(NCH_E, P, CH)
        v = get("peer_expert_v")[layer].reshape(P, NCH_E, CH)
        stream[g + NCH_Q + NCH_E:g + NCH_Q + 2 * NCH_E] = v.transpose(1, 0, 2)

    gb = get("gmlp_b_in")[0].reshape(2, NCH_Z, 512)
    mix_g, ffn_g = get("mix_norm_g"), get("ffn_norm_g")
    pos = np.arange(SEQ, dtype=np.float32)
    inv = (1.0 / (10000.0 ** (np.arange(0, HD, 2, dtype=np.float32) / HD))).astype(np.float32)
    ang = pos[:, None] * inv[None, :]
    rope = np.stack([np.cos(ang), np.sin(ang)]).astype(np.float32)
    keys = np.stack([get("peer_keys_1"), get("peer_keys_2")], 1)
    arrays = {
        "x": get("x").reshape(SEQ, D),
        "stream": stream,
        "gains": np.stack([mix_g[0], ffn_g[0], mix_g[1], ffn_g[1]]),
        "gmlp_bias": np.concatenate([gb[1], gb[0]]),
        "ln_gb": np.stack([get("gmlp_ln_g")[0], get("gmlp_ln_b")[0]]),
        "w_s": get("gmlp_w_s")[0].transpose(2, 0, 1),
        "b_s": get("gmlp_b_s")[0].T,
        "b_out": get("gmlp_b_out")[0],
        "qkv_bias": get("attn_b_qkv")[0][qkv_cols],
        "b_o": get("attn_b_o")[0],
        "qk_gain": np.concatenate([get("attn_q_gain")[0], get("attn_k_gain")[0]]),
        "sinks": get("attn_sinks")[0][order],
        "rope": rope.reshape(2, TB, P, HD // 2).transpose(2, 0, 1, 3),
        "keys": keys.transpose(0, 3, 1, 2),
    }
    nc = bacc.Bacc("TRN2", target_bir_lowering=False, num_devices=1)
    arrays = {f"in_{k}": np.ascontiguousarray(a) for k, a in arrays.items()}
    args = [nc.dram_tensor(k, a.shape, mybir.dt.from_np(a.dtype), kind="ExternalInput").ap()
            for k, a in arrays.items()]
    out = nc.dram_tensor("out", (SEQ, D), F32, kind="ExternalOutput").ap()
    build(nc, *args, out, stages=stages)
    r = run_bass_kernel_spmd(nc, [arrays], core_ids=[0])
    return r.results[0]["out"].reshape(1, SEQ, D)
```

```python
from contextlib import ExitStack

import concourse.bass as bass
from concourse import mybir

ALU = mybir.AluOpType
ACT = mybir.ActivationFunctionType
F32 = mybir.dt.float32
BF16 = mybir.dt.bfloat16
U32 = mybir.dt.uint32
AX_X = mybir.AxisListType.X

P = 128
SEQ = 512
D = 1024
TB = SEQ // P
KT = D // P
HALF = 3072
GW = HALF // 8
CH = 4096
NCH_Z = HALF // 512
NCH_OUT = 6
NCH_Q = 4
NCH_E = 32
NCH_QKV = 3
NCH_O = 2
HEADS = 16
HD = 64
QW = HEADS * HD
QK = QW + 256
PH = 8
TOPK = 16
BT = 32
EPS = 1e-6
NEG = -1e30
LOWEST = -3.0e38

G_V, G_U = 0, NCH_Z
G_OUT = 2 * NCH_Z
G_PEER = [G_OUT + NCH_OUT, 0]
G_QKV = G_PEER[0] + NCH_Q + 2 * NCH_E
G_WO = G_QKV + NCH_QKV
G_PEER[1] = G_WO + NCH_O
CHUNKS = G_PEER[1] + NCH_Q + 2 * NCH_E
QUADS = [[], [0, 1, 2], [3, 4], [5, 6, 7]]
UNITS = 2 * TB
AHEAD = 3
CREDIT = 2


def build(nc, x, stream, gains, gmlp_bias, ln_gb, w_s, b_s, b_out, qkv_bias, b_o,
          qk_gain, sinks, rope, keys, out, stages=4):
    with ExitStack() as ctx:
        def sb(name, shape, dt=F32):
            return ctx.enter_context(nc.sbuf_tensor(name, shape, dt))

        sems = {}

        def sem(name):
            if name not in sems:
                sems[name] = ctx.enter_context(nc.semaphore(name))
            return sems[name]

        xres = sb("xres", [P, TB, D])
        hT = [sb("hT_hi", [P, KT, SEQ], BF16), sb("hT_lo", [P, KT, SEQ], BF16)]
        raw = [sb(f"raw{b}", [P, CH]) for b in range(2)]
        wsp = [[sb(f"w_hi{b}", [P, CH], BF16), sb(f"w_lo{b}", [P, CH], BF16)] for b in range(2)]
        gain = sb("gain", [P, D])
        ident = sb("ident", [P, P])
        iota = sb("iota", [P, TOPK])
        iota_b = sb("iota_b", [P, P], BF16)
        epsilon = sb("epsilon", [P, 1])
        mask = sb("mask", [P, 192])
        sumsq = sb("sumsq", [P, TB])
        rootms = sb("rootms", [P, TB])
        rstd = sb("rstd", [P, TB])
        arena = sb("arena", [P, 26300])
        pb = [ctx.enter_context(nc.psum_tensor(f"bank{i}", [P, 512], F32)) for i in range(8)]

        def area(start, words, dt=F32):
            a = arena[:, start:start + words]
            return a if dt == F32 else a.bitcast(dt)

        s_dram = nc.dram_tensor("acts_scratch", (NCH_E, P, 2048), F32, kind="Internal").ap()
        a_dram = nc.dram_tensor("gates_scratch", (P, SEQ // BT, P * BT), F32, kind="Internal").ap()

        hn = area(24064, 2048).rearrange("p (b n) -> p b n", b=2)
        squares = area(12288, D)

        vmix = area(0, 12288).rearrange("p (c t n) -> p c t n", c=NCH_Z, t=TB)
        zt = area(12288, 1024).rearrange("p (b n) -> p b n", b=2)
        ytok = area(13312, 1024).rearrange("p (b n) -> p b n", b=2)
        zbias = area(14336, 1024).rearrange("p (b n) -> p b n", b=2)
        wsT = area(15360, 1024).rearrange("p (g i) -> p g i", g=8)
        ln_g = area(16384, HALF)
        ln_b = area(19456, HALF)
        bsT = area(22528, 8)
        bn = area(22536, 144).rearrange("p (t c s) -> p t c s", t=TB, c=NCH_Z)
        ln_mv = area(22688, 8).rearrange("p (t s) -> p t s", t=TB)
        ln_sd = area(22700, 4)
        ln_rs = area(22704, 4)
        ln_ve = area(22708, 4)
        ugel = area(22784, 1024).rearrange("p (b n) -> p b n", b=2)
        bout = ugel.rearrange("p b n -> p (b n)")

        def yT(c, tb, part):
            v = vmix[:, c, tb, 256 * part:256 * part + 256].bitcast(BF16)
            return v.rearrange("p (f t) -> p f t", f=4)

        qkv = area(0, 6144).rearrange("p (t n) -> p t n", t=TB)
        qr = [area(6144, 2048).rearrange("p (t n) -> p t n", t=TB),
              area(14208, 2048).rearrange("p (t n) -> p t n", t=TB),
              area(6144, 1024).rearrange("p (t n) -> p t n", t=TB)]
        tmp = area(16256, 2048)
        tabs = area(8704, 256).rearrange("p (s t n) -> p s t n", s=2, t=TB)
        qkg = area(8960, 128).rearrange("p (s n) -> p s n", s=2)
        qT = area(9088, 4096).rearrange("p (j t) -> p j t", j=8)
        kT = area(13184, 1024).rearrange("p (j t) -> p j t", j=2)
        prob = [area(start, 2048).rearrange("p (h k) -> p h k", h=8) for start in (14208, 16256, 6144)]
        probT = area(18304, 2048).rearrange("p (b n) -> p b n", b=4)
        qbias = area(20352, 1536)
        bo = area(18304, 1024)
        hss = area(23168, 32)
        hrt = area(23200, 32)
        hrs = area(23232, 32)
        sink = area(23264, 16)
        gtabs = area(21888, 1024).rearrange("p (w s t n) -> p w s t n", w=2, s=4, t=TB)
        smax, nmax, ssum, esink, srec = (area(23296 + 32 * r, 24).rearrange("p (u h) -> p u h", u=3)
                                         for r in range(5))

        scores = area(0, 8192).rearrange("p (t n) -> p t n", t=TB)
        hot1 = area(0, 2048, BF16).rearrange("p (s t n) -> p s t n", s=2, t=16)
        hot2 = [area(2048 + 2048 * r, 2048, BF16).rearrange("p (s t n) -> p s t n", s=2, t=16) for r in range(2)]
        pqT = area(8192, 8192).rearrange("p (j t) -> p j t", j=16)
        gstage = area(8192, 8192).rearrange("p (b e t) -> p b e t", b=2, t=BT)
        sstage = area(16384, 4096).rearrange("p (b e t) -> p b e t", b=2, e=4)
        sblk = area(8192, 2048).rearrange("p (j n) -> p j n", j=16)
        onehot = area(20480, 2048).rearrange("p (s j) -> p s j", j=TOPK)
        cand = area(22528, 512).rearrange("p (h n) -> p h n", h=2)
        posn = area(22528, 256, U32).rearrange("p (s n) -> p s n", s=2)
        posf = area(22784, 256).rearrange("p (s n) -> p s n", s=2)
        work = area(23040, 512)
        topif = area(23040, 256).rearrange("p (j k) -> p j k", j=16)
        selT = area(23552, 2048).rearrange("p (s t) -> p s t", s=4)
        sel = area(25600, 512).rearrange("p (s n) -> p s n", s=4)
        gate_b = area(26112, 64, BF16)
        topv = area(10240, 256).rearrange("p (j k) -> p j k", j=16)
        topi = area(10496, 256, U32).rearrange("p (j k) -> p j k", j=16)
        best = area(10752, P).rearrange("p (h k) -> p h k", h=PH)
        bestp = area(10880, P, U32).rearrange("p (h k) -> p h k", h=PH)
        tslice = sb("tslice", [P, 2, 4, BT])
        keysT = sb("keysT", [P, 2, P])
        gsum = sb("gsum", [P, PH])
        grec = sb("grec", [P, PH])
        s_in = [area(6144, 2048), area(0, 2048)]
        a_in = [area(20480, 2048), area(2048, 2048)]
        hsp = [[area(8192 + 2048 * b + 1024 * s, 1024, BF16).rearrange("p (e t) -> p e t", e=4)
                for s in range(2)] for b in range(2)]
        hf = [area(22528, 2048), area(4096, 2048)]

        raw_loaded = [sem("raw_loaded0"), sem("raw_loaded1")]
        hi_done, lo_done, chunk_used = sem("hi_done"), sem("lo_done"), sem("chunk_used")

        class Chain:
            def __init__(self, eng, name):
                self.eng, self.sem, self.n = eng, sem(name), 0

            def link(self, ins):
                ins.then_inc(self.sem, 1)
                self.n += 1
                self.eng.wait_ge(self.sem, self.n)

            def restart(self):
                self.eng.sem_clear(self.sem)
                self.n = 0

        def split_hi(act, c, h=0):
            b = c % 2
            act.wait_ge(raw_loaded[b], h * 16 + 16 * (c // 2 + 1))
            act.wait_ge(chunk_used, h * 2 + c + 1)
            nc.scalar.copy(wsp[b][0][:, :], raw[b][:, :]).then_inc(hi_done, 1)

        def split_lo(dve, c, h=0):
            b = c % 2
            dve.wait_ge(hi_done, h * 2 + c + 1)
            nc.vector.tensor_tensor(wsp[b][1][:, :], raw[b][:, :], wsp[b][0][:, :],
                                    ALU.subtract).then_inc(lo_done, 1)

        def wait_chunk(pe, c, h=0):
            pe.wait_ge(lo_done, h * 2 + c + 1 + CREDIT)

        def wait_output(eng, outs, c, base, s, h=0):
            if s < 3:
                eng.wait_ge(outs, h * 6 + 3 * (c - base) + s + 1)
            else:
                eng.wait_ge(chunk_used, h * 2 + c + 1 + CREDIT)

        def token_chunk(bank, c, tb, lhs, first=True, last=True):
            w = [v[:, :].rearrange("p (k n) -> p k n", k=8) for v in wsp[c % 2]]
            for k in range(8):
                for n, (a, b) in enumerate(((0, 0), (0, 1), (1, 0))):
                    mm = nc.tensor.matmul(bank[:, :], lhs(k, tb, a), w[b][:, k, :],
                                          start=first and k == 0 and n == 0,
                                          stop=last and k == 7 and n == 2)
            return mm

        def feature_chunk(bank, c, f, t0=0, t1=SEQ):
            w = [v[:, :].rearrange("p (k n) -> p k n", k=8) for v in wsp[c % 2]]
            for k in range(8):
                for n, (a, b) in enumerate(((0, 0), (0, 1), (1, 0))):
                    mm = nc.tensor.matmul(bank[:, t0:t1], w[a][:, k, f * P:(f + 1) * P], hT[b][:, k, t0:t1],
                                          start=k == 0 and n == 0, stop=k == 7 and n == 2)
            return mm

        def h_lhs(k, tb, part):
            return hT[part][:, k, tb * P:(tb + 1) * P]

        def z_items(eng, item):
            for c in (0, 1):
                for tb in range(TB):
                    item(c, tb, 0, c == 0 and tb == 0)
            with eng.Fori(0, NCH_Z // 2 - 1) as i:
                for c in (2, 3):
                    for tb in range(TB):
                        item(c, tb, i, False)

        def before(c, tb):
            return (c, tb - 1) if tb else (c - 1, TB - 1)

        Z_LAST = (NCH_Z - 1, TB - 1)

        block = ctx.enter_context(nc.Block())

        @block.sync
        def _(sp):
            used = min(CHUNKS, [0, G_PEER[0], G_QKV, G_PEER[1], CHUNKS][stages] + 1)
            s_stored = [sem("s_stored0"), sem("s_stored1")]
            a_stored = [sem("a_stored0"), sem("a_stored1")]

            def load_chunk(c, h=0):
                if c < used:
                    sp.wait_ge(lo_done, h * 2 + c + 1)
                    sp.dma_start(raw[c % 2][:, :], stream[h * 2 + c]).then_inc(raw_loaded[c % 2], 16)

            def load_run(first, end):
                end = min(end, used)
                pairs = (end - first) // 2
                if pairs > 1:
                    with sp.Fori(0, pairs) as i:
                        for b in range(2):
                            load_chunk(first + b, i)
                    first += 2 * pairs
                for c in range(first, end):
                    load_chunk(c)

            def store_acts(layer, c, h=0):
                sp.wait_ge(sem(f"gelu_done{layer}"), h * 8 + 4 + 4 * (c + 1))
                sp.dma_start(s_dram[h * 2 + c], sstage[:, c % 2, :, :].rearrange("p e t -> p (e t)")) \
                    .then_inc(s_stored[c % 2], 16)

            def store_gates(layer, g, h=0):
                sp.wait_ge(sem(f"gate_evac{layer}"), h * 16 + 3 + 8 * (g + 1))
                sp.dma_start(a_dram[:, bass.ds(h * 2 + g, 1), :],
                             gstage[:, g % 2:g % 2 + 1, :, :].rearrange("p o e t -> p o (e t)")) \
                    .then_inc(a_stored[g % 2], 16)

            def load_gated(c, h=0):
                sp.dma_start(s_in[c % 2], s_dram[h * 2 + c]).then_inc(sem(f"sa_loaded{c % 2}"), 16)
                sp.dma_start(a_in[c % 2].rearrange("p (g n) -> p g n", g=SEQ // BT),
                             a_dram[:, :, bass.ds((h * 2 + c) * (4 * BT), 4 * BT)]) \
                    .then_inc(sem(f"sa_loaded{c % 2}"), 16)

            def peer(layer):
                batches = SEQ // BT
                first = G_PEER[layer] + NCH_Q + AHEAD
                with sp.Fori(0, (NCH_E - batches) // 2) as i:
                    for b in range(2):
                        load_chunk(first + b, i)
                        store_acts(layer, b, i)
                with sp.Fori(0, batches // 2 - 1) as i:
                    for b in range(2):
                        load_chunk(first + NCH_E - batches + b, i)
                        store_acts(layer, NCH_E - batches + b, i)
                        store_gates(layer, b, i)
                load_chunk(first + NCH_E - 2)
                store_acts(layer, NCH_E - 2)
                store_gates(layer, batches - 2)
                for b in range(2):
                    sp.wait_ge(s_stored[b], 16 * (NCH_E // 2 * (layer + 1) + 1 - b))
                    sp.wait_ge(a_stored[b], 16 * (batches // 2 * (layer + 1) + 1 - b))
                sp.dma_start(s_in[0], s_dram[0]).then_inc(sem("sa_loaded0"), 16)
                sp.dma_start(a_in[0].rearrange("p (g n) -> p g n", g=batches)[:, 0:batches - 1, :],
                             a_dram[:, 0:batches - 1, 0:4 * BT]).then_inc(sem("sa_loaded0"), 16)
                store_acts(layer, NCH_E - 1)
                store_gates(layer, batches - 1)
                first += NCH_E
                sp.wait_ge(s_stored[1], 16 * (NCH_E // 2 * (layer + 1) + 1))
                sp.wait_ge(a_stored[1], 16 * (batches // 2 * (layer + 1) + 1))
                sp.wait_ge(sem(f"gate_mm{layer}"), 8 + 4 * (SEQ // 16))
                load_gated(1)
                load_chunk(first - 1)
                load_chunk(first)

                def slot(c, h=0):
                    if c:
                        load_chunk(first + c, h)
                    if c + 2 < NCH_E:
                        sp.wait_ge(sem(f"h_ready{layer}"), h * 2 + c + 1 + 2)
                        load_gated(c + 2, h)

                slot(0)
                slot(1)
                with sp.Fori(0, NCH_E // 2 - 3) as i:
                    for b in (2, 3):
                        slot(b, i)
                for c in range(NCH_E - 4, NCH_E):
                    slot(c)

            for b in range(2):
                sp.sem_inc(s_stored[b], 16)
                sp.sem_inc(a_stored[b], 16)
            for tb in range(TB):
                if tb == 2:
                    load_chunk(0)
                sp.dma_start(xres[:, tb, :], x[tb * P:(tb + 1) * P, :]).then_inc(sem(f"x_loaded{tb}"), 16)
            load_chunk(1)
            load_run(2, G_PEER[0] + NCH_Q + AHEAD)
            if stages > 1:
                peer(0)
            if stages > 2:
                load_run(G_QKV + AHEAD, G_PEER[1] + NCH_Q + AHEAD)
            if stages > 3:
                peer(1)
            for tb in range(TB):
                sp.wait_ge(sem("x_ready"), 4 * stages + tb + 1)
                sp.dma_start(out[tb * P:(tb + 1) * P, :], xres[:, tb, :]).then_inc(sem("out_stored"), 16)
            sp.wait_ge(sem("out_stored"), 16 * TB)

        @block.gpsimd
        def _(pool):
            def norm_gain(j):
                if j:
                    pool.wait_ge(sem("hn_ready"), 4 * j)
                pool.dma_start(gain[:, :], gains[j].partition_broadcast(P)).then_inc(sem("gain_loaded"), 16)

            def constants():
                nc.gpsimd.memset(ident[:, :], 0.0).then_inc(sem("pool_chain"), 1)
                nc.gpsimd.memset(mask[:, :], 0.0).then_inc(sem("pool_chain"), 1)
                pool.wait_ge(sem("pool_chain"), 2)
                nc.gpsimd.affine_select(out=ident[:, :], in_=ident[:, :], pattern=[[-1, P]],
                                        compare_op=ALU.not_equal, fill=1.0, base=0,
                                        channel_multiplier=1).then_inc(sem("ident_ready"), 1)
                nc.gpsimd.iota(iota[:, :], [[1, TOPK]], base=0, channel_multiplier=0,
                               allow_small_or_imprecise_dtypes=True).then_inc(sem("iota_ready"), 1)
                nc.gpsimd.iota(iota_b[:, :], [[1, P]], base=0, channel_multiplier=0,
                               allow_small_or_imprecise_dtypes=True).then_inc(sem("iota_ready"), 1)
                nc.gpsimd.memset(mask[0:64, 128:192], NEG).then_inc(sem("mask_ready"), 1)
                pool.wait_ge(sem("mask_ready"), 1)
                nc.gpsimd.memset(mask[64:128, 0:64], NEG).then_inc(sem("mask_ready"), 1)

            def gmlp():
                pool.dma_start(bout[:, :], b_out.partition_broadcast(P)).then_inc(sem("bout_loaded"), 16)
                pool.dma_start(wsT[:, :, :], w_s).then_inc(sem("ws_loaded"), 16)
                pool.dma_start(bsT[:, :], b_s).then_inc(sem("bs_loaded"), 16)
                pool.wait_ge(sem("ws_loaded"), 16)
                pool.wait_ge(sem("mask_ready"), 2)
                nc.gpsimd.memset(wsT[64:128, :, 0:64], 0.0).then_inc(sem("ws_masked"), 1)
                for c in range(2 * NCH_Z):
                    if c >= 2:
                        pool.wait_ge(sem("z_evac"), 4 + 4 * (c - 1))
                    pool.dma_start(zbias[:, c % 2, :], gmlp_bias[c].partition_broadcast(P)) \
                        .then_inc(sem(f"zbias_loaded{c % 2}"), 16)
                    if c == 1:
                        pool.dma_start(ln_g[:, :], ln_gb[0].partition_broadcast(P)).then_inc(sem("ln_loaded"), 16)
                        pool.dma_start(ln_b[:, :], ln_gb[1].partition_broadcast(P)).then_inc(sem("ln_loaded"), 16)

            def peer(layer):
                pool.dma_start(keysT[:, :, :], keys[layer]).then_inc(sem("keys_loaded"), 16)

            def attention():
                pool.dma_start(bo[:, :], b_o.partition_broadcast(P)).then_inc(sem("bo_loaded"), 16)
                pool.dma_start(qbias[:, :], qkv_bias.partition_broadcast(P)).then_inc(sem("attn_loaded"), 16)
                pool.dma_start(tabs[:, :, :, :], rope).then_inc(sem("attn_loaded"), 16)
                pool.dma_start(qkg[:, :, :].rearrange("p s n -> p (s n)"),
                               qk_gain.partition_broadcast(P)).then_inc(sem("attn_loaded"), 16)
                pool.dma_start(sink[:, :], sinks.partition_broadcast(P)).then_inc(sem("attn_loaded"), 16)

            norm_gain(0)
            constants()
            gmlp()
            norm_gain(1)
            if stages > 1:
                peer(0)
            if stages > 2:
                norm_gain(2)
                pool.wait_ge(sem("x_ready"), 12)
                attention()
                norm_gain(3)
                pool.wait_ge(sem("qk_tr"), 3 * TB)
                for r in range(3):
                    nc.gpsimd.memset(prob[r][:, :, 0:64], 0.0).then_inc(sem("left_zero"), 1)
            if stages > 3:
                peer(1)

        @block.scalar
        def _(act):
            def norm(j):
                def root(tb):
                    act.wait_ge(sem("x_ready"), 4 * j + tb + 1)
                    nc.scalar.activation(squares[:, :], xres[:, tb, :], ACT.Square,
                                         accum_out=sumsq[:, tb:tb + 1]).then_inc(sem("squared"), 1)
                    act.wait_ge(sem("squared"), 4 * j + tb + 1)
                    nc.scalar.activation(rootms[:, tb:tb + 1], sumsq[:, tb:tb + 1], ACT.Sqrt, scale=1.0 / D,
                                         bias=epsilon[:, 0:1]).then_inc(sem("root_ready"), 1)

                def high(tb):
                    for half in range(2):
                        act.wait_ge(sem("hT_tr"), 8 * j + 2 * tb + half + 1)
                        nc.scalar.copy(hT[0][:, 4 * half:4 * half + 4, tb * P:(tb + 1) * P],
                                       pb[2 * tb + half][:, :].rearrange("p (k t) -> p k t", k=4)) \
                            .then_inc(sem("hT_hi"), 1)

                root(0)
                root(1)
                if j == 0:
                    high(0)
                    high(1)
                    split_hi(act, 0)
                    root(2)
                    root(3)
                else:
                    root(2)
                    high(0)
                    high(1)
                    root(3)
                high(2)
                high(3)

            def v_item(c, tb, h, first):
                if tb == 0:
                    split_hi(act, G_V + c + 1, h)
                act.wait_ge(sem("z_evac"), h * 8 + 4 * (G_V + c) + tb + 1 + 4)
                nc.scalar.activation(vmix[:, bass.ds(h * 2 + c, 1), tb, :], zt[:, tb % 2:tb % 2 + 1, :],
                                     ACT.Gelu_apprx_tanh).then_inc(sem("z_gelu"), 1)

            def u_item(c, tb, h, first):
                act.wait_ge(sem("z_evac"), h * 8 + 4 * (G_U + c) + tb + 1 + 4)
                act.wait_ge(sem("y_done"), h * 8 + 4 * c + tb + 1)
                nc.scalar.activation(ugel[:, tb % 2, :], zt[:, tb % 2, :],
                                     ACT.Gelu_apprx_tanh).then_inc(sem("z_gelu"), 1)
                if not first:
                    y_hi(*before(c, tb), h)
                if tb == 0:
                    split_hi(act, G_U + c + 2, h)

            def y_hi(c, tb, h):
                act.wait_ge(sem("y_tr"), h * 8 + 4 * c + tb + 1 + 2)
                nc.scalar.copy(vmix[:, bass.ds(h * 2 + c, 1), tb, 0:256].bitcast(BF16),
                               pb[4 + tb % 2][:, :].rearrange("p (o n) -> p o n", o=1)).then_inc(sem("y_hi"), 1)

            def gmlp():
                act.sem_inc(sem("y_done"), 2)
                z_items(act, v_item)
                act.wait_ge(sem("lnv_ready"), 1)
                nc.scalar.activation(ln_sd[:, :], ln_ve[:, :], ACT.Sqrt).then_inc(sem("lnsd_ready"), 1)
                split_hi(act, G_U + 1)
                act.wait_ge(sem("bs_loaded"), 16)
                for c in range(NCH_Z):
                    for tb in range(TB):
                        idx = c * TB + tb
                        act.wait_ge(sem("mix_mm"), idx + 1)
                        at = 0
                        while at < 512:
                            g = (c * 512 + at) // GW
                            w = min(512, (g + 1) * GW - c * 512) - at
                            last = nc.scalar.activation(vmix[:, c, tb, at:at + w], pb[4 + idx % 4][:, at:at + w],
                                                        ACT.Identity, bias=bsT[:, g:g + 1])
                            at += w
                        last.then_inc(sem("mix_evac"), 1)
                z_items(act, u_item)
                y_hi(*Z_LAST, 0)
                for c in range(G_OUT + 1, G_OUT + NCH_OUT):
                    split_hi(act, c + 1)

            def query(layer):
                base, n = G_PEER[layer], f"{layer}"
                act.sem_inc(sem("q_evac" + n), 4)
                with act.Fori(0, NCH_Q // 2) as i:
                    for k in range(2):
                        split_hi(act, base + k + 1, i)
                        for f in range(4):
                            wait_output(act, sem("q_mm" + n), base + k, base, f, i)
                            nc.scalar.copy(pqT[:, bass.ds(i * 8 + 4 * k + f, 1), :],
                                           pb[f][:, :].rearrange("p (o n) -> p o n", o=1)) \
                                .then_inc(sem("q_evac" + n), 1)
                for idx in range(4 * TB):
                    act.wait_ge(sem("s_mm" + n), idx + 1)
                    nc.scalar.copy(scores[:, idx // 4, 512 * (idx % 4):512 * (idx % 4) + 512],
                                   pb[4 + idx % 4][:, :]).then_inc(sem("s_evac" + n), 1)

            def gelu_tile(layer, k, e, h, first):
                n, b = f"{layer}", k % 2
                base = G_PEER[layer] + NCH_Q
                if e == 0:
                    split_hi(act, base + first + k + 1, h)
                    act.wait_ge(sem(f"s_stored{b}"), h * 16 + 16 * ((first + k) // 2 + 1 + layer * NCH_E // 2))
                wait_output(act, sem("u_mm" + n), base + first + k, base, e, h)
                nc.scalar.activation(sstage[:, b, e, :], pb[e][:, :],
                                     ACT.Gelu_apprx_tanh).then_inc(sem("gelu_done" + n), 1)

            def experts_first(layer):
                n = f"{layer}"
                act.sem_inc(sem("gelu_done" + n), 4)
                with act.Fori(0, TB) as i:
                    act.wait_ge(sem("best_ready" + n), i + 1)
                    nc.scalar.copy(sblk[:, :, :].rearrange("p j n -> p (j n)").rearrange("p (o n) -> p o n", o=1),
                                   scores[:, bass.ds(i, 1), :]).then_inc(sem("sblk_ready" + n), 1)
                    for k in range(4):
                        for e in range(4):
                            if k == 3 and e == 0:
                                act.wait_ge(sem("best_ready" + n), i + 2)
                                nc.scalar.activation(best[:, :, :], best[:, :, :],
                                                     ACT.Exp).then_inc(sem("best_exp" + n), 1)
                            if k == 3 and e == 3:
                                act.wait_ge(sem("sel_tr" + n), i + 2)
                                nc.scalar.copy(selT[:, :, bass.ds(i * P, P)],
                                               pb[4][:, :].rearrange("p (s t) -> p s t", s=4)) \
                                    .then_inc(sem("selT_ready" + n), 1)
                            gelu_tile(layer, k, e, i * 2, 0)
                act.sem_inc(sem("gate_evac" + n), 3)
                with act.Fori(0, TB) as i:
                    for k in range(4):
                        b = k % 2
                        for e in range(4):
                            gelu_tile(layer, k, e, i * 2, NCH_E // 2)
                            for q in QUADS[e]:
                                if q == 0:
                                    act.wait_ge(sem(f"a_stored{b}"),
                                                i * 32 + 16 * (k // 2 + 1 + layer * SEQ // BT // 2))
                                act.wait_ge(sem("gate_mm" + n), i * 32 + 8 * k + q + 1 + 8)
                                nc.scalar.copy(gstage[:, b, :, 4 * q:4 * q + 4].rearrange("p e t -> p t e"),
                                               pb[5 + q % 3][:, :].rearrange("p (t e) -> p t e", t=4)) \
                                    .then_inc(sem("gate_evac" + n), 1)

            def h_hi(layer, k, h, first=False):
                n = f"{layer}"
                act.wait_ge(sem("hf_ready" + n), h * 2 + k + 1)
                if first:
                    nc.scalar.copy(hsp[k % 2][0][:, :, SEQ - BT:SEQ],
                                   hf[k % 2].rearrange("p (e t) -> p e t", e=4)[:, :, SEQ - BT:SEQ]) \
                        .then_inc(sem("h_hi" + n), 1)
                    return
                nc.scalar.copy(hsp[k % 2][0][:, :, :].rearrange("p e t -> p (e t)"), hf[k % 2]) \
                    .then_inc(sem("h_hi" + n), 1)

            def experts_second(layer):
                base = G_PEER[layer] + NCH_Q + NCH_E
                h_hi(layer, 0, 0, True)
                with act.Fori(0, NCH_E // 2 - 1) as i:
                    for k in range(2):
                        split_hi(act, base + k + 1, i)
                        h_hi(layer, k + 1, i)
                split_hi(act, base + NCH_E - 1)
                h_hi(layer, NCH_E - 1, 0)
                if base + NCH_E < CHUNKS:
                    split_hi(act, base + NCH_E)

            def attention():
                def heads_T(part, blocks=range(TB)):
                    n = 4 if part < 2 else 2
                    dst, at = (qT, 4 * part) if part < 2 else (kT, 0)
                    for tb in blocks:
                        act.wait_ge(sem("qk_tr"), TB * part + tb + 1)
                        nc.scalar.copy(dst[:, at:at + n, tb * P:(tb + 1) * P],
                                       pb[4 + tb][:, 0:n * P].rearrange("p (k t) -> p k t", k=n)) \
                            .then_inc(sem("qk_T"), 1)

                def squares_of(c, tb, width):
                    act.wait_ge(sem("qkv_evac"), TB * c + tb + 1)
                    nc.scalar.activation(tmp[:, 512 * tb:512 * tb + width], qkv[:, tb, 512 * c:512 * c + width],
                                         ACT.Square).then_inc(sem("heads_squared"), 1)

                def roots(done, cols):
                    act.wait_ge(sem("hss_ready"), done)
                    nc.scalar.activation(hrt[:, cols], hss[:, cols], ACT.Sqrt, scale=1.0 / HD,
                                         bias=epsilon[:, 0:1]).then_inc(sem("hroot_ready"), 1)

                for c in range(2):
                    split_hi(act, G_QKV + c + 1)
                    for tb in range(TB):
                        squares_of(c, tb, 512)
                    roots(c + 1, slice(0, 8 * TB))
                    if c:
                        heads_T(0)
                split_hi(act, G_WO)
                for tb in range(TB):
                    squares_of(2, tb, 256)
                    roots(3 + tb, slice(4 * tb, 4 * tb + 4))
                    if tb == 2:
                        heads_T(1)
                heads_T(2)

                def sink_exp(u):
                    act.wait_ge(sem("max_ready"), u + 1)
                    nc.scalar.activation(esink[:, u % 3, :], esink[:, u % 3, :], ACT.Exp)

                def exps(u, heads):
                    lo = 64 if u >= 2 else P
                    for h in heads:
                        last = nc.scalar.activation(prob[u % 3][:, h, lo:256], prob[u % 3][:, h, lo:256], ACT.Exp,
                                                    bias=nmax[:, u % 3, h:h + 1], accum_out=ssum[:, u % 3, h:h + 1])
                    return last

                def probs_T(u, r):
                    idx = 4 * u + r
                    act.wait_ge(sem("prob_tr"), idx + 1)
                    if idx >= 4:
                        act.wait_ge(sem("pv_mm"), idx - 3)
                    cols = slice(0, 512) if u >= 2 else slice(0, 256)
                    nc.scalar.copy(probT[:, r, cols], pb[4 + r % 2][:, cols]).then_inc(sem("probT_ready"), 1)

                def out_high(u):
                    tb, half = u // 2, u % 2
                    act.wait_ge(sem("pv_mm"), 4 * u + 4)
                    nc.scalar.copy(hT[0][:, 4 * half:4 * half + 4, tb * P:(tb + 1) * P],
                                   pb[6 + half][:, :].rearrange("p (k t) -> p k t", k=4)).then_inc(sem("oT_hi"), 1)

                for u in range(UNITS + 1):
                    if u < UNITS:
                        sink_exp(u)
                        exps(u, range(6))
                    if u:
                        probs_T(u - 1, 0)
                    if u < UNITS:
                        exps(u, (6, 7)).then_inc(sem("prob_exp"), 1)
                    if u:
                        for r in range(1, 4):
                            probs_T(u - 1, r)
                        out_high(u - 1)
                for c in range(NCH_O):
                    split_hi(act, G_WO + c + 1)

            act.wait_ge(sem("epsilon_ready"), 1)
            norm(0)
            gmlp()
            norm(1)
            if stages > 1:
                query(0)
                experts_first(0)
                experts_second(0)
            if stages > 2:
                norm(2)
                attention()
                norm(3)
            if stages > 3:
                query(1)
                experts_first(1)
                experts_second(1)

        @block.vector
        def _(dve):
            chain = Chain(dve, "dve_chain")
            link = chain.link

            def norm(j, produce):
                def scaled(tb):
                    dve.wait_ge(sem("root_ready"), 4 * j + tb + 1)
                    link(nc.vector.reciprocal(rstd[:, tb:tb + 1], rootms[:, tb:tb + 1]))
                    if tb >= 2:
                        dve.wait_ge(sem("hT_tr"), 8 * j + 2 * (tb - 1))
                    nc.vector.scalar_tensor_tensor(hn[:, tb % 2, :], xres[:, tb, :], rstd[:, tb:tb + 1],
                                                   gain[:, :], ALU.mult, ALU.mult).then_inc(sem("hn_ready"), 1)

                def low(tb):
                    for half in range(2):
                        dve.wait_ge(sem("hT_hi"), 8 * j + 2 * tb + half + 1)
                        at = (slice(None), slice(4 * half, 4 * half + 4), slice(tb * P, (tb + 1) * P))
                        nc.vector.tensor_tensor(hT[1][at],
                                                pb[2 * tb + half][:, :].rearrange("p (k t) -> p k t", k=4),
                                                hT[0][at], ALU.subtract).then_inc(sem("hT_lo"), 1)

                produce(0)
                produce(1)
                dve.wait_ge(sem("gain_loaded"), 16 * (j + 1))
                scaled(0)
                if j == 0:
                    scaled(1)
                    low(0)
                    low(1)
                    split_lo(dve, 0)
                    produce(2)
                    produce(3)
                    scaled(2)
                else:
                    produce(2)
                    scaled(1)
                    low(0)
                    scaled(2)
                    low(1)
                    produce(3)
                scaled(3)
                low(2)
                low(3)

            def x_loaded(tb):
                dve.wait_ge(sem(f"x_loaded{tb}"), 16)
                dve.sem_inc(sem("x_ready"), 1)

            def add_rows(row, waited):
                dve.wait_ge(sem(waited), 16)
                for tb in range(TB):
                    nc.vector.tensor_tensor(xres[:, tb, :], xres[:, tb, :], row[:, :], ALU.add) \
                        .then_inc(sem("bias_added"), 1)

            def bias_z(c, tb, h):
                if tb == 0:
                    dve.wait_ge(sem(f"zbias_loaded{c % 2}"), h * 16 + 16 * (c // 2 + 1))
                wait_output(dve, sem("z_mm"), c, 0, tb, h)
                dve.wait_ge(sem("z_gelu"), h * 8 + 4 * c + tb + 1)
                nc.vector.tensor_tensor(zt[:, tb % 2, :], pb[tb][:, :], zbias[:, c % 2, :],
                                        ALU.add).then_inc(sem("z_evac"), 1)

            def y_block(c, tb, h):
                dve.wait_ge(sem("z_gelu"), h * 8 + 4 * (G_U + c) + tb + 1 + 2)
                dve.wait_ge(sem("y_tr"), h * 8 + 4 * c + tb + 1)
                nc.vector.tensor_tensor(ytok[:, tb % 2:tb % 2 + 1, :], ugel[:, tb % 2:tb % 2 + 1, :],
                                        vmix[:, bass.ds(h * 2 + c, 1), tb, :], ALU.mult) \
                    .then_inc(sem("y_done"), 1)

            def y_lo(c, tb, h):
                dve.wait_ge(sem("y_hi"), h * 8 + 4 * c + tb + 1)
                at = bass.ds(h * 2 + c, 1)
                nc.vector.tensor_tensor(vmix[:, at, tb, 256:512].bitcast(BF16),
                                        pb[4 + tb % 2][:, :].rearrange("p (o n) -> p o n", o=1),
                                        vmix[:, at, tb, 0:256].bitcast(BF16), ALU.subtract) \
                    .then_inc(sem("y_lo"), 1)

            def v_stats(c, tb, h):
                dve.wait_ge(sem("z_gelu"), h * 8 + 4 * c + tb + 1 + 2)
                return nc.vector.bn_stats(bn[:, tb, bass.ds(h * 2 + c, 1), :].rearrange("p c s -> p (c s)"),
                                          vmix[:, bass.ds(h * 2 + c, 1), tb, :].rearrange("p c n -> p (c n)"))

            def v_item(c, tb, h, first):
                bias_z(G_V + c, tb, h)
                if tb == 0:
                    split_lo(dve, G_V + c + 1, h)
                if not first:
                    v_stats(*before(c, tb), h)

            def u_item(c, tb, h, first):
                bias_z(G_U + c, tb, h)
                if tb == 2:
                    split_lo(dve, G_U + c + 2, h)
                if not first:
                    y_lo(*before(c, tb), h)
                else:
                    dve.wait_ge(sem("mix_evac"), TB * NCH_Z)
                y_block(c, tb, h)

            def gmlp():
                dve.sem_inc(sem("z_gelu"), 2)
                dve.sem_inc(sem("y_lo"), 2)
                z_items(dve, v_item)
                link(v_stats(*Z_LAST, 0))
                for tb in range(TB):
                    last = nc.vector.bn_aggr(ln_mv[:, tb, :], bn[:, tb, :, :].rearrange("p c s -> p (c s)"))
                link(last)
                nc.vector.tensor_scalar(ln_ve[:, :], ln_mv[:, :, 1], EPS, None, ALU.add).then_inc(sem("lnv_ready"), 1)
                dve.wait_ge(sem("lnsd_ready"), 1)
                link(nc.vector.reciprocal(ln_rs[:, :], ln_sd[:, :]))
                dve.wait_ge(sem("ln_loaded"), 32)
                for c in range(NCH_Z):
                    cols = slice(512 * c, 512 * c + 512)
                    for tb in range(TB):
                        v = vmix[:, c, tb, :]
                        last = nc.vector.scalar_tensor_tensor(v, v, ln_mv[:, tb, 0:1], ln_g[:, cols],
                                                              ALU.subtract, ALU.mult)
                    link(last)
                    for tb in range(TB):
                        v = vmix[:, c, tb, :]
                        nc.vector.scalar_tensor_tensor(v, v, ln_rs[:, tb:tb + 1], ln_b[:, cols],
                                                       ALU.mult, ALU.add).then_inc(sem("vn_ready"), 1)
                split_lo(dve, G_U + 1)
                z_items(dve, u_item)
                y_lo(*Z_LAST, 0)
                for c in range(G_OUT + 1, G_OUT + NCH_OUT):
                    split_lo(dve, c + 1)
                    if c == G_OUT + 3:
                        first_half("zo_mm", 0, G_OUT + 2)

            def first_half(mm, layer, chunk):
                dve.wait_ge(sem("bias_added"), 4 * (layer + 1))
                for tb in range(TB):
                    add_half(mm, chunk, 0, tb)

            def add_half(mm, chunk, half, tb):
                if tb < 3:
                    dve.wait_ge(sem(mm), 3 * half + tb + 1)
                else:
                    dve.wait_ge(chunk_used, chunk + 1 + CREDIT)
                cols = slice(512 * half, 512 * half + 512)
                return nc.vector.tensor_tensor(xres[:, tb, cols], xres[:, tb, cols], pb[4 * half + tb][:, :], ALU.add)

            def mixed(mm, chunk):
                return lambda tb: add_half(mm, chunk, 1, tb).then_inc(sem("x_ready"), 1)

            def retrieved(layer):
                def produce(tb):
                    if tb < 3:
                        dve.wait_ge(sem(f"v_mm{layer}"), tb + 1)
                    else:
                        dve.wait_ge(chunk_used, G_PEER[layer] + NCH_Q + 2 * NCH_E + CREDIT)
                    for half in range(2):
                        cols = slice(512 * half, 512 * half + 512)
                        last = nc.vector.tensor_tensor(xres[:, tb, cols], xres[:, tb, cols],
                                                       pb[2 * tb + half][:, :], ALU.add)
                    last.then_inc(sem("x_ready"), 1)
                return produce

            def query(layer):
                base = G_PEER[layer]
                with dve.Fori(0, NCH_Q // 2) as i:
                    for k in range(2):
                        split_lo(dve, base + k + 1, i)

            def top16(values, index, src, spare):
                rows = range(len(src))
                for r in rows:
                    last = nc.vector.max(values[r][:, 0:8], src[r])
                link(last)
                for r in rows:
                    nc.vector.max_index(index[r][:, 0:8], values[r][:, 0:8], src[r])
                    last = nc.vector.match_replace(spare[r], values[r][:, 0:8], src[r], LOWEST)
                link(last)
                for r in rows:
                    last = nc.vector.max(values[r][:, 8:16], spare[r])
                link(last)
                for r in rows:
                    last = nc.vector.max_index(index[r][:, 8:16], values[r][:, 8:16], spare[r])
                link(last)

            def retrieve(k):
                js = range(4 * k, 4 * k + 4)
                top16([topv[:, j, :] for j in js], [topi[:, j, :] for j in js], [sblk[:, j, :] for j in js],
                      [work[:, P * r:P * r + P] for r in range(4)])
                for r in range(2):
                    a, b = topv[:, 4 * k + 2 * r, :], topv[:, 4 * k + 2 * r + 1, :]
                    last = nc.vector.tensor_tensor(cand[:, r, :].rearrange("p (a b) -> p a b", a=TOPK),
                                                   a.unsqueeze(2).broadcast_to([P, TOPK, TOPK]),
                                                   b.unsqueeze(1).broadcast_to([P, TOPK, TOPK]), ALU.add)
                link(last)
                top16([best[:, 2 * k + r, :] for r in range(2)], [bestp[:, 2 * k + r, :] for r in range(2)],
                      [cand[:, r, :] for r in range(2)], [work[:, 256 * r:256 * r + 256] for r in range(2)])

            def select(layer, i):
                n = f"{layer}"
                link(nc.vector.tensor_tensor(sel[:, 2, :].rearrange("p (h k) -> p h k", h=PH), best[:, :, :],
                                             best[:, :, 0:1].broadcast_to([P, PH, TOPK]), ALU.subtract))
                nc.vector.tensor_copy(best[:, :, :], sel[:, 2, :].rearrange("p (h k) -> p h k", h=PH)) \
                    .then_inc(sem("best_ready" + n), 1)
                flat = bestp[:, :, :].rearrange("p h k -> p (h k)")
                nc.vector.tensor_scalar(posn[:, 0, :], flat, 4, None, ALU.logical_shift_right)
                link(nc.vector.tensor_scalar(posn[:, 1, :], flat, 15, None, ALU.bitwise_and))
                nc.vector.tensor_copy(topif[:, :, :], topi[:, :, :])
                link(nc.vector.tensor_copy(posf[:, :, :], posn[:, :, :]))
                for s in range(2):
                    link(nc.vector.tensor_tensor(onehot[:, :, :], posf[:, s, :].unsqueeze(2).broadcast_to([P, P, TOPK]),
                                                 iota[:, 0:TOPK].unsqueeze(1).broadcast_to([P, P, TOPK]),
                                                 ALU.is_equal))
                    idx = topif[:, :, :].rearrange("p (h s) j -> p s h j", s=2)[:, s, :, :]
                    hot = onehot[:, :, :].rearrange("p (h k) j -> p h k j", h=PH)
                    link(nc.vector.tensor_tensor(hot, hot, idx.unsqueeze(2).broadcast_to([P, PH, TOPK, TOPK]),
                                                 ALU.mult))
                    link(nc.vector.tensor_reduce(sel[:, s, :], onehot[:, :, :], AX_X, ALU.add))
                dve.wait_ge(sem("best_exp" + n), i + 1)
                link(nc.vector.tensor_reduce(gsum[:, :], best[:, :, :], AX_X, ALU.add))
                link(nc.vector.reciprocal(grec[:, :], gsum[:, :]))
                gates = sel[:, 3, :]
                link(nc.vector.tensor_tensor(gates.rearrange("p (h k) -> p h k", h=PH), best[:, :, :],
                                             grec[:, :].unsqueeze(2).broadcast_to([P, PH, TOPK]), ALU.mult))
                link(nc.vector.tensor_copy(gate_b[:, :], gates))
                link(nc.vector.tensor_copy(sel[:, 2, :], gate_b[:, :]))
                nc.vector.tensor_tensor(sel[:, 3, :], gates, sel[:, 2, :],
                                        ALU.subtract).then_inc(sem("sel_ready" + n), 1)

            def experts_first(layer):
                n, base = f"{layer}", G_PEER[layer] + NCH_Q
                dve.wait_ge(sem("iota_ready"), 2)
                dve.sem_inc(sem("sel_ready" + n), 1)
                dve.sem_inc(sem("best_ready" + n), 1)
                with dve.Fori(0, TB) as i:
                    chain.restart()
                    dve.wait_ge(sem("sel_tr" + n), i + 1)
                    dve.wait_ge(sem("sblk_ready" + n), i + 1)
                    for k in range(3):
                        split_lo(dve, base + k + 1, i * 2)
                        retrieve(k)
                        if k == 0:
                            retrieve(3)
                    select(layer, i)
                    split_lo(dve, base + 4, i * 2)
                dve.wait_ge(sem("selT_ready" + n), TB)

                def one_hots(i, k, s):
                    dve.wait_ge(sem("gate_mm" + n), i * 32 + 8 * k + 4 * s + 4)
                    places = iota_b[:, :].unsqueeze(1).broadcast_to([P, 16, P])

                    def row(r):
                        return tslice[:, k % 2, r, 16 * s:16 * s + 16].unsqueeze(2).broadcast_to([P, 16, P])

                    link(nc.vector.tensor_tensor(hot2[0][:, s, :, :], places, row(1), ALU.is_equal))
                    nc.vector.tensor_tensor(hot1[:, s, :, :], places, row(0), ALU.is_equal)
                    link(nc.vector.tensor_tensor(hot2[1][:, s, :, :], hot2[0][:, s, :, :], row(3), ALU.mult))
                    nc.vector.tensor_tensor(hot2[0][:, s, :, :], hot2[0][:, s, :, :], row(2), ALU.mult) \
                        .then_inc(sem("hot_ready" + n), 1)

                with dve.Fori(0, TB) as i:
                    chain.restart()
                    for k in range(4):
                        link(nc.vector.tensor_copy(tslice[:, k % 2, :, :], selT[:, :, bass.ds(i * P + BT * k, BT)]))
                        one_hots(i, k, 0)
                        one_hots(i, k, 1)
                        split_lo(dve, base + NCH_E // 2 + k + 1, i * 2)

            def h_parts(layer, k, h, first=False):
                n, b = f"{layer}", k % 2
                dve.wait_ge(sem(f"sa_loaded{b}"), h * 32 + 32 * (k // 2 + 1 + layer * NCH_E // 2))
                high, low = (hsp[b][part].rearrange("p e (g t) -> p e g t", t=BT) for part in range(2))
                acts = s_in[b].rearrange("p (e g t) -> p e g t", e=4, t=BT)
                gates = a_in[b].rearrange("p (g e t) -> p e g t", e=4, t=BT)
                gated = hf[b].rearrange("p (e g t) -> p e g t", e=4, t=BT)
                if first:
                    g = SEQ // BT - 1
                    link(nc.vector.tensor_tensor(gated[:, :, 0:g, :], acts[:, :, 0:g, :], gates[:, :, 0:g, :], ALU.mult))
                    link(nc.vector.tensor_copy(high[:, :, 0:g, :], gated[:, :, 0:g, :]))
                    nc.vector.tensor_tensor(low[:, :, 0:g, :], gated[:, :, 0:g, :], high[:, :, 0:g, :], ALU.subtract)
                    dve.wait_ge(sem("gate_evac" + n), 3 + SEQ // 4)
                    nc.vector.tensor_tensor(gated[:, :, g, :], acts[:, :, g, :], gstage[:, 1, 0:4, :],
                                            ALU.mult).then_inc(sem("hf_ready" + n), 1)
                    dve.wait_ge(sem("h_hi" + n), 1)
                    nc.vector.tensor_tensor(low[:, :, g, :], gated[:, :, g, :], high[:, :, g, :],
                                            ALU.subtract).then_inc(sem("h_ready" + n), 1)
                else:
                    nc.vector.tensor_tensor(gated, acts, gates, ALU.mult).then_inc(sem("hf_ready" + n), 1)
                    dve.wait_ge(sem("h_hi" + n), h * 2 + k + 1)
                    nc.vector.tensor_tensor(hsp[b][1][:, :, :].rearrange("p e t -> p (e t)"), hf[b],
                                            hsp[b][0][:, :, :].rearrange("p e t -> p (e t)"), ALU.subtract) \
                        .then_inc(sem("h_ready" + n), 1)

            def experts_second(layer):
                n, base = f"{layer}", G_PEER[layer] + NCH_Q + NCH_E
                dve.sem_inc(sem("h_ready" + n), 2)
                h_parts(layer, 0, 0, True)
                with dve.Fori(0, NCH_E // 2 - 1) as i:
                    for k in range(2):
                        split_lo(dve, base + k + 1, i)
                        h_parts(layer, k + 1, i)
                split_lo(dve, base + NCH_E - 1)
                h_parts(layer, NCH_E - 1, 0)
                if base + NCH_E < CHUNKS:
                    split_lo(dve, base + NCH_E)

            def rope_part(part, t0=0, t1=TB):
                heads, at = (8, 512 * part) if part < 2 else (4, QW)
                half, blocks = HD // 2, t1 - t0
                done = part + 1 + t0
                dve.wait_ge(sem("hroot_ready"), done)
                cols = slice(heads * t0, heads * t1)
                link(nc.vector.reciprocal(hrs[:, cols], hrt[:, cols]))
                x_ = qkv[:, t0:t1, at:at + HD * heads].rearrange("p t (h d) -> p t h d", d=HD)
                rs = hrs[:, cols].rearrange("p (t h) -> p t h", h=heads)
                link(nc.vector.tensor_tensor(x_, x_, rs.unsqueeze(3).broadcast_to([P, blocks, heads, HD]), ALU.mult))
                cos1, sin2, cos2, sin1 = (gtabs[:, part // 2, r, t0:t1, :].unsqueeze(2)
                                          .broadcast_to([P, blocks, heads, half]) for r in range(4))
                x1, x2 = x_[:, :, :, 0:half], x_[:, :, :, half:]
                o = qr[part][:, t0:t1, 0:HD * heads].rearrange("p t (h d) -> p t h d", d=HD)
                t1, t2 = (tmp[:, 1024 * r:1024 * r + blocks * heads * half]
                          .rearrange("p (t h d) -> p t h d", t=blocks, d=half) for r in range(2))
                if part == 2:
                    dve.wait_ge(sem("qk_tr"), TB)
                nc.vector.tensor_tensor(t1, x1, cos1, ALU.mult)
                link(nc.vector.tensor_tensor(t2, x2, sin2, ALU.mult))
                link(nc.vector.tensor_tensor(o[:, :, :, 0:half], t1, t2, ALU.subtract))
                nc.vector.tensor_tensor(t1, x2, cos2, ALU.mult)
                link(nc.vector.tensor_tensor(t2, x1, sin1, ALU.mult))
                nc.vector.tensor_tensor(o[:, :, :, half:], t1, t2, ALU.add).then_inc(sem("qr_ready"), 1)
                dve.wait_ge(sem("qr_ready"), done)

            def masked(u):
                tb, half = u // 2, u % 2
                lo = 64 if tb else P
                width = 256 - lo
                pr = prob[u % 3]
                byp = pr[:, :, :].rearrange("p (m q r) k -> p m r q k", q=2, r=2)
                if u >= 3:
                    dve.wait_ge(sem("prob_tr"), 4 * (u - 2))
                elif u == 2:
                    dve.wait_ge(sem("qk_tr"), 3 * TB)
                for r in range(4):
                    dve.wait_ge(sem("qk_mm"), 4 * u + r // 2 * 2 + 2)
                    src = pb[r][:, :].rearrange("p (h k) -> p h k", h=2)[:, :, 0:width]
                    last = nc.vector.scalar_tensor_tensor(
                        byp[:, r // 2, r % 2, :, lo:256], src, HD ** -0.5,
                        mask[:, 192 - width:192].unsqueeze(1).broadcast_to([P, 2, width]), ALU.mult, ALU.add)
                last.then_inc(sem("scores_taken"), 1)
                dve.wait_ge(sem("scores_taken"), u + 1)
                link(nc.vector.tensor_reduce(smax[:, u % 3, :], pr[:, :, lo:256], AX_X, ALU.max))
                snk = sink[:, 8 * half:8 * half + 8]
                link(nc.vector.tensor_tensor(smax[:, u % 3, :], smax[:, u % 3, :], snk, ALU.max))
                nc.vector.tensor_tensor(esink[:, u % 3, :], snk, smax[:, u % 3, :], ALU.subtract)
                nc.vector.tensor_scalar(nmax[:, u % 3, :], smax[:, u % 3, :], -1.0, None,
                                        ALU.mult).then_inc(sem("max_ready"), 1)

            def normalised(u):
                lo = 64 if u >= 2 else P
                pr = prob[u % 3][:, :, lo:256]
                dve.wait_ge(sem("prob_exp"), u + 1)
                link(nc.vector.tensor_tensor(ssum[:, u % 3, :], ssum[:, u % 3, :], esink[:, u % 3, :], ALU.add))
                link(nc.vector.reciprocal(srec[:, u % 3, :], ssum[:, u % 3, :]))
                nc.vector.tensor_tensor(pr, pr, srec[:, u % 3, :].unsqueeze(2).broadcast_to([P, 8, 256 - lo]),
                                        ALU.mult).then_inc(sem("prob_ready"), 1)

            def out_low(u):
                tb, half = u // 2, u % 2
                dve.wait_ge(sem("oT_hi"), u + 1)
                at = (slice(None), slice(4 * half, 4 * half + 4), slice(tb * P, (tb + 1) * P))
                nc.vector.tensor_tensor(hT[1][at], pb[6 + half][:, :].rearrange("p (k t) -> p k t", k=4),
                                        hT[0][at], ALU.subtract).then_inc(sem("oT_lo"), 1)

            def attention():
                dve.wait_ge(sem("attn_loaded"), 64)
                dve.wait_ge(sem("mask_ready"), 2)
                for w in range(2):
                    for r, (table, side) in enumerate(((0, 0), (1, 1), (0, 1), (1, 0))):
                        g = qkg[:, w, HD // 2 * side:HD // 2 * (side + 1)]
                        last = nc.vector.tensor_tensor(gtabs[:, w, r, :, :], tabs[:, table, :, :],
                                                       g.unsqueeze(1).broadcast_to([P, TB, HD // 2]), ALU.mult)
                link(last)
                def add_bias(c, tb):
                    wait_output(dve, sem("qkv_mm"), G_QKV + c, G_QKV, tb)
                    nc.vector.tensor_tensor(qkv[:, tb, 512 * c:512 * c + 512], pb[tb][:, :],
                                            qbias[:, 512 * c:512 * c + 512], ALU.add) \
                        .then_inc(sem("qkv_evac"), 1)

                def square_sums(c, tb, heads):
                    dve.wait_ge(sem("heads_squared"), TB * c + tb + 1)
                    return nc.vector.tensor_reduce(
                        hss[:, heads * tb:heads * tb + heads],
                        tmp[:, 512 * tb:512 * tb + HD * heads].rearrange("p (h d) -> p h d", d=HD), AX_X, ALU.add)

                for c in range(2):
                    for tb in range(TB):
                        add_bias(c, tb)
                        if tb:
                            square_sums(c, tb - 1, 8)
                        else:
                            split_lo(dve, G_QKV + c + 1)
                    square_sums(c, TB - 1, 8).then_inc(sem("hss_ready"), 1)
                    rope_part(c)
                for tb in range(TB):
                    add_bias(2, tb)
                    square_sums(2, tb, 4).then_inc(sem("hss_ready"), 1)
                    rope_part(2, tb, tb + 1)
                dve.wait_ge(sem("qk_tr"), 2 * TB)
                for u in range(UNITS + 2):
                    if u < UNITS:
                        masked(u)
                    if 1 <= u <= UNITS:
                        normalised(u - 1)
                    if u >= 2:
                        out_low(u - 2)
                    if u == UNITS:
                        split_lo(dve, G_WO)
                for c in range(NCH_O):
                    split_lo(dve, G_WO + c + 1)
                first_half("ao_mm", 1, G_WO)

            dve.sem_inc(lo_done, CREDIT)
            dve.sem_inc(sem("z_evac"), 4)
            nc.vector.memset(epsilon[:, :], EPS).then_inc(sem("epsilon_ready"), 1)
            norm(0, x_loaded)
            add_rows(bout, "bout_loaded")
            gmlp()
            norm(1, mixed("zo_mm", G_OUT + NCH_OUT - 1))
            if stages > 1:
                query(0)
                experts_first(0)
                experts_second(0)
            if stages > 2:
                norm(2, retrieved(0))
                add_rows(bo, "bo_loaded")
                attention()
                norm(3, mixed("ao_mm", G_WO + 1))
            if stages > 3:
                query(1)
                experts_first(1)
                experts_second(1)
            if stages % 2 == 0:
                for tb in range(TB):
                    retrieved(stages // 2 - 1)(tb)

        @block.tensor
        def _(pe):
            def norm_tr(j, tb):
                pe.wait_ge(sem("hn_ready"), 4 * j + tb + 1)
                for half in range(2):
                    for k in range(4):
                        f = 4 * half + k
                        last = nc.tensor.transpose(pb[2 * tb + half][:, k * P:(k + 1) * P],
                                                   hn[:, tb % 2, f * P:(f + 1) * P], ident[:, :])
                    last.then_inc(sem("hT_tr"), 1)

            def wait_h(j, blocks):
                pe.wait_ge(sem("hT_lo"), 8 * j + 2 * blocks)

            def z_block(c, tb, h):
                if tb == 0:
                    wait_chunk(pe, c, h)
                pe.wait_ge(sem("z_evac"), h * 8 + 4 * c + tb + 1)
                token_chunk(pb[tb], c, tb, h_lhs).then_inc(sem("z_mm") if tb < 3 else chunk_used, 1)

            def v_item(c, tb, h, first):
                if c == 0:
                    wait_h(0, tb + 1)
                z_block(G_V + c, tb, h)
                if first:
                    norm_tr(0, 2)
                    norm_tr(0, 3)

            def out_block(n, kg, tb):
                c = G_OUT + 3 * n + kg
                if tb == 0:
                    wait_chunk(pe, c)
                mm = token_chunk(pb[4 * n + tb], c, tb,
                                 lambda k, t, part: yT(2 * kg + k // 4, t, part)[:, k % 4, :],
                                 first=kg == 0, last=kg == 2)
                if kg == 2 and tb < 3:
                    mm.then_inc(sem("zo_mm"), 1)
                elif tb == 3:
                    mm.then_inc(chunk_used, 1)

            def y_transpose(c, tb, h):
                pe.wait_ge(sem("y_done"), h * 8 + 4 * c + tb + 1 + 2)
                pe.wait_ge(sem("y_lo"), h * 8 + 4 * c + tb + 1)
                for f in range(4):
                    last = nc.tensor.transpose(pb[4 + tb % 2][:, f * P:(f + 1) * P],
                                               ytok[:, tb % 2, f * P:(f + 1) * P], ident[:, :])
                last.then_inc(sem("y_tr"), 1)

            def gmlp():
                pe.sem_inc(sem("y_tr"), 2)
                z_items(pe, v_item)
                for tb in range(TB):
                    z_block(G_U, tb, 0)
                pe.wait_ge(sem("ws_masked"), 1)
                for c in range(NCH_Z):
                    for tb in range(TB):
                        idx = c * TB + tb
                        pe.wait_ge(sem("vn_ready"), idx + 1)
                        if idx >= 4:
                            pe.wait_ge(sem("mix_evac"), idx - 3)
                        at = 0
                        while at < 512:
                            g = (c * 512 + at) // GW
                            w = min(512, (g + 1) * GW - c * 512) - at
                            last = nc.tensor.matmul(pb[4 + idx % 4][:, at:at + w], wsT[:, g, :],
                                                    vmix[:, c, tb, at:at + w], start=True, stop=True)
                            at += w
                        last.then_inc(sem("mix_mm"), 1)
                with pe.Fori(0, (NCH_Z - 2) // 2) as i:
                    for c in range(2):
                        for tb in range(TB):
                            z_block(G_U + c + 1, tb, i)
                            y_transpose(c, tb, i)
                for tb in range(TB):
                    z_block(G_U + NCH_Z - 1, tb, 0)
                    y_transpose(NCH_Z - 2, tb, 0)
                for tb in range(TB):
                    pe.wait_ge(sem("z_evac"), 4 * (G_U + NCH_Z) + tb + 1)
                    out_block(0, 0, tb)
                    y_transpose(NCH_Z - 1, tb, 0)
                for n, kg in ((0, 1), (0, 2), (1, 0), (1, 1), (1, 2)):
                    if (n, kg) == (0, 2):
                        pe.wait_ge(sem("y_lo"), 2 + NCH_Z * TB)
                    for tb in range(TB):
                        out_block(n, kg, tb)
                        if (n, kg, tb) == (1, 2, 2):
                            norm_tr(1, 0)
                            norm_tr(1, 1)

            def query(layer):
                base, n = G_PEER[layer], f"{layer}"
                j = 2 * layer + 1
                norm_tr(j, 2)
                wait_chunk(pe, base)
                for t0, t1 in ((0, 2 * P), (2 * P, 3 * P), (3 * P, SEQ)):
                    wait_h(j, t1 // P)
                    for f in range(4):
                        mm = feature_chunk(pb[f], base, f, t0, t1)
                        if t1 == SEQ:
                            mm.then_inc(sem("q_mm" + n) if f < 3 else chunk_used, 1)
                        if t0 == 0 and f == 1:
                            norm_tr(j, 3)
                for k in range(1, NCH_Q):
                    wait_chunk(pe, base + k)
                    for f in range(4):
                        pe.wait_ge(sem("q_evac" + n), 4 * k + f + 1)
                        feature_chunk(pb[f], base + k, f).then_inc(sem("q_mm" + n) if f < 3 else chunk_used, 1)
                pe.wait_ge(sem("q_evac" + n), 4 + 16)
                pe.wait_ge(sem("keys_loaded"), 16 * (layer + 1))
                for idx in range(4 * TB):
                    tb = idx // 4
                    if idx >= 4:
                        pe.wait_ge(sem("s_evac" + n), idx - 3)
                    for r in range(4):
                        j = 4 * (idx % 4) + r
                        last = nc.tensor.matmul(pb[4 + idx % 4][:, r * P:(r + 1) * P], pqT[:, j, tb * P:(tb + 1) * P],
                                                keysT[:, j % 2, :], start=True, stop=True)
                    last.then_inc(sem("s_mm" + n), 1)

            def expert_tile(layer, k, e, h, first):
                n = f"{layer}"
                base = G_PEER[layer] + NCH_Q
                if e == 0:
                    wait_chunk(pe, base + first + k, h)
                pe.wait_ge(sem("gelu_done" + n), h * 8 + 4 * (first + k) + e + 1)
                feature_chunk(pb[e], base + first + k, e).then_inc(sem("u_mm" + n) if e < 3 else chunk_used, 1)

            def experts_first(layer):
                n = f"{layer}"
                pe.sem_inc(sem("sel_tr" + n), 1)
                with pe.Fori(0, TB) as i:
                    for k in range(4):
                        for e in range(4):
                            if k == 3 and e == 3:
                                pe.wait_ge(sem("sel_ready" + n), i + 2)
                                for s in range(4):
                                    last = nc.tensor.transpose(pb[4][:, s * P:(s + 1) * P], sel[:, s, :],
                                                               ident[:, :])
                                last.then_inc(sem("sel_tr" + n), 1)
                            expert_tile(layer, k, e, i * 2, 0)
                pe.sem_inc(sem("gate_mm" + n), 8)
                with pe.Fori(0, TB) as i:
                    for k in range(4):
                        for e in range(4):
                            expert_tile(layer, k, e, i * 2, NCH_E // 2)
                            for q in QUADS[e]:
                                s = q // 4
                                if q % 4 == 0:
                                    pe.wait_ge(sem("hot_ready" + n), i * 8 + 2 * k + s + 1)
                                pe.wait_ge(sem("gate_evac" + n), i * 32 + 8 * k + (q + 1 if q > 1 else q + 2))
                                for t in range(4):
                                    u = 4 * (q % 4) + t
                                    for r in range(2):
                                        last = nc.tensor.matmul(pb[5 + q % 3][:, t * P:(t + 1) * P],
                                                                hot1[:, s, u, :], hot2[r][:, s, u, :],
                                                                start=r == 0, stop=r == 1)
                                last.then_inc(sem("gate_mm" + n), 1)

            def value_chunk(layer, k, h=0):
                n, c = f"{layer}", G_PEER[layer] + NCH_Q + NCH_E + k
                final = k == NCH_E - 1
                wait_chunk(pe, c, h)
                pe.wait_ge(sem("h_ready" + n), h * 2 + k + 1 + 2)
                w = [v[:, :].rearrange("p (e n) -> p e n", e=4) for v in wsp[c % 2]]
                for e, tb in ([(e, tb) for tb in range(TB) for e in range(4)] if final else
                              [(e, tb) for e in range(4) for tb in range(TB)]):
                    for m, (a, b) in enumerate(((0, 0), (0, 1), (1, 0))):
                        for half in range(2):
                            mm = nc.tensor.matmul(pb[2 * tb + half][:, :],
                                                  hsp[k % 2][a][:, e, tb * P:(tb + 1) * P],
                                                  w[b][:, e, 512 * half:512 * half + 512],
                                                  start=k == 0 and e == 0 and m == 0,
                                                  stop=final and e == 3 and m == 2)
                    if final and e == 3 and tb < 3:
                        mm.then_inc(sem("v_mm" + n), 1)
                        if tb == 2 and layer == 0 and stages > 2:
                            norm_tr(2, 0)
                            norm_tr(2, 1)
                mm.then_inc(chunk_used, 1)

            def experts_second(layer):
                n = f"{layer}"
                pe.wait_ge(sem("gelu_done" + n), 4 + 4 * NCH_E)
                pe.wait_ge(sem("gate_evac" + n), 3 + SEQ // 4)
                pe.wait_ge(sem("selT_ready" + n), TB)
                value_chunk(layer, 0)
                value_chunk(layer, 1)
                with pe.Fori(0, NCH_E // 2 - 2) as i:
                    for k in (2, 3):
                        value_chunk(layer, k, i)
                value_chunk(layer, NCH_E - 2)
                value_chunk(layer, NCH_E - 1)

            def attention():
                def heads_tr(part, tb):
                    pe.wait_ge(sem("qr_ready"), part + 1 if part < 2 else part + tb + 1)
                    if part:
                        pe.wait_ge(sem("qk_T"), TB * (part - 1) + tb + 1)
                    for k in range(4 if part < 2 else 2):
                        last = nc.tensor.transpose(pb[4 + tb][:, k * P:(k + 1) * P],
                                                   qr[part][:, tb, k * P:(k + 1) * P], ident[:, :])
                    last.then_inc(sem("qk_tr"), 1)

                for c in range(NCH_QKV):
                    wait_chunk(pe, G_QKV + c)
                    for tb in range(TB):
                        if c:
                            pe.wait_ge(sem("qkv_evac"), TB * (c - 1) + tb + 1)
                        else:
                            wait_h(2, tb + 1)
                        if c == 2 and tb == 3:
                            for t in range(TB):
                                heads_tr(1, t)
                        token_chunk(pb[tb], G_QKV + c, tb, h_lhs) \
                            .then_inc(sem("qkv_mm") if tb < 3 else chunk_used, 1)
                        if c == 0 and tb == 0:
                            norm_tr(2, 3)
                    if c == 1:
                        for tb in range(TB):
                            heads_tr(0, tb)
                for tb in range(3):
                    heads_tr(2, tb)
                pe.wait_ge(sem("qkv_evac"), TB * NCH_QKV)

                def score(u):
                    tb, half = u // 2, u % 2
                    key0 = (tb * P - 64) if tb else 0
                    width = 192 if tb else P
                    pe.wait_ge(sem("qk_T"), 2 * TB + tb + 1)
                    if u:
                        pe.wait_ge(sem("scores_taken"), u)
                    for r in range(4):
                        for par in range(2):
                            rows = slice(64 * par, 64 * par + 64)
                            at = 256 * (r % 2)
                            mm = nc.tensor.matmul(pb[r // 2 * 2 + par][:, at:at + width],
                                                  qT[rows, 4 * half + r, tb * P:(tb + 1) * P],
                                                  kT[rows, half, key0:key0 + width], start=True, stop=True)
                            if r % 2:
                                mm.then_inc(sem("qk_mm"), 1)

                def prob_transpose(u, r):
                    idx = 4 * u + r
                    if idx >= 2:
                        pe.wait_ge(sem("probT_ready"), idx - 1)
                    for at, (par, blk) in enumerate(((0, 1), (1, 1), (0, 0), (1, 0))[:4 if u >= 2 else 2]):
                        last = nc.tensor.transpose(pb[4 + r % 2][:, at * P:(at + 1) * P],
                                                   prob[u % 3][:, 2 * r + par, blk * P:(blk + 1) * P], ident[:, :])
                    last.then_inc(sem("prob_tr"), 1)

                def weighted(u, r):
                    tb, half = u // 2, u % 2
                    pe.wait_ge(sem("probT_ready"), 4 * u + r + 1)
                    if r == 0 and u >= 2:
                        pe.wait_ge(sem("oT_lo"), u - 1)
                    for par in range(2):
                        kv = 2 * half + par
                        cols = slice(QK + HD * kv, QK + HD * kv + HD)
                        o = pb[6 + half][64 * par:64 * par + 64, r * P:(r + 1) * P]
                        last = nc.tensor.matmul(o, qkv[:, tb, cols], probT[:, r, par * P:(par + 1) * P],
                                                start=True, stop=tb == 0)
                        if tb:
                            last = nc.tensor.matmul(o, qkv[:, tb - 1, cols], probT[:, r, (2 + par) * P:(3 + par) * P],
                                                    start=False, stop=True)
                    last.then_inc(sem("pv_mm"), 1)

                score(0)
                heads_tr(2, 3)
                score(1)
                for u in range(UNITS):
                    if u + 2 < UNITS:
                        score(u + 2)
                    pe.wait_ge(sem("prob_ready"), u + 1)
                    if u == 2:
                        pe.wait_ge(sem("left_zero"), 3)
                    for r in range(5):
                        if r < 4:
                            prob_transpose(u, r)
                        if r:
                            weighted(u, r - 1)
                pe.wait_ge(sem("oT_lo"), UNITS)
                for c in range(NCH_O):
                    wait_chunk(pe, G_WO + c)
                    for tb in range(TB):
                        token_chunk(pb[4 * c + tb], G_WO + c, tb, h_lhs) \
                            .then_inc(sem("ao_mm") if tb < 3 else chunk_used, 1)
                        if c == 1 and tb == 2:
                            norm_tr(3, 0)
                            norm_tr(3, 1)

            pe.sem_inc(chunk_used, CREDIT)
            pe.wait_ge(sem("ident_ready"), 1)
            norm_tr(0, 0)
            norm_tr(0, 1)
            gmlp()
            if stages > 1:
                query(0)
                experts_first(0)
                experts_second(0)
            if stages > 2:
                norm_tr(2, 2)
                attention()
            if stages > 3:
                query(1)
                experts_first(1)
                experts_second(1)


def kernel(stages=4, **inputs):
    import numpy as np
    import concourse.bacc as bacc
    from concourse.bass_utils import run_bass_kernel_spmd

    def get(name):
        return np.asarray(inputs[name])

    def columns(w, n=512):
        return w.reshape(KT, P, -1, n).transpose(2, 1, 0, 3).reshape(-1, P, CH)

    order = np.array([(4 * (2 * m + par) + g) for m in range(2) for g in range(4) for par in range(2)])
    q_cols = (order[:, None] * HD + np.arange(HD)[None, :]).ravel()
    qkv_cols = np.concatenate([q_cols, np.arange(QW, QW + 512)])

    stream = np.empty((CHUNKS, P, CH), np.float32)
    w_in = get("gmlp_w_in")[0]
    stream[G_V:G_V + NCH_Z] = columns(w_in[:, HALF:])
    stream[G_U:G_U + NCH_Z] = columns(w_in[:, :HALF])
    stream[G_OUT:G_OUT + NCH_OUT] = get("gmlp_w_out")[0].reshape(3, 8, P, 2, 512) \
        .transpose(3, 0, 2, 1, 4).reshape(NCH_OUT, P, CH)
    stream[G_QKV:G_QKV + NCH_QKV] = columns(get("attn_w_qkv")[0][:, qkv_cols])
    stream[G_WO:G_WO + NCH_O] = columns(get("attn_w_o")[0][q_cols, :])
    for layer in range(2):
        g = G_PEER[layer]
        stream[g:g + NCH_Q] = columns(get("peer_w_query")[layer])
        u = get("peer_expert_u")[layer].reshape(P, NCH_E, 4, KT, P)
        stream[g + NCH_Q:g + NCH_Q + NCH_E] = u.transpose(1, 4, 3, 2, 0).reshape(NCH_E, P, CH)
        v = get("peer_expert_v")[layer].reshape(P, NCH_E, CH)
        stream[g + NCH_Q + NCH_E:g + NCH_Q + 2 * NCH_E] = v.transpose(1, 0, 2)

    gb = get("gmlp_b_in")[0].reshape(2, NCH_Z, 512)
    mix_g, ffn_g = get("mix_norm_g"), get("ffn_norm_g")
    pos = np.arange(SEQ, dtype=np.float32)
    inv = (1.0 / (10000.0 ** (np.arange(0, HD, 2, dtype=np.float32) / HD))).astype(np.float32)
    ang = pos[:, None] * inv[None, :]
    rope = np.stack([np.cos(ang), np.sin(ang)]).astype(np.float32)
    keys = np.stack([get("peer_keys_1"), get("peer_keys_2")], 1)
    arrays = {
        "x": get("x").reshape(SEQ, D),
        "stream": stream,
        "gains": np.stack([mix_g[0], ffn_g[0], mix_g[1], ffn_g[1]]),
        "gmlp_bias": np.concatenate([gb[1], gb[0]]),
        "ln_gb": np.stack([get("gmlp_ln_g")[0], get("gmlp_ln_b")[0]]),
        "w_s": get("gmlp_w_s")[0].transpose(2, 0, 1),
        "b_s": get("gmlp_b_s")[0].T,
        "b_out": get("gmlp_b_out")[0],
        "qkv_bias": get("attn_b_qkv")[0][qkv_cols],
        "b_o": get("attn_b_o")[0],
        "qk_gain": np.concatenate([get("attn_q_gain")[0], get("attn_k_gain")[0]]),
        "sinks": get("attn_sinks")[0][order],
        "rope": rope.reshape(2, TB, P, HD // 2).transpose(2, 0, 1, 3),
        "keys": keys.transpose(0, 3, 1, 2),
    }
    nc = bacc.Bacc("TRN2", target_bir_lowering=False, num_devices=1)
    arrays = {f"in_{k}": np.ascontiguousarray(a) for k, a in arrays.items()}
    args = [nc.dram_tensor(k, a.shape, mybir.dt.from_np(a.dtype), kind="ExternalInput").ap()
            for k, a in arrays.items()]
    out = nc.dram_tensor("out", (SEQ, D), F32, kind="ExternalOutput").ap()
    build(nc, *args, out, stages=stages)
    r = run_bass_kernel_spmd(nc, [arrays], core_ids=[0])
    return r.results[0]["out"].reshape(1, SEQ, D)
```
